# Optimizing a Trainium2 kernel written in Bass

```python
import jax, jax.numpy as jnp
from jax import lax
import numpy as np

D_MODEL = 1024
BATCH = 1
SEQ = 128
DEPTH = 2
DEC_BATCH = 1
DEC_SEQ = 256
PAST_LEN = 128

GRID_W = 64
HEAD_DIM = 64
N_HEADS_NA = 8
WIN_ROWS = 8
WIN_COLS = 16
N_HEADS_SWA = 4
N_KV_SWA = 2
SWA_RADIUS = 128
SWA_BLOCK = 128
N_HEADS_RET = 4
RET_CHUNK = 128
CTX_Q_BLOCK = 128
WIDTH_NA = N_HEADS_NA * HEAD_DIM
WIDTH_SWA = N_HEADS_SWA * HEAD_DIM
WIDTH_KV_SWA = N_KV_SWA * HEAD_DIM
WIDTH_RET = N_HEADS_RET * HEAD_DIM
IN_SPLITS = (WIDTH_NA, WIDTH_NA, WIDTH_NA, WIDTH_SWA, WIDTH_KV_SWA, WIDTH_KV_SWA,
             WIDTH_RET, WIDTH_RET, WIDTH_RET, WIDTH_RET, D_MODEL, D_MODEL, D_MODEL)
IN_COLS = sum(IN_SPLITS)
N_GROUPS = 4
EXPERTS_PER_GROUP = 4
N_EXPERTS = N_GROUPS * EXPERTS_PER_GROUP
TOP_K_EXPERT = 2
D_EXPERT = D_MODEL // 4
ROPE_BASE = 10000.0
EPS = 1e-6

kernel_name = "hybrid_dit_natten_swa_retention_hmoe_step"

F32 = jnp.float32

def _rms(x, g):
    xf = x.astype(F32)
    y = xf * lax.rsqrt(jnp.mean(xf * xf, axis=-1, keepdims=True) + EPS)
    return (y * g.astype(F32)).astype(x.dtype)

def _heads(t, n):
    return t.reshape(t.shape[:-1] + (n, HEAD_DIM))

def _split_in(z):
    idx = np.cumsum(IN_SPLITS)[:-1].tolist()
    return jnp.split(z, idx, axis=-1)

def _modulation(cond, ada_w, ada_b):
    m = jax.nn.silu(cond) @ ada_w + ada_b
    return jnp.split(m, 6, axis=-1)

def _axial_rope(x):
    T = x.shape[1]
    t = jnp.arange(T)
    n_freq = HEAD_DIM // 4
    inv = ROPE_BASE ** (-jnp.arange(n_freq, dtype=F32) / n_freq)
    ang = jnp.concatenate([(t // GRID_W).astype(F32)[:, None] * inv,
                           (t % GRID_W).astype(F32)[:, None] * inv], axis=-1)
    cos = jnp.cos(ang)[None, :, None, :].astype(x.dtype)
    sin = jnp.sin(ang)[None, :, None, :].astype(x.dtype)
    x1, x2 = x[..., 0::2], x[..., 1::2]
    return jnp.stack([x1 * cos - x2 * sin, x1 * sin + x2 * cos], axis=-1).reshape(x.shape)

def _ctx_attention(q, k, v, sink):
    B, L, Hq, d = q.shape
    Hkv = k.shape[1]
    G = Hq // Hkv
    nb = L // CTX_Q_BLOCK
    qb = q.reshape(B, nb, CTX_Q_BLOCK, Hkv, G, d).transpose(1, 0, 2, 3, 4, 5)

    def block(qblk):
        s = jnp.einsum('bqkgd,bksd->bkgqs', qblk, k).astype(F32) * d ** -0.5
        if sink is not None:
            s_sink = jnp.broadcast_to(sink.astype(F32).reshape(1, Hkv, G, 1, 1), s.shape[:-1] + (1,))
            s = jnp.concatenate([s_sink, s], axis=-1)
        pr = jax.nn.softmax(s, axis=-1)
        if sink is not None:
            pr = pr[..., 1:]
        return jnp.einsum('bkgqs,bksd->bqkgd', pr.astype(v.dtype), v)

    o = lax.map(block, qb)
    return o.transpose(1, 0, 2, 3, 4, 5).reshape(B, L, Hq * d)

def _neigh_attention(q, k, v, k_ctx, v_ctx, rpb):
    B, T, H, d = q.shape
    rows = T // GRID_W
    wr = min(WIN_ROWS, rows)
    r = np.arange(rows)
    cc = np.arange(GRID_W)
    row_start = np.clip(r - wr // 2, 0, rows - wr)
    col_start = np.clip(cc - WIN_COLS // 2, 0, GRID_W - WIN_COLS)
    col_idx = col_start[:, None] + np.arange(WIN_COLS)[None, :]
    row_off = row_start[:, None] + np.arange(wr)[None, :] - r[:, None]
    col_off = col_idx - cc[:, None]
    bias = rpb[:, row_off[:, :, None, None] + WIN_ROWS - 1,
               col_off[None, None, :, :] + WIN_COLS - 1]
    bias = bias.transpose(1, 0, 3, 2, 4)
    kg = k.reshape(B, rows, GRID_W, H, d)
    vg = v.reshape(B, rows, GRID_W, H, d)
    qg = q.reshape(B, rows, GRID_W, H, d).transpose(1, 0, 2, 3, 4)
    Lc = k_ctx.shape[2]
    scale = d ** -0.5

    def one_row(args):
        rs, q_row, b_row = args
        k_blk = lax.dynamic_slice_in_dim(kg, rs, wr, axis=1)
        v_blk = lax.dynamic_slice_in_dim(vg, rs, wr, axis=1)
        k_nb = k_blk[:, :, col_idx]
        v_nb = v_blk[:, :, col_idx]
        s_loc = jnp.einsum('bqhd,brqwhd->bhqrw', q_row, k_nb).astype(F32) * scale + b_row.astype(F32)
        s_ctx = jnp.einsum('bqhd,bhsd->bhqs', q_row, k_ctx).astype(F32) * scale
        s = jnp.concatenate([s_ctx, s_loc.reshape(B, H, GRID_W, wr * WIN_COLS)], axis=-1)
        pr = jax.nn.softmax(s, axis=-1).astype(v.dtype)
        p_ctx = pr[..., :Lc]
        p_loc = pr[..., Lc:].reshape(B, H, GRID_W, wr, WIN_COLS)
        return (jnp.einsum('bhqs,bhsd->bqhd', p_ctx, v_ctx)
                + jnp.einsum('bhqrw,brqwhd->bqhd', p_loc, v_nb))

    o = lax.map(one_row, (jnp.asarray(row_start, jnp.int32), qg, bias))
    return o.transpose(1, 0, 2, 3, 4).reshape(B, T, H * d)

def _window_attention(q, k, v, k_ctx, v_ctx, sink):
    B, T, Hq, d = q.shape
    Hkv = k.shape[2]
    G = Hq // Hkv
    blk = SWA_BLOCK
    nb = T // blk
    pad = ((0, 0), (blk, blk), (0, 0), (0, 0))
    kp = jnp.pad(k, pad).reshape(B, nb + 2, blk, Hkv, d)
    vp = jnp.pad(v, pad).reshape(B, nb + 2, blk, Hkv, d)
    kw = jnp.concatenate([kp[:, :-2], kp[:, 1:-1], kp[:, 2:]], axis=2)
    vw = jnp.concatenate([vp[:, :-2], vp[:, 1:-1], vp[:, 2:]], axis=2)
    qb = q.reshape(B, nb, blk, Hkv, G, d)
    qpos = np.arange(nb)[:, None, None] * blk + np.arange(blk)[None, :, None]
    kpos = (np.arange(nb)[:, None, None] - 1) * blk + np.arange(3 * blk)[None, None, :]
    valid = (np.abs(qpos - kpos) <= SWA_RADIUS) & (kpos >= 0) & (kpos < T)
    scale = d ** -0.5
    s_loc = jnp.einsum('bnqkgd,bnskd->bnkgqs', qb, kw).astype(F32) * scale
    s_loc = jnp.where(valid[None, :, None, None], s_loc, -jnp.inf)
    s_ctx = jnp.einsum('bnqkgd,bksd->bnkgqs', qb, k_ctx).astype(F32) * scale
    s_sink = jnp.broadcast_to(sink.astype(F32).reshape(1, 1, Hkv, G, 1, 1), s_ctx.shape[:-1] + (1,))
    s = jnp.concatenate([s_sink, s_ctx, s_loc], axis=-1)
    pr = jax.nn.softmax(s, axis=-1).astype(v.dtype)
    Lc = k_ctx.shape[2]
    p_ctx = pr[..., 1:1 + Lc]
    p_loc = pr[..., 1 + Lc:]
    o = (jnp.einsum('bnkgqs,bksd->bnqkgd', p_ctx, v_ctx)
         + jnp.einsum('bnkgqs,bnskd->bnqkgd', p_loc, vw))
    return o.reshape(B, T, Hq * d)

def _retention_scan(q, k, v, log_gamma, s0):
    B, T, H, d = q.shape
    C = RET_CHUNK
    n = T // C

    def chunks(t):
        return t.reshape(B, n, C, H, d).transpose(1, 0, 3, 2, 4)

    pos = jnp.arange(C, dtype=F32)
    diff = pos[:, None] - pos[None, :]
    intra = jnp.where(diff >= 0, jnp.exp(log_gamma[:, None, None] * jnp.maximum(diff, 0.0)), 0.0)
    q_dec = jnp.exp(log_gamma[:, None] * (pos + 1.0))[..., None]
    k_dec = jnp.exp(log_gamma[:, None] * (C - 1.0 - pos))[..., None]
    c_dec = jnp.exp(log_gamma * C)[:, None, None]

    def step(s, qkv):
        qc, kc, vc = qkv
        a = jnp.einsum('bhqd,bhkd->bhqk', qc, kc) * intra
        o = jnp.einsum('bhqk,bhke->bhqe', a, vc) + jnp.einsum('bhqd,bhde->bhqe', qc, s) * q_dec
        s = c_dec * s + jnp.einsum('bhkd,bhke->bhde', kc * k_dec, vc)
        return s, o

    s_fin, o = lax.scan(step, s0, (chunks(q), chunks(k), chunks(v)))
    return o.transpose(1, 0, 3, 2, 4).reshape(B, T, H, d), s_fin

def _retention(q, k, v, gate, decay_logit, norm_g, s0_f, s0_b):
    qf = q.astype(F32)
    kf = k.astype(F32) * HEAD_DIM ** -0.5
    vf = v.astype(F32)
    lg = jax.nn.log_sigmoid(decay_logit.astype(F32))
    o_f, s_f = _retention_scan(qf, kf, vf, lg[0], s0_f.astype(F32))
    o_b, s_b = _retention_scan(qf[:, ::-1], kf[:, ::-1], vf[:, ::-1], lg[1], s0_b.astype(F32))
    o = o_f + o_b[:, ::-1]
    o = o * lax.rsqrt(jnp.mean(o * o, axis=-1, keepdims=True) + EPS)
    o = o.reshape(o.shape[:2] + (-1,)) * norm_g.astype(F32)
    return o.astype(q.dtype) * jax.nn.silu(gate), s_f, s_b

def _merge_branches(o_na, o_swa, o_ret, ga, gs, gr, p):
    z = (jax.nn.sigmoid(ga) * (o_na @ p["w_br_na"])
         + jax.nn.sigmoid(gs) * (o_swa @ p["w_br_swa"])
         + jax.nn.sigmoid(gr) * (o_ret @ p["w_br_ret"]))
    return z @ p["w_out"]

def _hier_moe(h, p):
    B, T, Dm = h.shape
    x = h.reshape(B * T, Dm)
    g_logit = (x @ p["router_group_w"] + p["router_group_b"]).astype(F32)
    g_prob = jax.nn.softmax(g_logit, axis=-1)
    _, g_sel = lax.top_k(g_logit, 1)
    p_group = jnp.take_along_axis(g_prob, g_sel, axis=-1)
    e_logit = (x @ p["router_expert_w"] + p["router_expert_b"]).astype(F32)
    e_logit = e_logit.reshape(-1, N_GROUPS, EXPERTS_PER_GROUP)
    e_in = jnp.take_along_axis(e_logit, g_sel[:, :, None], axis=1)[:, 0]
    e_top, e_sel = lax.top_k(e_in, TOP_K_EXPERT)
    w = jax.nn.softmax(e_top, axis=-1) * p_group
    eid = g_sel * EXPERTS_PER_GROUP + e_sel
    combine = jnp.sum(jax.nn.one_hot(eid, N_EXPERTS, dtype=F32) * w[..., None], axis=1)
    hg = jnp.einsum('nd,edf->nef', x, p["w_gate"])
    hu = jnp.einsum('nd,edf->nef', x, p["w_up"])
    a = jax.nn.silu(hg) * hu * combine.astype(x.dtype)[..., None]
    y = jnp.einsum('nef,efd->nd', a, p["w_down"])
    return y.reshape(B, T, Dm)

def _context_layer(x, mod, p):
    B, L, _ = x.shape
    sh1, sc1, g1, sh2, sc2, g2 = mod
    h = _rms(x, p["norm1_g"]) * (1 + sc1) + sh1
    qa, ka, va, qs, ks, vs, qr, kr, vr, gr, ga, gs, gre = _split_in(h @ p["w_in"])
    ka_c = _heads(ka, N_HEADS_NA).transpose(0, 2, 1, 3)
    va_c = _heads(va, N_HEADS_NA).transpose(0, 2, 1, 3)
    ks_c = _heads(ks, N_KV_SWA).transpose(0, 2, 1, 3)
    vs_c = _heads(vs, N_KV_SWA).transpose(0, 2, 1, 3)
    o_na = _ctx_attention(_heads(qa, N_HEADS_NA), ka_c, va_c, None)
    o_swa = _ctx_attention(_heads(qs, N_HEADS_SWA), ks_c, vs_c, p["swa_sink"])
    zero = jnp.zeros((B, N_HEADS_RET, HEAD_DIM, HEAD_DIM), F32)
    o_ret, s_f, s_b = _retention(_heads(qr, N_HEADS_RET), _heads(kr, N_HEADS_RET), _heads(vr, N_HEADS_RET),
                                 gr, p["ret_decay"], p["ret_norm_g"], zero, zero)
    x = x + g1 * _merge_branches(o_na, o_swa, o_ret, ga, gs, gre, p)
    h2 = _rms(x, p["norm2_g"]) * (1 + sc2) + sh2
    x = x + g2 * _hier_moe(h2, p)
    return x, ka_c, va_c, ks_c, vs_c, jnp.stack([s_f, s_b], axis=1)

def _latent_layer(x, mod, p, k_na_c, v_na_c, k_swa_c, v_swa_c, s_ret_c):
    sh1, sc1, g1, sh2, sc2, g2 = mod
    h = _rms(x, p["norm1_g"]) * (1 + sc1) + sh1
    qa, ka, va, qs, ks, vs, qr, kr, vr, gr, ga, gs, gre = _split_in(h @ p["w_in"])
    o_na = _neigh_attention(_heads(qa, N_HEADS_NA), _heads(ka, N_HEADS_NA), _heads(va, N_HEADS_NA),
                            k_na_c, v_na_c, p["na_rpb"])
    o_swa = _window_attention(_axial_rope(_heads(qs, N_HEADS_SWA)), _axial_rope(_heads(ks, N_KV_SWA)),
                              _heads(vs, N_KV_SWA), k_swa_c, v_swa_c, p["swa_sink"])
    o_ret, _, _ = _retention(_heads(qr, N_HEADS_RET), _heads(kr, N_HEADS_RET), _heads(vr, N_HEADS_RET),
                             gr, p["ret_decay"], p["ret_norm_g"], s_ret_c[:, 0], s_ret_c[:, 1])
    x = x + g1 * _merge_branches(o_na, o_swa, o_ret, ga, gs, gre, p)
    h2 = _rms(x, p["norm2_g"]) * (1 + sc2) + sh2
    return x + g2 * _hier_moe(h2, p)

def setup_inputs(seed: int = 0) -> dict:
    key = jax.random.key(seed)
    ks = jax.random.split(key, 40)
    D = D_MODEL

    def nrm(k, shape, scale):
        return jax.random.normal(k, shape, F32) * scale

    ret_init = jnp.log(2.0 ** jnp.arange(5, 5 + N_HEADS_RET, dtype=F32) - 1.0)
    return {
        "x_prompt": nrm(ks[0], (BATCH, SEQ, D), 1.0),
        "x_sample": nrm(ks[1], (DEC_BATCH, DEC_SEQ, D), 1.0),
        "c": nrm(ks[2], (DEC_BATCH, D), 1.0),
        "cache_na_k": nrm(ks[3], (DEC_BATCH, DEPTH, N_HEADS_NA, PAST_LEN, HEAD_DIM), 1.0),
        "cache_na_v": nrm(ks[4], (DEC_BATCH, DEPTH, N_HEADS_NA, PAST_LEN, HEAD_DIM), 1.0),
        "cache_swa_k": nrm(ks[5], (DEC_BATCH, DEPTH, N_KV_SWA, PAST_LEN, HEAD_DIM), 1.0),
        "cache_swa_v": nrm(ks[6], (DEC_BATCH, DEPTH, N_KV_SWA, PAST_LEN, HEAD_DIM), 1.0),
        "state_ret": nrm(ks[7], (DEC_BATCH, DEPTH, 2, N_HEADS_RET, HEAD_DIM, HEAD_DIM), 0.5),
        "c_ctx": nrm(ks[8], (D,), 1.0),
        "ada_w": nrm(ks[9], (DEPTH, D, 6 * D), 0.5 * D ** -0.5),
        "ada_b": nrm(ks[10], (DEPTH, 6 * D), 0.02),
        "norm1_g": 1.0 + nrm(ks[11], (DEPTH, D), 0.05),
        "norm2_g": 1.0 + nrm(ks[12], (DEPTH, D), 0.05),
        "w_in": nrm(ks[13], (DEPTH, D, IN_COLS), D ** -0.5),
        "na_rpb": nrm(ks[14], (DEPTH, N_HEADS_NA, 2 * WIN_ROWS - 1, 2 * WIN_COLS - 1), 0.1),
        "swa_sink": nrm(ks[15], (DEPTH, N_HEADS_SWA), 0.5),
        "ret_decay": ret_init + nrm(ks[16], (DEPTH, 2, N_HEADS_RET), 0.1),
        "ret_norm_g": 1.0 + nrm(ks[17], (DEPTH, WIDTH_RET), 0.05),
        "w_br_na": nrm(ks[18], (DEPTH, WIDTH_NA, D), WIDTH_NA ** -0.5),
        "w_br_swa": nrm(ks[19], (DEPTH, WIDTH_SWA, D), WIDTH_SWA ** -0.5),
        "w_br_ret": nrm(ks[20], (DEPTH, WIDTH_RET, D), WIDTH_RET ** -0.5),
        "w_out": nrm(ks[21], (DEPTH, D, D), D ** -0.5),
        "router_group_w": nrm(ks[22], (DEPTH, D, N_GROUPS), D ** -0.5),
        "router_group_b": nrm(ks[23], (DEPTH, N_GROUPS), 0.01),
        "router_expert_w": nrm(ks[24], (DEPTH, D, N_EXPERTS), D ** -0.5),
        "router_expert_b": nrm(ks[25], (DEPTH, N_EXPERTS), 0.01),
        "w_gate": nrm(ks[26], (DEPTH, N_EXPERTS, D, D_EXPERT), D ** -0.5),
        "w_up": nrm(ks[27], (DEPTH, N_EXPERTS, D, D_EXPERT), D ** -0.5),
        "w_down": nrm(ks[28], (DEPTH, N_EXPERTS, D_EXPERT, D), D_EXPERT ** -0.5),
        "final_norm_g": 1.0 + nrm(ks[29], (D,), 0.05),
    }

def reference(x_prompt, x_sample, c, cache_na_k, cache_na_v, cache_swa_k, cache_swa_v, state_ret,
              c_ctx, ada_w, ada_b, norm1_g, norm2_g, w_in, na_rpb, swa_sink, ret_decay, ret_norm_g,
              w_br_na, w_br_swa, w_br_ret, w_out, router_group_w, router_group_b, router_expert_w,
              router_expert_b, w_gate, w_up, w_down, final_norm_g):
    xp = x_prompt
    xs = x_sample
    na_k, na_v, swa_k, swa_v, ret_s = [], [], [], [], []
    for l in range(DEPTH):
        p = {
            "norm1_g": norm1_g[l], "norm2_g": norm2_g[l], "w_in": w_in[l], "na_rpb": na_rpb[l],
            "swa_sink": swa_sink[l], "ret_decay": ret_decay[l], "ret_norm_g": ret_norm_g[l],
            "w_br_na": w_br_na[l], "w_br_swa": w_br_swa[l], "w_br_ret": w_br_ret[l], "w_out": w_out[l],
            "router_group_w": router_group_w[l], "router_group_b": router_group_b[l],
            "router_expert_w": router_expert_w[l], "router_expert_b": router_expert_b[l],
            "w_gate": w_gate[l], "w_up": w_up[l], "w_down": w_down[l],
        }
        mod_ctx = _modulation(c_ctx, ada_w[l], ada_b[l])
        xp, ka, va, ksw, vsw, sr = _context_layer(xp, mod_ctx, p)
        na_k.append(ka)
        na_v.append(va)
        swa_k.append(ksw)
        swa_v.append(vsw)
        ret_s.append(sr)
        mod_lat = _modulation(c[:, None, :], ada_w[l], ada_b[l])
        xs = _latent_layer(xs, mod_lat, p, cache_na_k[:, l], cache_na_v[:, l],
                           cache_swa_k[:, l], cache_swa_v[:, l], state_ret[:, l])
    y_prompt = _rms(xp, final_norm_g)
    y_sample = _rms(xs, final_norm_g)
    new_na_k = jnp.stack(na_k, axis=1)
    new_na_v = jnp.stack(na_v, axis=1)
    new_swa_k = jnp.stack(swa_k, axis=1)
    new_swa_v = jnp.stack(swa_v, axis=1)
    new_state_ret = jnp.stack(ret_s, axis=1)
    return (y_prompt, y_sample, new_na_k, new_na_v, new_swa_k, new_swa_v, new_state_ret)


_drawn_inputs = setup_inputs


def setup_inputs(seed=0):
    import zlib

    import numpy as np

    out = dict(_drawn_inputs(seed))
    spreads = {}
    factors = {'cache_swa_k': 3.52,
     'na_rpb': 23.596,
     'swa_sink': 39.11,
     'ret_norm_g': 5.761,
     'router_group_b': 17.637,
     'router_expert_b': 22.873,
     'cache_na_k': 2.761}
    for name, (base, spread) in spreads.items():
        noise = np.random.default_rng([zlib.crc32(name.encode()), seed]).standard_normal(out[name].shape)
        drawn = base * np.exp(spread * noise) if base else spread * noise
        out[name] = __import__('jax').numpy.asarray(drawn.astype(out[name].dtype))
    for name, factor in factors.items():
        out[name] = (out[name] * factor).astype(out[name].dtype)
    return out
```

```python
from contextlib import ExitStack

import numpy as np

import concourse.bass as bass
from concourse import mybir

F32 = mybir.dt.float32
ALU = mybir.AluOpType
ACT = mybir.ActivationFunctionType
AX_X = mybir.AxisListType.X

P = 128
D = 1024
DEPTH = 2
TILES = 3
TOK = TILES * P
KT = D // P
GRID_W = 64
HD = 64
HEADS_NA, HEADS_SWA, KV_SWA, HEADS_RET = 8, 4, 2, 4
WIN_COLS, WIN_ROWS = 16, 8
RPB_W = 2 * WIN_COLS - 1
RPB = (2 * WIN_ROWS - 1) * RPB_W
GRID_ROWS = 256 // GRID_W
N_EXP, N_GRP, D_EXP = 16, 4, 256
IN_COLS = 6144
EPS = 1e-6
NEG = -1e30

QA, KA, VA, QS, KS, VS, QR, KR, VR, GR = 0, 512, 1024, 1536, 1792, 1920, 2048, 2304, 2560, 2816
Z_COLS = 3072

CH = 256
SLOTS = 4
Z_CHUNKS = Z_COLS // CH
G_CHUNKS = (IN_COLS - Z_COLS) // CH
LAYER_CHUNKS = 6 * 4 + Z_CHUNKS + G_CHUNKS + 4 + 4 + 2 * N_EXP + N_EXP
SLOT_LOADS = 16 * LAYER_CHUNKS // SLOTS

BIAS_W = P + 6 * GRID_W + P

C_IDENT, C_COS, C_SIN = 0, 128, 192
C_COLMASK = 256
C_SWAMASK = 320
C_POS = 1088
C_IOTA = 1092
C_TURN = 1108
C_END = 1236
C_MASKF, C_MASKB, C_DIFFF, C_DIFFB = 1236, 1364, 1492, 1620
C_ALL = 1748


def constants():
    c = np.zeros((P, C_ALL), np.float32)
    p = np.arange(P)
    c[:, C_IDENT:C_IDENT + P] = np.eye(P)
    inv = (np.float32(10000.0) ** (-np.arange(16, dtype=np.float32) / np.float32(16))).astype(np.float32)
    for t in range(2):
        tok = p + P * t
        ang = np.concatenate([(tok // GRID_W).astype(np.float32)[:, None] * inv,
                              (tok % GRID_W).astype(np.float32)[:, None] * inv], axis=1)
        c[:, C_COS + 32 * t:C_COS + 32 * t + 32] = np.cos(ang)
        c[:, C_SIN + 32 * t:C_SIN + 32 * t + 32] = np.sin(ang)
    col = p % GRID_W
    start = np.clip(col - WIN_COLS // 2, 0, GRID_W - WIN_COLS)
    k = np.arange(GRID_W)
    inside = (k[None] >= start[:, None]) & (k[None] < start[:, None] + WIN_COLS)
    c[:, C_COLMASK:C_COLMASK + GRID_W] = np.where(inside, 0, NEG)
    keys = np.arange(256)
    far0 = np.abs(p[:, None] - keys[None]) > 128
    far1 = np.abs(p[:, None] + P - keys[None]) > 128
    c[:, C_SWAMASK:C_SWAMASK + 256] = np.where(far0, NEG, 0)
    c[:, C_SWAMASK + 384 + 128:C_SWAMASK + 768] = np.where(far1, NEG, 0)
    q = np.arange(P)[None]
    kk = p[:, None]
    c[:, C_MASKF:C_MASKF + P] = q >= kk
    c[:, C_MASKB:C_MASKB + P] = kk >= q
    c[:, C_DIFFF:C_DIFFF + P] = np.maximum(q - kk, 0)
    c[:, C_DIFFB:C_DIFFB + P] = np.maximum(kk - q, 0)
    c[:, C_POS:C_POS + 4] = np.stack([p + 1, P - p, P - 1 - p, p], 1)
    c[:, C_IOTA:C_IOTA + 16] = np.arange(16)[None]
    c[p, C_TURN + (p // GRID_W) * GRID_W + (GRID_W - 1 - p % GRID_W)] = 1
    return c


def build(nc, a, out):
    ctx = ExitStack()
    with ctx:
        def sb(name, shape):
            return ctx.enter_context(nc.sbuf_tensor(name, shape, F32))

        def sem(name):
            return ctx.enter_context(nc.semaphore(name))

        x = sb("x", [P, TILES, D])
        hT = sb("hT", [P, KT, TOK])
        arena = sb("arena", [P, 72 * 256])
        zt = arena[:, 0:TILES * Z_COLS].rearrange("p (t c) -> p t c", t=TILES)
        gates = arena[:, 9216:18432].rearrange("p (f n) -> p f n", n=TOK)
        qkT = arena[:, 9216:9216 + 15 * TOK].rearrange("p (b n) -> p b n", n=TOK)
        rot = arena[:, 15000:15000 + TILES * 384].rearrange("p (t c) -> p t c", t=TILES)
        ret_o = arena[:, 16152:16152 + 768]
        ret_u = arena[:, 16920:16920 + 768]
        ret_w = arena[:, 17688:17688 + 512]
        bias_turned = arena[:, 12288:12288 + HEADS_NA * 384].rearrange("p (h c) -> p h c", c=384)
        zT = arena[:, 0:KT * TOK].rearrange("p (b n) -> p b n", n=TOK)
        aT = arena[:, 0:12288].rearrange("p (e j n) -> p e j n", j=2, n=TOK)
        cw = arena[:, 12288:18432].rearrange("p (e n) -> p e n", n=TOK)
        tgr = arena[:, 15000:15768].rearrange("p (t c) -> p t c", t=TILES)
        ring = sb("ring", [P, SLOTS, KT, CH])
        biasT = sb("biasT", [P, HEADS_NA * BIAS_W])
        bias = biasT[:, :].rearrange("p (h c) -> p h c", c=BIAS_W)
        oT = biasT[:, 0:KT * TOK].rearrange("p (b n) -> p b n", n=TOK)
        gb = sb("gb", [P, 2, D])
        mrow = sb("mrow", [2, 2 * D])
        work = sb("work", [P, 15 * 256])
        sbuf_s = work[:, 0:3072].rearrange("p (g h c) -> p g h c", g=2, h=4)
        pT = work[:, 3072:3840].rearrange("p (b c) -> p b c", b=2)
        xn = work[:, 0:3072].rearrange("p (t c) -> p t c", t=TILES)
        rprod = work[:, 0:1536].rearrange("p (n t h i) -> p n t h i", n=4, t=2, h=6)
        am = work[:, 0:1536].rearrange("p (t c) -> p t c", t=TILES)
        br_u = work[:, 0:384]
        br_w = work[:, 384:768]
        tg = work[:, 0:1536].rearrange("p (a j n) -> p a j n", a=2, j=2)
        gu = work[:, 1536:3072].rearrange("p (a j n) -> p a j n", a=2, j=2)
        cst = sb("cst", [P, C_END])
        once = work[:, 2048:2560]
        kcT = sb("kcT", [P, 5, P])
        cache_k = sb("cache_k", [P, 10, HD])
        cache_v = sb("cache_v", [P, 10, HD])
        cond = sb("cond", [P, KT, 2])
        condr = sb("condr", [P, 2, KT])
        condt = sb("condt", [P, 2, KT])
        gain = sb("gain", [P, 2, KT])
        shift = sb("shift", [P, KT, 2])
        scale = sb("scale", [P, KT, 2])
        ssq = sb("ssq", [P, TILES])
        msq = sb("msq", [P, TILES])
        rstd = sb("rstd", [P, TILES])
        ssq12 = sb("ssq12", [P, 12])
        msq12 = sb("msq12", [P, 12])
        rstd12 = sb("rstd12", [P, 12])
        mhalf = sb("mhalf", [P, 12])
        rw = sb("rw", [P, KT, 20])
        rb = sb("rb", [P, 20])
        ret_g = sb("ret_g", [P, 256])
        sink = sb("sink", [P, 4])
        state0 = sb("state0", [P, 2, 2, HD])
        state1 = sb("state1", [P, 2, 2, HD])
        state_out = sb("state_out", [P, 2, 2, HD])
        kd = sb("kd", [P, 4, 256])
        lg = sb("lg", [P, 16])
        lgt = sb("lgt", [P, 4, 16])
        qdec = sb("qdec", [P, DEPTH, 2, 4])
        kdec = sb("kdec", [P, DEPTH, 2, 4])
        cdec = sb("cdec", [P, DEPTH, 2, 2])
        cdl = sb("cdl", [P, DEPTH, 2, 2])
        dec = sb("dec", [P, DEPTH, 4, P])
        mx = sb("mx", [P, 2, 4])
        nmx = sb("nmx", [P, 2, 4])
        den = sb("den", [P, 2, 4])
        rden = sb("rden", [P, 2, 4])
        sk = sb("sk", [P, 2, 4])
        lo = sb("lo", [P, TILES, 20])
        r4 = sb("r4", [P, 3, TILES, 4])
        r16 = sb("r16", [P, 4, TILES, 16])
        r1 = sb("r1", [P, 8, TILES])
        comb = sb("comb", [P, TILES, 16])
        combT = work[0:16, 0:TOK]
        fing = biasT[:, 0:D]
        ps = ctx.enter_context(nc.psum_tensor("ps", [P, 8, 512], F32))

        ident = cst[:, C_IDENT:C_IDENT + P]

        init_loaded = sem("init_loaded")
        INIT_LOADS = 7
        SMALL_L = 16 * 27
        init_dve = sem("init_dve")
        act_init = sem("act_init")
        slot_loaded = [sem(f"slot_loaded{i}") for i in range(SLOTS)]
        chunk_done = sem("chunk_done")
        gains_loaded = sem("gains_loaded")
        small_loaded = sem("small_loaded")
        adab_loaded = sem("adab_loaded")
        ADA = 12
        ada_row = sem("ada_row")
        mod_psum, MODP = sem("mod_psum"), 2
        mod_ready, MODR = sem("mod_ready"), 4
        gb_psum, GB = sem("gb_psum"), 8
        gb_ready = sem("gb_ready")
        x_ready, XR = sem("x_ready"), 2
        ssq_ready, SSQ = sem("ssq_ready"), 6
        pool_step = sem("pool_step")
        POOL_L = 3
        rstd_ready, RS = sem("rstd_ready"), 2
        xn_ready, XN = sem("xn_ready"), 6
        xT_psum, XT = sem("xT_psum"), 16
        hT_dve, HT = sem("hT_dve"), 16
        hT_act = sem("hT_act")
        zt_dve, ZD = sem("zt_dve"), Z_CHUNKS // 2
        zt_act = sem("zt_act")
        kv_stored = sem("kv_stored")
        KV_L = 5 * 16
        rot_act = sem("rot_act")
        rot_dve = sem("rot_dve")
        RD = 6
        t_psum, TP = sem("t_psum"), 17
        t_dve, TD = sem("t_dve"), 9
        t_act, TA = sem("t_act"), 8
        bias_psum = sem("bias_psum")
        bias_ready = sem("bias_ready")
        BIAS_L = 2 + HEADS_NA
        s_psum, SU = sem("s_psum"), 36
        s_ready = sem("s_ready")
        nmax_ready, NG = sem("nmax_ready"), 9
        exp_ready = sem("exp_ready")
        sink_exp = sem("sink_exp")
        pt_psum = sem("pt_psum")
        pT_ready = sem("pT_ready")
        pv_done = sem("pv_done")
        o_ready = sem("o_ready")
        kd_ready = sem("kd_ready")
        kv_psum = sem("kv_psum")
        state_ready = sem("state_ready")
        a_psum = sem("a_psum")
        am_ready = sem("am_ready")
        ro_psum = sem("ro_psum")
        tgr_ready = sem("tgr_ready")
        ret_ssq = sem("ret_ssq")
        rsq_ready = sem("rsq_ready")
        router_sub = sem("router_sub")
        router_exp = sem("router_exp")
        ro_ready = sem("ro_ready")
        ot_psum = sem("ot_psum")
        ot_dve = sem("ot_dve")
        ot_act = sem("ot_act")
        gate_psum = sem("gate_psum")
        GT = 24
        gate_ready = sem("gate_ready")
        br_psum = sem("br_psum")
        br_read = sem("br_read")
        zT_ready = sem("zT_ready")
        out_read = sem("out_read")
        lo_psum = sem("lo_psum")
        comb_ready = sem("comb_ready")
        combT_psum = sem("combT_psum")
        combT_ready = sem("combT_ready")
        cw_psum = sem("cw_psum")
        cw_ready = sem("cw_ready")
        e_tanh = sem("e_tanh")
        e_mul = sem("e_mul")
        e_read = sem("e_read")
        aT_ready = sem("aT_ready")
        dve_chain = sem("dve_chain")
        DVE_CHAIN = 103
        fin_ready = sem("fin_ready")
        stored = sem("stored")

        w_in = a["w_in"]
        w_br = [a["w_br_na"], a["w_br_swa"], a["w_br_ret"]]

        GROUPS = [(t, kind) for t in range(TILES) for kind in range(3)]
        SCALED = (0, 1, 2, 3, 8, 9, 13, 14)
        POSITION = [0, 2, 1, 3]

        SEG = {}
        n = 0
        for name, count in (("ada0", 8), ("z", Z_CHUNKS), ("g", G_CHUNKS), ("ada2", 4), ("br", 4), ("out", 4),
                            ("ada3", 8), ("exp", 2 * N_EXP), ("ada5", 4), ("down", N_EXP)):
            SEG[name] = n
            n += count
        BR_EXTRA = 32
        SLOT_LAYER = SLOT_LOADS + BR_EXTRA

        passed = sem("passed")

        def wait_apart(eng, semaphore, value):
            eng.wait_ge(semaphore, value)
            eng.sem_inc(passed, 1)

        INTER = {1: (3, 0), 2: (4, 1)}

        block = ctx.enter_context(nc.Block())

        @block.sync
        def _(sp):
            sp.sem_inc(chunk_done, SLOTS)
            for one in (x_ready, aT_ready, ada_row, zt_dve, zt_act):
                sp.sem_inc(one, 1)
            sp.dma_start(x[:, 0, :], a["x_prompt"][0]).then_inc(init_loaded, 16)
            sp.dma_start(x[:, 1:3, :], a["x_sample"][0].rearrange("(t p) d -> p t d", p=P)).then_inc(init_loaded, 16)
            sp.dma_start(cst[:, :], a["consts"][:, 0:C_END]).then_inc(init_loaded, 16)
            sp.dma_start(condr[:, 0, :], a["c_ctx"].rearrange("(p k) -> p k", k=KT)).then_inc(init_loaded, 16)
            sp.dma_start(condr[:, 1, :], a["c"][0].rearrange("(p k) -> p k", k=KT)).then_inc(init_loaded, 16)
            sp.dma_start(lgt[:, 0, :], a["ret_decay"].rearrange("l r h -> (l r h)").unsqueeze(0).to_broadcast([P, 16])).then_inc(init_loaded, 16)

            sp.dma_start(once, a["consts"][:, C_END:C_ALL]).then_inc(init_loaded, 16)

            def put(slot, src, l, seq):
                sp.wait_ge(chunk_done, l * LAYER_CHUNKS + (seq + 1))
                sp.dma_start(ring[:, slot] if src.shape[1] == KT else
                             ring[:, slot].rearrange("p k c -> p (k c)").rearrange("p (j n) -> p j n", n=D),
                             src).then_inc(slot_loaded[slot], 16)

            with sp.Fori(0, DEPTH) as l:
                seq = [0]

                def columns(w, first, count, rows="(p k) c -> p k c"):
                    base = seq[0]
                    with sp.Fori(0, count // SLOTS) as i:
                        for s in range(SLOTS):
                            col = sp.snap(i * (SLOTS * CH) + (first + s * CH))
                            kw = {"k": KT} if rows.startswith("(p k)") else {"p": P}
                            src = w[bass.ds(l, 1)].rearrange("a r c -> (a r) c").rearrange(rows, **kw)[:, :, bass.ds(col, CH)]
                            put(s, src, l, i * SLOTS + (base + s))
                    seq[0] += count

                columns(a["ada_w"], 0, 8)
                columns(w_in, 0, Z_CHUNKS)
                columns(w_in, Z_COLS, G_CHUNKS)
                columns(a["ada_w"], 2 * D, 4)
                for s in range(4):
                    sp.wait_ge(chunk_done, l * LAYER_CHUNKS + (seq[0] + s + 1))
                    for w, k0, kn in ((0, 0, 4), (1, 4, 2), (2, 6, 2)):
                        sp.dma_start(ring[:, s, k0:k0 + kn, :],
                                     w_br[w][bass.ds(l, 1)].rearrange("a (k p) c -> p (a k) c", p=P)[:, :, s * CH:(s + 1) * CH]
                                     ).then_inc(slot_loaded[s], 16)
                seq[0] += 4
                columns(a["w_out"], 0, 4, "(k p) c -> p k c")
                columns(a["ada_w"], 3 * D, 8)
                base = seq[0]
                with sp.Fori(0, N_EXP // 2) as i:
                    for s in range(SLOTS):
                        w = (a["w_gate"], a["w_up"])[s % 2]
                        e = sp.snap(l * N_EXP + i * 2 + s // 2)
                        src = w.rearrange("l e r c -> (l e) r c")[bass.ds(e, 1)].rearrange("a (p k) c -> p (a k) c", k=KT)
                        put(s, src, l, i * SLOTS + (base + s))
                seq[0] += 2 * N_EXP
                columns(a["ada_w"], 5 * D, 4)
                base = seq[0]
                with sp.Fori(0, N_EXP // SLOTS) as i:
                    for s in range(SLOTS):
                        e = sp.snap(l * N_EXP + i * SLOTS + s)
                        src = a["w_down"].rearrange("l e r c -> (l e) r c")[bass.ds(e, 1)].rearrange("a (p j) c -> p (a j) c", j=2)
                        put(s, src, l, i * SLOTS + (base + s))
                seq[0] += N_EXP
                assert seq[0] == LAYER_CHUNKS

        @block.tensor
        def _(pe):
            def loaded(seg, l, i, s):
                first = 16 * (SEG[seg] // SLOTS + 1) + (BR_EXTRA if SEG[seg] >= SEG["br"] else 0)
                pe.wait_ge(slot_loaded[s], l * SLOT_LAYER + i * 16 + first)

            def columns_of_mod(l, section, which):
                pe.wait_ge(ada_row, l * ADA + 2 * section + 4 + 1)
                for sec in range(2):
                    for k in range(KT):
                        mm = pe.matmul(ps[:, 4, (sec * KT + k) * 2:(sec * KT + k) * 2 + 2],
                                       mrow[0:2, sec * D + k:(sec + 1) * D:KT], cst[0:2, C_IDENT:C_IDENT + 2],
                                       start=True, stop=True)
                mm.then_inc(mod_psum, 1)

            def broadcast_gate(l, section):
                pe.wait_ge(ada_row, l * ADA + 2 * section + 2 + 1)
                for cnd in range(2):
                    for half in range(2):
                        pe.matmul(ps[:, 4 + 2 * cnd + half, :], cst[0:2, C_IDENT + cnd:C_IDENT + cnd + 1].to_broadcast([2, P]),
                                  mrow[0:2, half * 512:(half + 1) * 512], start=True, stop=True).then_inc(gb_psum, 1)

            def norm_transposes(l, which):
                pe.wait_ge(mod_ready, l * MODR + 2 * which + 2)
                pe.wait_ge(xn_ready, l * XN + 3 * which + 3)
                for k in range(KT):
                    for t in range(TILES):
                        mm = pe.transpose(ps[:, k, t * P:(t + 1) * P], xn[:, t, k:D:KT], ident)
                    mm.then_inc(xT_psum, 1)
                pe.wait_ge(hT_dve, l * HT + 8 * which + 8)
                wait_apart(pe, hT_act, l * HT + 8 * which + 8)

            pe.wait_ge(init_loaded, 16 * INIT_LOADS)
            pe.wait_ge(init_dve, 3)
            with pe.Fori(0, DEPTH) as l:
                def ada_rows(seg, section, count):
                    wait_apart(pe, ada_row, l * ADA + 2 * section + 1)
                    with pe.Fori(0, count) as i:
                        pe.wait_ge(ada_row, l * ADA + i * 2 + 2 * section + 1)
                        for s in range(SLOTS):
                            loaded(seg, l, i, s)
                            for k in range(KT):
                                mm = pe.matmul(ps[0:2, s // 2, (s % 2) * CH:(s % 2 + 1) * CH], cond[:, k, :],
                                               ring[:, s, k, :], start=(k == 0), stop=(k == KT - 1))
                            mm.then_inc(chunk_done, 1)

                pe.wait_ge(x_ready, l * XR + 1)
                ada_rows("ada0", 0, 2)
                columns_of_mod(l, 0, 0)
                norm_transposes(l, 0)
                with pe.Fori(0, Z_CHUNKS // SLOTS) as i:
                    for s in range(SLOTS):
                        loaded("z", l, i, s)
                        b = 3 * (s % 2)
                        if s % 2 == 0:
                            pe.wait_ge(zt_dve, l * ZD + i * 2 + s // 2 + 1)
                        else:
                            pe.wait_ge(zt_act, l * ZD + i * 2 + s // 2 + 1)
                        for t in range(TILES):
                            for k in range(KT):
                                mm = pe.matmul(ps[:, b + t, 0:CH], hT[:, k, t * P:(t + 1) * P], ring[:, s, k, :],
                                               start=(k == 0), stop=(k == KT - 1))
                        mm.then_inc(chunk_done, 1)

                pe.wait_ge(zt_dve, l * ZD + ZD + 1)
                pe.wait_ge(zt_act, l * ZD + ZD + 1)
                pe.wait_ge(small_loaded, l * SMALL_L + SMALL_L)
                for h in range(HEADS_NA):
                    pe.matmul(ps[:, h, 0:384], cst[:, C_TURN:C_TURN + P], bias_turned[:, h, :],
                              start=True, stop=True).then_inc(bias_psum, 1)

                pe.wait_ge(bias_ready, l * BIAS_L + BIAS_L)
                for u in range(TP):
                    if u == 10:
                        pe.wait_ge(rot_dve, l * RD + RD)
                        pe.wait_ge(rot_act, l * 2 + 2)
                    if u >= 8:
                        pe.wait_ge(*((t_dve, l * TD + ((u - 8) // 2 + 1)) if u % 2 == 0 else
                                     (t_act, l * TA + ((u - 8) // 2 + 1))))
                    b = u % 8
                    if u == 8:
                        for j in range(4):
                            mm = pe.transpose(ps[:, b, j * P:(j + 1) * P],
                                              cache_k[:, 2 * j:2 * j + 2, :].rearrange("p h d -> p (h d)"), ident)
                    elif u == 9:
                        mm = pe.transpose(ps[:, b, 0:P], cache_k[:, 8:10, :].rearrange("p h d -> p (h d)"), ident)
                    else:
                        v = u if u < 8 else u - 2
                        for t in range(TILES):
                            if v < 8:
                                src = zt[:, t, QA + v * P:QA + (v + 1) * P]
                            elif v < 11:
                                src = rot[:, t, (v - 8) * P:(v - 7) * P]
                            else:
                                src = zt[:, t, QR + (v - 11) * P:QR + (v - 10) * P]
                            mm = pe.transpose(ps[:, b, t * P:(t + 1) * P], src, ident)
                    mm.then_inc(t_psum, 1)

                pe.wait_ge(t_dve, l * TD + TD)
                pe.wait_ge(t_act, l * TA + TA)

                def heads_of(g):
                    t, kind = GROUPS[g]
                    for j in range(4):
                        if kind < 2:
                            h = 4 * kind + j
                            hp, qb, kb, cb = HD * (h % 2), h // 2, 4 + h // 2, h // 2
                            v0, vc = VA + h * HD, h
                        else:
                            pos = POSITION[j]
                            hp, qb, kb, cb = HD * (pos % 2), 8 + pos // 2, 10, 4
                            v0, vc = VS + (j // 2) * HD, 8 + j // 2
                        yield t, j, hp, qb, kb, cb, v0, vc

                def scores(g):
                    for t, j, hp, qb, kb, cb, v0, vc in heads_of(g):
                        u = 4 * g + j
                        if u >= 4:
                            pe.wait_ge(s_ready, l * SU + (u - 3))
                        q = qkT[hp:hp + HD, qb, t * P:(t + 1) * P]
                        if t == 0:
                            mm = pe.matmul(ps[:, u % 4, 0:P], q, qkT[hp:hp + HD, kb, 0:P], start=True, stop=True)
                        else:
                            loc, c0 = (0, 256) if t == 1 else (P, 0)
                            pe.matmul(ps[:, u % 4, loc:loc + 256], q, qkT[hp:hp + HD, kb, P:TOK], start=True, stop=True)
                            mm = pe.matmul(ps[:, u % 4, c0:c0 + P], q, kcT[hp:hp + HD, cb, :], start=True, stop=True)
                        mm.then_inc(s_psum, 1)

                def prob_transposes(g, j):
                    t = GROUPS[g][0]
                    u = 4 * g + j
                    pe.wait_ge(exp_ready, l * SU + (u + 1))
                    if u >= 2:
                        pe.wait_ge(pT_ready, l * SU + (u - 1))
                    for c in range(1 if t == 0 else 3):
                        mm = pe.transpose(ps[:, 4 + u % 2, c * P:(c + 1) * P], sbuf_s[:, g % 2, j, c * P:(c + 1) * P], ident)
                    mm.then_inc(pt_psum, 1)

                def values(g, jj):
                    for t, j, hp, qb, kb, cb, v0, vc in heads_of(g):
                        if j != jj:
                            continue
                        u = 4 * g + j
                        if j == 0 and g >= 2:
                            pe.wait_ge(o_ready, l * NG + (g - 1))
                        pe.wait_ge(pT_ready, l * SU + (u + 1))
                        new = [zt[:, tt, v0:v0 + HD] for tt in (1, 2)]
                        old = cache_v[:, vc, :]
                        vs = {0: [zt[:, 0, v0:v0 + HD]], 1: new + [old], 2: [old] + new}[t]
                        for c, v in enumerate(vs):
                            mm = pe.matmul(ps[:, 6 + g % 2, j * HD:(j + 1) * HD], pT[:, u % 2, c * P:(c + 1) * P], v,
                                           start=(c == 0), stop=(c == len(vs) - 1))
                        mm.then_inc(pv_done, 1)

                scores(0)
                for g in range(NG):
                    if g + 1 < NG:
                        scores(g + 1)
                    prob_transposes(g, 0)
                    for j in range(4):
                        if j < 3:
                            prob_transposes(g, j + 1)
                        values(g, j)

                pe.wait_ge(o_ready, l * NG + NG)
                pe.wait_ge(kd_ready, l * 4 + 4)
                for i, t in enumerate((0, 0, 1, 2)):
                    for hb in range(2):
                        mm = pe.matmul(ps[:, i // 2, ((i % 2) * 2 + hb) * P:((i % 2) * 2 + hb + 1) * P],
                                       kd[:, i, hb * P:(hb + 1) * P], zt[:, t, VR + hb * P:VR + (hb + 1) * P],
                                       start=True, stop=True)
                    if i % 2:
                        mm.then_inc(kv_psum, 1)
                for t in range(TILES):
                    for h in range(4):
                        hp = HD * (h % 2)
                        mm = pe.matmul(ps[:, (2, 5)[h % 2] + t, (h // 2) * P:(h // 2 + 1) * P], qkT[hp:hp + HD, 13 + h // 2, t * P:(t + 1) * P],
                                       qkT[hp:hp + HD, 11 + h // 2, t * P:(t + 1) * P], start=True, stop=True)
                    mm.then_inc(a_psum, 1)
                for t in range(TILES):
                    pe.wait_ge(am_ready, l * 3 + (t + 1))
                    if t == 1:
                        pe.wait_ge(state_ready, l * 10 + 10)
                    for h in range(4):
                        mm = pe.matmul(ps[:, 5 + t, h * HD:(h + 1) * HD], am[:, t, h * P:(h + 1) * P],
                                       zt[:, t, VR + h * HD:VR + (h + 1) * HD], start=True, stop=True)
                    if t:
                        for d in range(2):
                            st = state0 if (t == 1) == (d == 0) else state1
                            for h in range(4):
                                hp = HD * (h % 2)
                                o = (2 * d + h // 2) * HD
                                mm = pe.matmul(ps[:, INTER[t][h % 2], o:o + HD], qkT[hp:hp + HD, 11 + h // 2, t * P:(t + 1) * P],
                                               st[hp:hp + HD, d, h // 2, :], start=True, stop=True)
                    mm.then_inc(ro_psum, 1)

                pe.wait_ge(ro_ready, l * 1 + 1)
                for j in range(KT):
                    c0 = (QA + j * P) if j < 4 else (QS + (j - 4) * P) if j < 6 else QR + (j - 6) * P
                    for t in range(TILES):
                        mm = pe.transpose(ps[:, j, t * P:(t + 1) * P], zt[:, t, c0:c0 + P], ident)
                    mm.then_inc(ot_psum, 1)

                pe.wait_ge(ot_dve, l * 4 + 4)
                wait_apart(pe, ot_act, l * 4 + 4)
                with pe.Fori(0, G_CHUNKS // SLOTS) as i:
                    for s in range(SLOTS):
                        loaded("g", l, i, s)
                        for j in range(2):
                            b = 2 * s + j
                            pe.wait_ge(gate_ready, l * GT + i * 8 + (b + 1))
                            for k in range(KT):
                                mm = pe.matmul(ps[:, b, 0:TOK], ring[:, s, k, j * P:(j + 1) * P], hT[:, k, :],
                                               start=(k == 0), stop=(k == KT - 1))
                            mm.then_inc(gate_psum if j == 0 else chunk_done, 1)

                pe.wait_ge(gate_ready, l * GT + GT + 8)
                ada_rows("ada2", 2, 1)
                broadcast_gate(l, 2)

                for j in range(KT):
                    s = j // 2
                    b = 3 * (j % 2)
                    if j % 2 == 0:
                        first = 16 * (SEG["br"] // SLOTS) + 48
                        pe.wait_ge(slot_loaded[s], l * SLOT_LAYER + first)
                    if j == 0:
                        pe.wait_ge(gb_ready, l * GB + 4)
                    if j >= 2:
                        pe.wait_ge(br_read, l * 8 + (j - 1))
                    for n_, (k0, kn) in enumerate(((0, 4), (4, 2), (6, 2))):
                        for k in range(k0, k0 + kn):
                            mm = pe.matmul(ps[:, b + n_, 0:TOK], ring[:, s, k, (j % 2) * P:(j % 2 + 1) * P], oT[:, k, :],
                                           start=(k == k0), stop=(k == k0 + kn - 1))
                    mm.then_inc(br_psum if j % 2 == 0 else chunk_done, 1)

                pe.wait_ge(br_read, l * 8 + 8)
                pe.wait_ge(zT_ready, l * 8 + 8)
                for s in range(4):
                    loaded("out", l, 0, s)
                    if s >= 2:
                        pe.wait_ge(out_read, l * 4 + (s - 1))
                    for t in range(TILES):
                        for k in range(KT):
                            mm = pe.matmul(ps[:, 3 * (s % 2) + t, 0:CH], zT[:, k, t * P:(t + 1) * P], ring[:, s, k, :],
                                           start=(k == 0), stop=(k == KT - 1))
                    mm.then_inc(chunk_done, 1)

                pe.wait_ge(out_read, l * 4 + 4)
                ada_rows("ada3", 3, 2)
                columns_of_mod(l, 3, 1)
                norm_transposes(l, 1)

                for t in range(TILES):
                    for k in range(KT):
                        mm = pe.matmul(ps[:, 0, t * 20:(t + 1) * 20], hT[:, k, t * P:(t + 1) * P], rw[:, k, :],
                                       start=(k == 0), stop=(k == KT - 1))
                mm.then_inc(lo_psum, 1)
                pe.wait_ge(comb_ready, l * 1 + 1)
                for t in range(TILES):
                    mm = pe.transpose(ps[0:16, 1, t * P:(t + 1) * P], comb[:, t, :], ident)
                mm.then_inc(combT_psum, 1)
                pe.wait_ge(combT_ready, l * 1 + 1)
                for e in range(N_EXP):
                    if e >= 6:
                        pe.wait_ge(cw_ready, l * N_EXP + (e - 5))
                    pe.matmul(ps[:, 2 + e % 6, 0:TOK], cst[0:16, C_IDENT + e:C_IDENT + e + 1].to_broadcast([16, P]),
                              combT, start=True, stop=True).then_inc(cw_psum, 1)

                wait_apart(pe, cw_ready, l * N_EXP + N_EXP)
                with pe.Fori(0, N_EXP // 2) as i:
                    for ab in range(2):
                        pe.wait_ge(e_read, l * N_EXP + i * 2 + (ab + 1))
                        for w in range(2):
                            s = 2 * ab + w
                            loaded("exp", l, i, s)
                            for j in range(2):
                                for k in range(KT):
                                    mm = pe.matmul(ps[:, 4 * ab + 2 * w + j, 0:TOK], ring[:, s, k, j:CH:2], hT[:, k, :],
                                                   start=(k == 0), stop=(k == KT - 1))
                            mm.then_inc(chunk_done, 1)

                pe.wait_ge(e_read, l * N_EXP + N_EXP + 2)
                ada_rows("ada5", 5, 1)
                broadcast_gate(l, 5)

                pe.wait_ge(aT_ready, l * N_EXP + N_EXP + 1)
                pe.wait_ge(ada_row, l * ADA + ADA + 1)
                pe.wait_ge(gb_ready, l * GB + GB)
                for e in range(N_EXP):
                    s = e % SLOTS
                    loaded("down", l, e // SLOTS, s)
                    w = ring[:, s].rearrange("p k c -> p (k c)").rearrange("p (j n) -> p j n", n=D)
                    for t in range(TILES):
                        for half in range(2):
                            for j in range(2):
                                mm = pe.matmul(ps[:, 2 * t + half, :], aT[:, e, j, t * P:(t + 1) * P],
                                               w[:, j, half * 512:(half + 1) * 512],
                                               start=(e == 0 and j == 0), stop=(e == N_EXP - 1 and j == 1))
                    mm.then_inc(chunk_done, 1)

        @block.vector
        def _(dve):
            count = [0]

            def link(ins):
                count[0] += 1
                ins.then_inc(dve_chain, 1)

            def linked(l):
                dve.wait_ge(dve_chain, l * DVE_CHAIN + count[0])

            def bcast(ap, shape, axis):
                return ap.unsqueeze(axis).to_broadcast(shape)

            dve.wait_ge(init_loaded, 16 * INIT_LOADS)
            dve.memset(mhalf[:, :], -0.5)
            dve.scalar_tensor_tensor(out=lgt[:, 1, :], in0=lgt[:, 0, :], scalar=-1.0, in1=lgt[:, 0, :],
                                     op0=ALU.mult, op1=ALU.max).then_inc(init_dve, 1)
            dve.wait_ge(act_init, 1)
            dve.scalar_tensor_tensor(out=cond[:, :, :].rearrange("p k c -> p c k"), in0=condt[:, :, :], scalar=1.0, in1=condr[:, :, :],
                                     op0=ALU.add, op1=ALU.mult).then_inc(init_dve, 1)
            dve.wait_ge(init_dve, 2)
            dve.tensor_scalar(cond[:, :, :], cond[:, :, :], 0.5, None, ALU.mult).then_inc(init_dve, 1)
            dve.wait_ge(act_init, 3)
            dve.scalar_tensor_tensor(out=lg[:, :], in0=lgt[:, 0, :], scalar=0.0, in1=lgt[:, 3, :],
                                     op0=ALU.min, op1=ALU.subtract).then_inc(init_dve, 1)
            dve.wait_ge(init_dve, 4)
            lgv = lg[:, :].rearrange("p (l r h) -> p l r h", l=DEPTH, r=2)
            for d in range(2):
                dve.tensor_scalar(qdec[:, :, d, :], lgv[:, :, d, :], cst[:, C_POS + d:C_POS + d + 1], None,
                                  ALU.mult).then_inc(init_dve, 1)
                dve.tensor_scalar(kdec[:, :, d, :], lgv[:, :, d, :], cst[:, C_POS + 2 + d:C_POS + 3 + d], None,
                                  ALU.mult).then_inc(init_dve, 1)
                rows = slice(d * HD, (d + 1) * HD)
                dve.tensor_scalar(cdl[rows, :, :, :], lgv[rows, :, :, d:4:2], float(P), None,
                                  ALU.mult).then_inc(init_dve, 1)
            dve.wait_ge(act_init, 22)
            dve.tensor_scalar(kdec[:, :, :, :], kdec[:, :, :, :], HD ** -0.5, None, ALU.mult).then_inc(init_dve, 1)
            decv = dec[:, :, :, :].rearrange("p l h q -> p (l h) q")
            back = work[:, 0:1024].rearrange("p (n q) -> p n q", q=P)
            dve.tensor_tensor(decv, decv, bcast(once[:, 0:128], [P, 8, P], 1), ALU.mult).then_inc(init_dve, 1)
            dve.tensor_tensor(back, back, bcast(once[:, 128:256], [P, 8, P], 1), ALU.mult).then_inc(init_dve, 1)
            dve.wait_ge(init_dve, 13)
            dve.tensor_tensor(decv, decv, back, ALU.add).then_inc(init_dve, 1)
            dve.wait_ge(init_dve, 14)

            with dve.Fori(0, DEPTH) as l:
                def done(seg, n):
                    dve.wait_ge(chunk_done, l * LAYER_CHUNKS + (SEG[seg] + SLOTS) + n)

                def ada_rows(seg, which, count):
                    wait_apart(dve, adab_loaded, l * 64 + 16 * (which + 1))
                    with dve.Fori(0, count) as i:
                        for b in range(2):
                            done(seg, i * SLOTS + 2 * (b + 1))
                            row = mrow[0:2, bass.ds(i * D + b * 512, 512)]
                            dve.tensor_tensor(row, row, ps[0:2, b, :], ALU.add).then_inc(ada_row, 1)

                def modulation_columns(which):
                    dve.wait_ge(mod_psum, l * MODP + which + 1)
                    dve.wait_ge(gains_loaded, l * 32 + 32)
                    v = ps[:, 4, 0:32].rearrange("p (s k c) -> p s k c", s=2, c=2)
                    dve.tensor_copy(shift[:, :, :], v[:, 0]).then_inc(mod_ready, 1)
                    dve.scalar_tensor_tensor(out=scale[:, :, :], in0=v[:, 1], scalar=1.0,
                                             in1=bcast(gain[:, which, :], [P, KT, 2], 2),
                                             op0=ALU.add, op1=ALU.mult).then_inc(mod_ready, 1)

                def norm(which):
                    dve.wait_ge(rstd_ready, l * RS + which + 1)
                    for t in range(TILES):
                        dve.tensor_scalar(xn[:, t, :], x[:, t, :], rstd[:, t:t + 1], None, ALU.mult).then_inc(xn_ready, 1)
                    dve.wait_ge(mod_ready, l * MODR + 2 * which + 2)
                    for k in range(0, KT, 2):
                        dve.wait_ge(xT_psum, l * XT + 8 * which + k + 1)
                        for c, (n0, n1) in enumerate(((0, P), (P, TOK))):
                            dve.tensor_scalar(hT[:, k, n0:n1], ps[:, k, n0:n1], scale[:, k, c:c + 1], shift[:, k, c:c + 1],
                                              ALU.mult, ALU.add).then_inc(hT_dve, 1)

                ada_rows("ada0", 0, 2)
                modulation_columns(0)
                norm(0)

                with dve.Fori(0, Z_CHUNKS // SLOTS) as i:
                    for s in (0, 2):
                        done("z", i * SLOTS + (s + 1))
                        dve.tensor_copy(zt[:, :, bass.ds(i * (SLOTS * CH) + s * CH, CH)],
                                        ps[:, 0:3, 0:CH]).then_inc(zt_dve, 1)

                for h in range(HEADS_NA):
                    dve.wait_ge(bias_psum, l * HEADS_NA + h + 1)
                    dve.tensor_tensor(bias[:, h, P:P + 384].rearrange("p (s c) -> p s c", s=6),
                                      ps[:, h, 0:384].rearrange("p (s c) -> p s c", s=6),
                                      bcast(cst[:, C_COLMASK:C_COLMASK + GRID_W], [P, 6, GRID_W], 1),
                                      ALU.add).then_inc(bias_ready, 1)

                dve.wait_ge(zt_dve, l * ZD + ZD + 1)
                dve.wait_ge(zt_act, l * ZD + ZD + 1)
                for n, (odd, tab) in enumerate(((0, C_COS), (1, C_SIN), (0, C_SIN), (1, C_COS))):
                    src = zt[:, 1:3, QS + odd:QS + 384:2].rearrange("p t (h i) -> p t h i", i=32)
                    tabs = bcast(cst[:, tab:tab + 64].rearrange("p (t i) -> p t i", t=2), [P, 2, 6, 32], 2)
                    link(dve.tensor_tensor(rprod[:, n], src, tabs, ALU.mult))
                linked(l)
                for odd in range(2):
                    op = ALU.add if odd else ALU.subtract
                    for t in range(2):
                        o = rot[:, 1 + t, odd:256:2].rearrange("p (ha hb i) -> p hb ha i", ha=2, hb=2)
                        i0, i1 = (rprod[:, 2 * odd + m, t, 0:4, :].rearrange("p (hb ha) i -> p hb ha i", ha=2) for m in range(2))
                        dve.tensor_tensor(o, i0, i1, op).then_inc(rot_dve, 1)
                    dve.tensor_tensor(rot[:, 1:3, 256 + odd:384:2].rearrange("p t (h i) -> p t h i", i=32),
                                      rprod[:, 2 * odd, :, 4:6, :], rprod[:, 2 * odd + 1, :, 4:6, :], op).then_inc(rot_dve, 1)

                for u in range(0, TP, 2):
                    dve.wait_ge(t_psum, l * TP + u + 1)
                    if u == 8:
                        dve.tensor_copy(kcT[:, 0:4, :].rearrange("p b n -> p (b n)"), ps[:, 0, :]).then_inc(t_dve, 1)
                        continue
                    v = u if u < 8 else u - 2
                    dve.tensor_scalar(qkT[:, v, :], ps[:, u % 8, 0:TOK], HD ** -0.5 if v in SCALED else 1.0, None,
                                      ALU.mult).then_inc(t_dve, 1)

                dve.wait_ge(bias_ready, l * BIAS_L + BIAS_L)
                dve.wait_ge(small_loaded, l * SMALL_L + SMALL_L)

                def maxima(g):
                    t, kind = GROUPS[g]
                    if g >= 2:
                        dve.wait_ge(pt_psum, l * SU + 4 * (g - 1))
                    for j in range(4):
                        wait_apart(dve, s_psum, l * SU + 4 * g + j + 1)
                        w = P if t == 0 else 384
                        h = 4 * kind + j if kind < 2 else 0
                        if kind == 2 and t:
                            add = cst[:, C_SWAMASK + 384 * (t - 1):C_SWAMASK + 384 * t]
                        else:
                            add = bias[:, h, (0, 256, 0)[t]:(0, 256, 0)[t] + w]
                        dve.tensor_tensor_reduce(sbuf_s[:, g % 2, j, 0:w], ps[:, (4 * g + j) % 4, 0:w], add, 1.0, NEG,
                                                 ALU.add, ALU.max, mx[:, g % 2, j:j + 1]).then_inc(s_ready, 1)
                    dve.wait_ge(s_ready, l * SU + 4 * g + 4)
                    if kind == 2:
                        link(dve.tensor_tensor(mx[:, g % 2, :], mx[:, g % 2, :], sink[:, :], ALU.max))
                        linked(l)
                        link(dve.tensor_scalar(nmx[:, g % 2, :], mx[:, g % 2, :], -1.0, None, ALU.mult))
                        linked(l)
                        dve.tensor_tensor(sk[:, g % 2, :], sink[:, :], nmx[:, g % 2, :], ALU.add).then_inc(nmax_ready, 1)
                    else:
                        dve.tensor_scalar(nmx[:, g % 2, :], mx[:, g % 2, :], -1.0, None, ALU.mult).then_inc(nmax_ready, 1)

                def normalise(g):
                    t, kind = GROUPS[g]
                    dve.wait_ge(exp_ready, l * SU + 4 * g + 4)
                    if kind == 2:
                        dve.wait_ge(sink_exp, l * 3 + t + 1)
                        link(dve.tensor_tensor(den[:, g % 2, :], den[:, g % 2, :], sk[:, g % 2, :], ALU.add))
                        linked(l)
                    link(dve.reciprocal(rden[:, g % 2, :], den[:, g % 2, :]))
                    linked(l)
                    dve.wait_ge(pv_done, l * SU + 4 * g + 4)
                    o0 = QA + 256 * kind if kind < 2 else QS
                    dve.tensor_tensor(zt[:, t, o0:o0 + 256].rearrange("p (h d) -> p h d", d=HD),
                                      ps[:, 6 + g % 2, 0:256].rearrange("p (h d) -> p h d", d=HD),
                                      bcast(rden[:, g % 2, :], [P, 4, HD], 2), ALU.mult).then_inc(o_ready, 1)

                maxima(0)
                for g in range(NG):
                    if g + 1 < NG:
                        maxima(g + 1)
                    normalise(g)

                def diagonal(bank, i, par):
                    v = ps[par * HD:(par + 1) * HD, bank, :].rearrange("p (i b e) -> p i b e", i=2, b=2)
                    return v[:, i, :, par * HD:(par + 1) * HD]

                dve.wait_ge(kv_psum, l * 2 + 1)
                for par in range(2):
                    rows = slice(par * HD, (par + 1) * HD)
                    v = ps[rows, 0, :].rearrange("p (i b e) -> p i b e", i=2, b=2)
                    dve.tensor_copy(state_out[rows, :, :, :], v[:, :, :, par * HD:(par + 1) * HD]).then_inc(state_ready, 1)
                dve.wait_ge(kv_psum, l * 2 + 2)
                for d in range(2):
                    for par in range(2):
                        rows = slice(par * HD, (par + 1) * HD)
                        for hb in range(2):
                            dve.scalar_tensor_tensor(
                                out=state1[rows, d, hb, :], in0=state0[rows, d, hb, :],
                                scalar=cdec[rows, :, :, :].rearrange("p l r b -> p (l r b)")[:, bass.ds(l * 4 + (2 * d + hb), 1)],
                                in1=diagonal(1, d, par)[:, hb, :], op0=ALU.mult, op1=ALU.add).then_inc(state_ready, 1)
                def by_parity(ap, n):
                    return ap.rearrange("p (b r n) -> p r b n", b=2, n=n)

                decl = dec[:, :, :, :].rearrange("p l h q -> p (l h q)")[:, bass.ds(l * 512, 512)]
                for t in range(TILES):
                    dve.wait_ge(a_psum, l * 3 + t + 1)
                    for par in range(2):
                        ins = dve.tensor_tensor(by_parity(am[:, t, :], P)[:, par],
                                                ps[:, (2, 5)[par] + t, 0:256].rearrange("p (b q) -> p b q", b=2),
                                                by_parity(decl, P)[:, par], ALU.mult)
                        if par == 0:
                            link(ins)
                    ins.then_inc(am_ready, 1)

                def head_view(ap):
                    return ap.rearrange("p (h d) -> p h d", d=HD)

                for t in range(TILES):
                    dve.wait_ge(ro_psum, l * 3 + t + 1)
                    ot = ret_o[:, t * 256:(t + 1) * 256]
                    if t == 0:
                        link(dve.tensor_copy(ot, ps[:, 5, 0:256]))
                        continue
                    u, w = ret_u[:, t * 256:(t + 1) * 256], ret_w[:, (t - 1) * 256:t * 256]
                    for d, dst in ((0, u), (1, w)):
                        qd = by_parity(qdec[:, :, :, :].rearrange("p l r h -> p (l r h)")[:, bass.ds(l * 8 + 4 * d, 4)], 1)
                        for par in range(2):
                            link(dve.tensor_tensor(by_parity(dst, HD)[:, par],
                                                   ps[:, INTER[t][par], 128 * d:128 * d + 128].rearrange("p (b n) -> p b n", b=2),
                                                   qd[:, par].to_broadcast([P, 2, HD]), ALU.mult))
                    linked(l)
                    link(dve.tensor_tensor(u, u, w, ALU.add))
                    linked(l)
                    link(dve.tensor_tensor(ot, ps[:, 5 + t, 0:256], u, ALU.add))
                linked(l)
                link(dve.tensor_tensor(ret_u, ret_o, ret_o, ALU.mult))
                linked(l)
                dve.tensor_reduce(ssq12[:, :], head_view(ret_u), AX_X, ALU.add).then_inc(ret_ssq, 1)
                dve.wait_ge(rsq_ready, l * 1 + 1)
                link(dve.tensor_tensor(head_view(ret_o), head_view(ret_o), bcast(rstd12[:, :], [P, 12, HD], 2), ALU.mult))
                dve.wait_ge(tgr_ready, l * 1 + 1)
                dve.wait_ge(ret_ssq, l * 1 + 1)
                link(dve.scalar_tensor_tensor(out=ret_u.rearrange("p (t c) -> p t c", t=TILES), in0=tgr, scalar=1.0,
                                              in1=zt[:, :, GR:GR + 256], op0=ALU.add, op1=ALU.mult))
                linked(l)
                ro3 = ret_o.rearrange("p (t c) -> p t c", t=TILES)
                link(dve.tensor_tensor(ro3, ro3, bcast(ret_g[:, :], [P, TILES, 256], 1), ALU.mult))
                linked(l)
                dve.scalar_tensor_tensor(out=zt[:, :, QR:QR + 256], in0=ro3, scalar=0.5,
                                         in1=ret_u.rearrange("p (t c) -> p t c", t=TILES),
                                         op0=ALU.mult, op1=ALU.mult).then_inc(ro_ready, 1)

                for j in range(0, KT, 2):
                    dve.wait_ge(ot_psum, l * KT + j + 1)
                    dve.tensor_copy(oT[:, j, :], ps[:, j, 0:TOK]).then_inc(ot_dve, 1)

                ada_rows("ada2", 1, 1)

                dve.wait_ge(gate_ready, l * GT + GT + 8)
                dve.wait_ge(kv_stored, l * KV_L + KV_L)
                for j in range(KT):
                    if j % 2 == 0:
                        dve.wait_ge(br_psum, l * 4 + j // 2 + 1)
                    else:
                        done("br", j // 2 + 1)
                    b = 3 * (j % 2)
                    dsts = (zT[:, j, :], br_u, br_w)
                    for n in range(3):
                        ins = dve.scalar_tensor_tensor(out=dsts[n], in0=gates[:, n * KT + j, :], scalar=1.0,
                                                       in1=ps[:, b + n, 0:TOK], op0=ALU.add, op1=ALU.mult)
                        if n < 2:
                            link(ins)
                    ins.then_inc(br_read, 1)
                    linked(l)
                    link(dve.tensor_tensor(zT[:, j, :], zT[:, j, :], br_u, ALU.add))
                    linked(l)
                    dve.wait_ge(br_read, l * 8 + j + 1)
                    dve.tensor_tensor(zT[:, j, :], zT[:, j, :], br_w, ALU.add).then_inc(zT_ready, 1)
                    dve.wait_ge(zT_ready, l * 8 + j + 1)

                dve.wait_ge(gb_ready, l * GB + 4)
                for s in range(4):
                    done("out", s + 1)
                    b = 3 * (s % 2)
                    cols = slice(s * CH, (s + 1) * CH)
                    tmp = work[:, (s % 2) * 768:(s % 2 + 1) * 768].rearrange("p (t c) -> p t c", t=TILES)
                    link(dve.tensor_tensor(tmp[:, 0], ps[:, b, 0:CH], gb[:, 0, cols], ALU.mult))
                    dve.tensor_tensor(tmp[:, 1:3], ps[:, b + 1:b + 3, 0:CH], bcast(gb[:, 1, cols], [P, 2, CH], 1),
                                      ALU.mult).then_inc(out_read, 1)
                    linked(l)
                    dve.wait_ge(out_read, l * 4 + s + 1)
                    ins = dve.tensor_tensor(x[:, :, cols], x[:, :, cols], tmp, ALU.add)
                    if s < 3:
                        link(ins)
                    else:
                        ins.then_inc(x_ready, 1)

                ada_rows("ada3", 2, 2)
                modulation_columns(1)
                linked(l)
                dve.wait_ge(x_ready, l * XR + 1 + 1)
                norm(1)

                iota16 = cst[:, C_IOTA:C_IOTA + 16]
                iota4 = cst[:, C_IOTA:C_IOTA + 4]

                def one_hot(values, n, iota, maximum, tmp, idx, out_hot):
                    link(dve.tensor_reduce(maximum, values, AX_X, ALU.max))
                    linked(l)
                    link(dve.tensor_tensor(tmp, values, bcast(maximum, [P, TILES, n], 2), ALU.is_equal))
                    linked(l)
                    link(dve.scalar_tensor_tensor(out=tmp, in0=tmp, scalar=-99.0, in1=bcast(iota, [P, TILES, n], 1),
                                                  op0=ALU.mult, op1=ALU.add))
                    linked(l)
                    link(dve.tensor_reduce(idx, tmp, AX_X, ALU.min))
                    linked(l)
                    link(dve.tensor_tensor(out_hot, tmp, bcast(idx, [P, TILES, n], 2), ALU.is_equal))
                    linked(l)

                dve.wait_ge(lo_psum, l * 1 + 1)
                link(dve.tensor_tensor(lo[:, :, :], ps[:, 0, 0:60].rearrange("p (t c) -> p t c", t=TILES),
                                       bcast(rb[:, :], [P, TILES, 20], 1), ALU.add))
                linked(l)
                g = lo[:, :, 0:4]
                one_hot(g, 4, iota4, r1[:, 0, :], r4[:, 0], r1[:, 1, :], r4[:, 1])
                dve.tensor_tensor(r4[:, 2], g, bcast(r1[:, 0, :], [P, TILES, 4], 2), ALU.subtract).then_inc(router_sub, 1)
                e4 = lo[:, :, 4:20].rearrange("p t (g e) -> p t g e", e=4)
                em = r16[:, 0]
                link(dve.tensor_tensor(em.rearrange("p t (g e) -> p t g e", e=4), e4,
                                       bcast(r4[:, 1], [P, TILES, 4, 4], 3), ALU.mult))
                link(dve.tensor_scalar(r4[:, 0], r4[:, 1], -NEG, NEG, ALU.mult, ALU.add))
                linked(l)
                link(dve.tensor_tensor(em.rearrange("p t (g e) -> p t g e", e=4), em.rearrange("p t (g e) -> p t g e", e=4),
                                       bcast(r4[:, 0], [P, TILES, 4, 4], 3), ALU.add))
                linked(l)
                one_hot(em, 16, iota16, r1[:, 2, :], r16[:, 1], r1[:, 1, :], r16[:, 2])
                link(dve.scalar_tensor_tensor(out=em, in0=r16[:, 2], scalar=2 * NEG, in1=em, op0=ALU.mult, op1=ALU.add))
                linked(l)
                one_hot(em, 16, iota16, r1[:, 3, :], r16[:, 1], r1[:, 1, :], r16[:, 3])
                dve.tensor_tensor(r1[:, 4, :], r1[:, 3, :], r1[:, 2, :], ALU.subtract).then_inc(router_sub, 1)
                dve.wait_ge(router_exp, l * 2 + 1)
                link(dve.tensor_reduce(r1[:, 5, :], r4[:, 2], AX_X, ALU.add))
                linked(l)
                dve.wait_ge(router_exp, l * 2 + 2)
                link(dve.tensor_scalar(r1[:, 6, :], r1[:, 4, :], 1.0, None, ALU.add))
                linked(l)
                link(dve.tensor_tensor(r1[:, 5, :], r1[:, 5, :], r1[:, 6, :], ALU.mult))
                linked(l)
                link(dve.reciprocal(r1[:, 6, :], r1[:, 5, :]))
                linked(l)
                link(dve.tensor_tensor(r1[:, 7, :], r1[:, 6, :], r1[:, 4, :], ALU.mult))
                link(dve.tensor_tensor(r16[:, 0], r16[:, 2], bcast(r1[:, 6, :], [P, TILES, 16], 2), ALU.mult))
                linked(l)
                link(dve.tensor_tensor(r16[:, 1], r16[:, 3], bcast(r1[:, 7, :], [P, TILES, 16], 2), ALU.mult))
                linked(l)
                dve.tensor_tensor(comb[:, :, :], r16[:, 0], r16[:, 1], ALU.add).then_inc(comb_ready, 1)
                dve.wait_ge(combT_psum, l * 1 + 1)
                dve.tensor_copy(combT, ps[0:16, 1, 0:TOK]).then_inc(combT_ready, 1)

                wait_apart(dve, cw_ready, l * N_EXP + N_EXP)
                with dve.Fori(0, N_EXP // 2) as i:
                    for ab in range(2):
                        dve.wait_ge(e_tanh, l * N_EXP + i * 2 + ab + 1)
                        dve.scalar_tensor_tensor(out=gu[:, ab], in0=tg[:, ab], scalar=1.0,
                                                 in1=ps[:, 4 * ab:4 * ab + 2, 0:TOK], op0=ALU.add,
                                                 op1=ALU.mult).then_inc(e_mul, 1)
                        dve.wait_ge(e_mul, l * N_EXP + i * 2 + ab + 1)
                        done("exp", i * SLOTS + 2 * ab + 2)
                        dve.tensor_tensor(gu[:, ab], gu[:, ab], ps[:, 4 * ab + 2:4 * ab + 4, 0:TOK],
                                          ALU.mult).then_inc(e_read, 1)
                        dve.wait_ge(e_read, l * N_EXP + i * 2 + ab + 3)
                        dve.tensor_tensor(arena[:, bass.ds(i * 1536 + ab * 768, 768)].rearrange("p (j n) -> p j n", j=2),
                                          gu[:, ab],
                                          bcast(arena[:, bass.ds(i * 768 + (12288 + ab * 384), 384)], [P, 2, TOK], 1),
                                          ALU.mult).then_inc(aT_ready, 1)

                ada_rows("ada5", 3, 1)
                dve.wait_ge(gb_ready, l * GB + GB)
                dve.wait_ge(aT_ready, l * N_EXP + N_EXP + 1)
                done("down", N_EXP)
                tmp = work[:, 0:3072].rearrange("p (t c) -> p t c", t=TILES)
                for t in range(TILES):
                    link(dve.tensor_tensor(tmp[:, t].rearrange("p (h c) -> p h c", h=2), ps[:, 2 * t:2 * t + 2, :],
                                           gb[:, min(t, 1), :].rearrange("p (h c) -> p h c", h=2), ALU.mult))
                linked(l)
                dve.tensor_tensor(x[:, :, :], x[:, :, :], tmp, ALU.add).then_inc(x_ready, 1)
                dve.wait_ge(x_ready, l * XR + XR + 1)
                assert count[0] == DVE_CHAIN, count[0]

            dve.wait_ge(rstd_ready, DEPTH * RS + 1)
            dve.wait_ge(stored, 16)
            for t in range(TILES):
                dve.scalar_tensor_tensor(out=xn[:, t, :], in0=x[:, t, :], scalar=rstd[:, t:t + 1], in1=fing,
                                         op0=ALU.mult, op1=ALU.mult).then_inc(fin_ready, 1)

        @block.scalar
        def _(act):
            act.wait_ge(init_loaded, 16 * INIT_LOADS)
            act.activation(condt[:, :, :], condr[:, :, :], ACT.Tanh, scale=0.5).then_inc(act_init, 1)
            act.wait_ge(init_dve, 1)
            act.activation(lgt[:, 2, :], lgt[:, 1, :], ACT.Exp, scale=-1.0).then_inc(act_init, 1)
            act.wait_ge(act_init, 2)
            act.activation(lgt[:, 3, :], lgt[:, 2, :], ACT.Ln, bias=1.0).then_inc(act_init, 1)
            act.wait_ge(init_dve, 10)
            act.activation(qdec[:, :, :, :], qdec[:, :, :, :], ACT.Exp).then_inc(act_init, 1)
            act.activation(kdec[:, :, :, :], kdec[:, :, :, :], ACT.Exp).then_inc(act_init, 1)
            act.activation(cdec[:, :, :, :], cdl[:, :, :, :], ACT.Exp).then_inc(act_init, 1)
            for ll in range(DEPTH):
                for h in range(4):
                    n = ll * 8 + h
                    act.activation(dec[:, ll, h, :], once[:, 256:384], ACT.Exp,
                                   scale=lg[:, n:n + 1]).then_inc(act_init, 1)
                    act.activation(work[:, (ll * 4 + h) * P:(ll * 4 + h + 1) * P], once[:, 384:512], ACT.Exp,
                                   scale=lg[:, n + 4:n + 5]).then_inc(act_init, 1)
            act.wait_ge(init_dve, 14)

            def squares(ready):
                act.wait_ge(*ready)
                for t in range(TILES):
                    act.activation(xn[:, t, :], x[:, t, :], ACT.Square, accum_out=ssq[:, t:t + 1]).then_inc(ssq_ready, 1)

            with act.Fori(0, DEPTH) as l:
                def done(seg, n):
                    act.wait_ge(chunk_done, l * LAYER_CHUNKS + (SEG[seg] + SLOTS) + n)

                act.wait_ge(aT_ready, l * N_EXP + 1)
                row = bass.ds(l, 1)
                for n, name in enumerate(("norm1_g", "norm2_g")):
                    act.dma_start(gain[:, n, :], a[name][row].rearrange("a (p k) -> p (a k)", k=KT)).then_inc(gains_loaded, 16)
                loads = [
                    (rw[:, :, 0:4], a["router_group_w"][row].rearrange("a (p k) c -> p (a k) c", k=KT)),
                    (rw[:, :, 4:20], a["router_expert_w"][row].rearrange("a (p k) c -> p (a k) c", k=KT)),
                    (rb[:, 0:4], a["router_group_b"][row].to_broadcast([P, 4])),
                    (rb[:, 4:20], a["router_expert_b"][row].to_broadcast([P, 16])),
                    (ret_g[:, :], a["ret_norm_g"][row].to_broadcast([P, 256])),
                    (sink[:, :], a["swa_sink"][row].to_broadcast([P, 4])),
                    (cache_k[:, 0:8, :], a["cache_na_k"][0][row].rearrange("a h s d -> s (a h) d")),
                    (cache_k[:, 8:10, :], a["cache_swa_k"][0][row].rearrange("a h s d -> s (a h) d")),
                    (cache_v[:, 0:8, :], a["cache_na_v"][0][row].rearrange("a h s d -> s (a h) d")),
                    (cache_v[:, 8:10, :], a["cache_swa_v"][0][row].rearrange("a h s d -> s (a h) d")),
                    (state0[:, :, :, :].rearrange("p r b e -> p (r b) e"),
                     a["state_ret"][0][row].rearrange("a r h d e -> (a r h d) e").rearrange("(n p) e -> p n e", p=P)),
                ]
                for dst, src in loads:
                    act.dma_start(dst, src).then_inc(small_loaded, 16)
                for rp in range(2):
                    for h in range(HEADS_NA):
                        off = l * (HEADS_NA * RPB) + (h * RPB + (5 - rp) * RPB_W + WIN_COLS - GRID_W)
                        src = bass.AP(tensor=a["na_rpb_flat"].tensor, offset=off,
                                      ap=[[1, GRID_W], [RPB_W, 6], [1, GRID_W]])
                        act.dma_start(bias_turned[rp * GRID_W:(rp + 1) * GRID_W, h, :].rearrange("p (s c) -> p s c", s=6),
                                      src).then_inc(small_loaded, 16)

                def norm(which):
                    act.wait_ge(mod_ready, l * MODR + 2 * which + 2)
                    for k in range(1, KT, 2):
                        act.wait_ge(xT_psum, l * XT + 8 * which + k + 1)
                        for c, (n0, n1) in enumerate(((0, P), (P, TOK))):
                            act.activation(hT[:, k, n0:n1], ps[:, k, n0:n1], ACT.Identity, scale=scale[:, k, c:c + 1],
                                           bias=shift[:, k, c:c + 1]).then_inc(hT_act, 1)

                def gate_rows(which, factor):
                    for n in range(4):
                        act.wait_ge(gb_psum, l * GB + 4 * which + n + 1)
                        act.activation(gb[:, n // 2, (n % 2) * 512:(n % 2 + 1) * 512], ps[:, 4 + n, :], ACT.Copy,
                                       scale=factor).then_inc(gb_ready, 1)

                squares((x_ready, l * XR + 1))
                norm(0)

                with act.Fori(0, Z_CHUNKS // SLOTS) as i:
                    for s in (1, 3):
                        done("z", i * SLOTS + (s + 1))
                        act.activation(zt[:, :, bass.ds(i * (SLOTS * CH) + s * CH, CH)], ps[:, 3:6, 0:CH],
                                       ACT.Copy).then_inc(zt_act, 1)

                act.wait_ge(bias_psum, l * HEADS_NA + HEADS_NA)
                act.wait_ge(zt_dve, l * ZD + ZD + 1)
                act.wait_ge(zt_act, l * ZD + ZD + 1)
                act.activation(rot[:, 0, 0:256].rearrange("p (ha hb i) -> p hb ha i", ha=2, hb=2),
                               zt[:, 0, QS:QS + 256].rearrange("p (hb ha i) -> p hb ha i", ha=2, hb=2), ACT.Copy).then_inc(rot_act, 1)
                act.activation(rot[:, 0, 256:384], zt[:, 0, KS:KS + P], ACT.Copy).then_inc(rot_act, 1)

                for u in range(1, TP, 2):
                    act.wait_ge(t_psum, l * TP + u + 1)
                    if u == 9:
                        act.activation(kcT[:, 4, :], ps[:, 1, 0:P], ACT.Copy).then_inc(t_act, 1)
                        continue
                    v = u if u < 8 else u - 2
                    act.activation(qkT[:, v, :], ps[:, u % 8, 0:TOK], ACT.Copy,
                                   scale=HD ** -0.5 if v in SCALED else 1.0).then_inc(t_act, 1)
                act.activation(tgr, zt[:, :, GR:GR + 256], ACT.Tanh, scale=0.5).then_inc(tgr_ready, 1)

                def exps(g):
                    t, kind = GROUPS[g]
                    w = P if t == 0 else 384
                    act.wait_ge(nmax_ready, l * NG + g + 1)
                    for j in range(4):
                        act.activation(sbuf_s[:, g % 2, j, 0:w], sbuf_s[:, g % 2, j, 0:w], ACT.Exp,
                                       bias=nmx[:, g % 2, j:j + 1], accum_out=den[:, g % 2, j:j + 1]).then_inc(exp_ready, 1)
                    if kind == 2:
                        act.activation(sk[:, g % 2, :], sk[:, g % 2, :], ACT.Exp).then_inc(sink_exp, 1)

                def copies(g):
                    t = GROUPS[g][0]
                    w = P if t == 0 else 384
                    for j in range(4):
                        u = 4 * g + j
                        act.wait_ge(pt_psum, l * SU + u + 1)
                        if u >= 2:
                            act.wait_ge(pv_done, l * SU + u - 1)
                        act.activation(pT[:, u % 2, 0:w], ps[:, 4 + u % 2, 0:w], ACT.Copy).then_inc(pT_ready, 1)

                exps(0)
                for g in range(NG):
                    if g + 1 < NG:
                        exps(g + 1)
                    copies(g)

                for j in range(1, KT, 2):
                    act.wait_ge(ot_psum, l * KT + j + 1)
                    act.activation(oT[:, j, :], ps[:, j, 0:TOK], ACT.Copy).then_inc(ot_act, 1)

                with act.Fori(0, G_CHUNKS // SLOTS) as i:
                    for b in range(8):
                        if b % 2 == 0:
                            act.wait_ge(gate_psum, l * G_CHUNKS + i * SLOTS + b // 2 + 1)
                        else:
                            done("g", i * SLOTS + b // 2 + 1)
                        act.activation(arena[:, bass.ds(i * (8 * TOK) + (9216 + b * TOK), TOK)], ps[:, b, 0:TOK],
                                       ACT.Tanh, scale=0.5).then_inc(gate_ready, 1)
                gate_rows(0, 0.5)

                squares((x_ready, l * XR + 1 + 1))
                norm(1)

                act.wait_ge(router_sub, l * 2 + 1)
                act.activation(r4[:, 2], r4[:, 2], ACT.Exp).then_inc(router_exp, 1)
                act.wait_ge(router_sub, l * 2 + 2)
                act.activation(r1[:, 4, :], r1[:, 4, :], ACT.Exp).then_inc(router_exp, 1)
                for e in range(N_EXP):
                    act.wait_ge(cw_psum, l * N_EXP + e + 1)
                    act.activation(cw[:, e, :], ps[:, 2 + e % 6, 0:TOK], ACT.Copy, scale=0.5).then_inc(cw_ready, 1)

                with act.Fori(0, N_EXP // 2) as i:
                    for ab in range(2):
                        act.wait_ge(e_read, l * N_EXP + i * 2 + ab + 1)
                        done("exp", i * SLOTS + 2 * ab + 1)
                        act.activation(tg[:, ab], ps[:, 4 * ab:4 * ab + 2, 0:TOK], ACT.Tanh, scale=0.5).then_inc(e_tanh, 1)
                gate_rows(1, 1.0)

            squares((x_ready, DEPTH * XR + 1))

        @block.gpsimd
        def _(pool):
            def root(n, ready, src, mid, dst, width, mean, signal):
                wait_apart(pool, *ready)
                pool.tensor_scalar(mid[:, :], src[:, :], 1.0 / mean, EPS, ALU.mult, ALU.add).then_inc(pool_step, 1)
                pool.wait_ge(pool_step, n)
                pool.tensor_tensor(dst[:, :], mid[:, :], mhalf[:, 0:width], ALU.pow).then_inc(signal, 1)

            pool.wait_ge(init_dve, 14)
            pool.sem_inc(gate_ready, 8)
            pool.sem_inc(e_read, 2)
            with pool.Fori(0, DEPTH) as l:
                def ada_bias(first, count, ready):
                    pool.wait_ge(*ready)
                    pool.dma_start(mrow[0:2, 0:count], a["ada_b"][bass.ds(l, 1), first:first + count].to_broadcast([2, count])
                                   ).then_inc(adab_loaded, 16)

                wait_apart(pool, x_ready, l * XR + 1)
                ada_bias(0, 2 * D, (x_ready, l * XR + 1))
                for c0 in (0, P + 384):
                    pool.memset(bias[:, :, c0:c0 + P], 0.0).then_inc(bias_ready, 1)
                root(l * POOL_L + 1, (ssq_ready, l * SSQ + 3), ssq, msq, rstd, 3, D, rstd_ready)
                ada_bias(2 * D, D, (mod_psum, l * MODP + 1))
                pool.wait_ge(zt_dve, l * ZD + ZD + 1)
                pool.wait_ge(zt_act, l * ZD + ZD + 1)
                for i, (t, d) in enumerate(((0, 0), (0, 1), (1, 0), (2, 1))):
                    kdl = kdec[:, :, :, :].rearrange("p l r h -> p (l r h)")[:, bass.ds(l * 8 + 4 * d, 4)]
                    pool.tensor_tensor(kd[:, i, :].rearrange("p (h d) -> p h d", d=HD),
                                       zt[:, t, KR:KR + 256].rearrange("p (h d) -> p h d", d=HD),
                                       kdl.unsqueeze(2).to_broadcast([P, 4, HD]), ALU.mult).then_inc(kd_ready, 1)
                for name, c0, n in (("new_na_k", KA, 8), ("new_na_v", VA, 8), ("new_swa_k", KS, 2), ("new_swa_v", VS, 2)):
                    pool.dma_start(out[name][0][bass.ds(l, 1)].rearrange("a h s d -> s (a h) d"),
                                   zt[:, 0, c0:c0 + n * HD].rearrange("p (h d) -> p h d", d=HD)).then_inc(kv_stored, 16)
                pool.wait_ge(state_ready, l * 10 + 2)
                pool.dma_start(out["new_state"][0][bass.ds(l, 1)].rearrange("a r h d e -> (a r h d) e").rearrange("(n p) e -> p n e", p=P),
                               state_out[:, :, :, :].rearrange("p r b e -> p (r b) e")).then_inc(kv_stored, 16)
                root(l * POOL_L + 2, (ret_ssq, l * 1 + 1), ssq12, msq12, rstd12, 12, HD, rsq_ready)
                ada_bias(3 * D, 2 * D, (gb_psum, l * GB + 4))
                root(l * POOL_L + 3, (ssq_ready, l * SSQ + 6), ssq, msq, rstd, 3, D, rstd_ready)
                ada_bias(5 * D, D, (mod_psum, l * MODP + 2))

            pool.dma_start(fing, a["final_norm_g"].unsqueeze(0).to_broadcast([P, D])).then_inc(stored, 16)
            root(DEPTH * POOL_L + 1, (ssq_ready, DEPTH * SSQ + 3), ssq, msq, rstd, 3, D, rstd_ready)
            pool.wait_ge(fin_ready, 1)
            pool.dma_start(out["y_prompt"][0], xn[:, 0, :]).then_inc(stored, 16)
            pool.wait_ge(fin_ready, 3)
            pool.dma_start(out["y_sample"][0].rearrange("(t p) d -> p t d", p=P), xn[:, 1:3, :]).then_inc(stored, 16)
            pool.wait_ge(kv_stored, DEPTH * KV_L)
            pool.wait_ge(stored, 48)


_OUTS = {"y_prompt": (1, 128, 1024), "y_sample": (1, 256, 1024), "new_na_k": (1, 2, 8, 128, 64),
         "new_na_v": (1, 2, 8, 128, 64), "new_swa_k": (1, 2, 2, 128, 64), "new_swa_v": (1, 2, 2, 128, 64),
         "new_state": (1, 2, 2, 4, 64, 64)}


def kernel(**inputs):
    import numpy as _np
    import concourse.bacc as _bacc
    from concourse.bass_utils import run_bass_kernel_spmd as _run

    nc = _bacc.Bacc("TRN2", target_bir_lowering=False, num_devices=1)
    arrays, args, outs = {}, {}, {}
    laid = {k: _np.ascontiguousarray(v) for k, v in inputs.items()}
    laid["na_rpb_flat"] = laid.pop("na_rpb").reshape(1, -1)
    laid["consts"] = constants()
    for name, v in laid.items():
        arrays[f"in_{name}"] = v
        args[name] = nc.dram_tensor(f"in_{name}", v.shape, mybir.dt.from_np(v.dtype), kind="ExternalInput").ap()
    for name, shape in _OUTS.items():
        outs[name] = nc.dram_tensor(f"out_{name}", shape, F32, kind="ExternalOutput").ap()
    build(nc, args, outs)
    r = _run(nc, [arrays], core_ids=[0])
    return tuple(r.results[0][f"out_{name}"] for name in _OUTS)
```

```python
from contextlib import ExitStack

import numpy as np

import concourse.bass as bass
from concourse import mybir

F32 = mybir.dt.float32
U32 = mybir.dt.uint32
I32 = mybir.dt.int32
ALU = mybir.AluOpType
ACT = mybir.ActivationFunctionType
AX_X = mybir.AxisListType.X

P = 128
D = 1024
DEPTH = 2
TILES = 3
TOK = TILES * P
KT = D // P
GRID_W = 64
HD = 64
HEADS_NA, HEADS_SWA, KV_SWA, HEADS_RET = 8, 4, 2, 4
WIN_COLS, WIN_ROWS = 16, 8
RPB_W = 2 * WIN_COLS - 1
RPB = (2 * WIN_ROWS - 1) * RPB_W
GRID_ROWS = 256 // GRID_W
N_EXP, N_GRP, D_EXP = 16, 4, 256
IN_COLS = 6144
EPS = 1e-6
NEG = -1e30
EXTRA = 5
BLOCKS = N_EXP + EXTRA

QA, KA, VA, QS, KS, VS, QR, KR, VR, GR = 0, 512, 1024, 1536, 1792, 1920, 2048, 2304, 2560, 2816
Z_COLS = 3072

CH = 256
SLOTS = 4
Z_CHUNKS = Z_COLS // CH
G_CHUNKS = (IN_COLS - Z_COLS) // CH
LAYER_CHUNKS = 6 * 4 + Z_CHUNKS + G_CHUNKS + 4 + 4 + 2 * N_EXP + N_EXP
SLOT_LOADS = 16 * LAYER_CHUNKS // SLOTS

BIAS_W = P + 6 * GRID_W + P

C_IDENT, C_COS, C_SIN = 0, 128, 192
C_COLMASK = 256
C_SWAMASK = 320
C_POS = 1088
C_IOTA = 1092
C_TURN = 1108
C_BEFORE = 1236
C_ONE = 1364
C_BLOCK = 1365
C_IOTA5 = 1381
C_END = 1461
C_MASKF, C_MASKB, C_DIFFF, C_DIFFB = 1461, 1589, 1717, 1845
C_ALL = 1973


def constants():
    c = np.zeros((P, C_ALL), np.float32)
    p = np.arange(P)
    c[:, C_IDENT:C_IDENT + P] = np.eye(P)
    inv = (np.float32(10000.0) ** (-np.arange(16, dtype=np.float32) / np.float32(16))).astype(np.float32)
    for t in range(2):
        tok = p + P * t
        ang = np.concatenate([(tok // GRID_W).astype(np.float32)[:, None] * inv,
                              (tok % GRID_W).astype(np.float32)[:, None] * inv], axis=1)
        c[:, C_COS + 32 * t:C_COS + 32 * t + 32] = np.cos(ang)
        c[:, C_SIN + 32 * t:C_SIN + 32 * t + 32] = np.sin(ang)
    col = p % GRID_W
    start = np.clip(col - WIN_COLS // 2, 0, GRID_W - WIN_COLS)
    k = np.arange(GRID_W)
    inside = (k[None] >= start[:, None]) & (k[None] < start[:, None] + WIN_COLS)
    c[:, C_COLMASK:C_COLMASK + GRID_W] = np.where(inside, 0, NEG)
    keys = np.arange(256)
    far0 = np.abs(p[:, None] - keys[None]) > 128
    far1 = np.abs(p[:, None] + P - keys[None]) > 128
    c[:, C_SWAMASK:C_SWAMASK + 256] = np.where(far0, NEG, 0)
    c[:, C_SWAMASK + 384 + 128:C_SWAMASK + 768] = np.where(far1, NEG, 0)
    q = np.arange(P)[None]
    kk = p[:, None]
    c[:, C_MASKF:C_MASKF + P] = q >= kk
    c[:, C_MASKB:C_MASKB + P] = kk >= q
    c[:, C_DIFFF:C_DIFFF + P] = np.maximum(q - kk, 0)
    c[:, C_DIFFB:C_DIFFB + P] = np.maximum(kk - q, 0)
    c[:, C_POS:C_POS + 4] = np.stack([p + 1, P - p, P - 1 - p, p], 1)
    c[:, C_IOTA:C_IOTA + 16] = np.arange(16)[None]
    c[:, C_BEFORE:C_BEFORE + P] = kk < q
    c[:, C_ONE] = 1
    c[:, C_BLOCK:C_BLOCK + 16] = P * np.arange(16)[None]
    c[:, C_IOTA5:C_IOTA5 + 80] = np.repeat(np.arange(5), 16)[None]
    c[p, C_TURN + (p // GRID_W) * GRID_W + (GRID_W - 1 - p % GRID_W)] = 1
    return c


def build(nc, a, out):
    ctx = ExitStack()
    with ctx:
        def sb(name, shape):
            return ctx.enter_context(nc.sbuf_tensor(name, shape, F32))

        def sem(name):
            return ctx.enter_context(nc.semaphore(name))

        x = sb("x", [P, TILES, D])
        hT = sb("hT", [P, KT, TOK])
        arena = sb("arena", [P, 72 * 256])
        zt = arena[:, 0:TILES * Z_COLS].rearrange("p (t c) -> p t c", t=TILES)
        gates = arena[:, 9216:18432].rearrange("p (f n) -> p f n", n=TOK)
        qkT = arena[:, 9216:9216 + 15 * TOK].rearrange("p (b n) -> p b n", n=TOK)
        rot = arena[:, 15000:15000 + TILES * 384].rearrange("p (t c) -> p t c", t=TILES)
        ret_o = arena[:, 16152:16152 + 768]
        ret_u = arena[:, 16920:16920 + 768]
        ret_w = arena[:, 17688:17688 + 512]
        bias_turned = arena[:, 12288:12288 + HEADS_NA * 384].rearrange("p (h c) -> p h c", c=384)
        zT = arena[:, 0:KT * TOK].rearrange("p (b n) -> p b n", n=TOK)
        xg = arena[:, 0:4096].rearrange("p (b c) -> p b c", b=4)
        yb = arena[:, 4096:8192].rearrange("p (b c) -> p b c", b=4)
        hgT = arena[:, 8192:10240].rearrange("p (b k n) -> p b k n", b=2, k=KT)
        act_a = arena[:, 10240:10752].rearrange("p (b c) -> p b c", b=2)
        act_t = arena[:, 10752:11264].rearrange("p (b c) -> p b c", b=2)
        aTs = arena[:, 11264:11776].rearrange("p (b j n) -> p b j n", b=2, j=2)
        hotsum = arena[:, 11776:11824].rearrange("p (t e) -> p t e", e=16)
        e16 = arena[:, 11824:11888].rearrange("p (n e) -> p n e", e=16)
        owner = arena[:, 11888:11968].rearrange("p (n e) -> p n e", e=16)
        ownerf = arena[:, 11968:11973]
        r16 = arena[:, 11976:12168].rearrange("p (n t e) -> p n t e", n=4, t=TILES)
        lo = arena[:, 12168:12228].rearrange("p (t c) -> p t c", t=TILES)
        yg = arena[:, 12288:18432].rearrange("p (k t c) -> p k t c", k=2, t=TILES)
        tgr = arena[:, 15000:15768].rearrange("p (t c) -> p t c", t=TILES)
        ring = sb("ring", [P, SLOTS, KT, CH])
        biasT = sb("biasT", [P, HEADS_NA * BIAS_W])
        bias = biasT[:, :].rearrange("p (h c) -> p h c", c=BIAS_W)
        oT = biasT[:, 0:KT * TOK].rearrange("p (b n) -> p b n", n=TOK)
        gb = sb("gb", [P, 2, D])
        mrow = sb("mrow", [2, 2 * D])
        work = sb("work", [P, 15 * 256])
        sbuf_s = work[:, 0:3072].rearrange("p (g h c) -> p g h c", g=2, h=4)
        pT = work[:, 3072:3840].rearrange("p (b c) -> p b c", b=2)
        xn = work[:, 0:3072].rearrange("p (t c) -> p t c", t=TILES)
        rprod = work[:, 0:1536].rearrange("p (n t h i) -> p n t h i", n=4, t=2, h=6)
        am = work[:, 0:1536].rearrange("p (t c) -> p t c", t=TILES)
        br_u = work[:, 0:384]
        br_w = work[:, 384:768]
        cst = sb("cst", [P, C_END])
        once = work[:, 2048:2560]
        kcT = sb("kcT", [P, 5, P])
        cache_k = sb("cache_k", [P, 10, HD])
        cache_v = sb("cache_v", [P, 10, HD])
        cond = sb("cond", [P, KT, 2])
        condr = sb("condr", [P, 2, KT])
        condt = sb("condt", [P, 2, KT])
        gain = sb("gain", [P, 2, KT])
        shift = sb("shift", [P, KT, 2])
        scale = sb("scale", [P, KT, 2])
        ssq = sb("ssq", [P, TILES])
        msq = sb("msq", [P, TILES])
        rstd = sb("rstd", [P, TILES])
        ssq12 = sb("ssq12", [P, 12])
        msq12 = sb("msq12", [P, 12])
        rstd12 = sb("rstd12", [P, 12])
        mhalf = sb("mhalf", [P, 12])
        zero1 = sb("zero1", [P, 1])
        rw = sb("rw", [P, KT, 20])
        rb = sb("rb", [P, 20])
        ret_g = sb("ret_g", [P, 256])
        sink = sb("sink", [P, 4])
        state0 = sb("state0", [P, 2, 2, HD])
        state1 = sb("state1", [P, 2, 2, HD])
        state_out = sb("state_out", [P, 2, 2, HD])
        kd = sb("kd", [P, 4, 256])
        lg = sb("lg", [P, 16])
        lgt = sb("lgt", [P, 4, 16])
        qdec = sb("qdec", [P, DEPTH, 2, 4])
        kdec = sb("kdec", [P, DEPTH, 2, 4])
        cdec = sb("cdec", [P, DEPTH, 2, 2])
        cdl = sb("cdl", [P, DEPTH, 2, 2])
        dec = sb("dec", [P, DEPTH, 4, P])
        mx = sb("mx", [P, 2, 4])
        nmx = sb("nmx", [P, 2, 4])
        den = sb("den", [P, 2, 4])
        rden = sb("rden", [P, 2, 4])
        sk = sb("sk", [P, 2, 4])
        r4 = sb("r4", [P, 3, TILES, 4])
        r1 = sb("r1", [P, 8, TILES])
        slot_f = sb("slot_f", [P, 2, TILES])
        slot_i = ctx.enter_context(nc.sbuf_tensor("slot_i", [P, 2, TILES], U32))
        extra_i = ctx.enter_context(nc.sbuf_tensor("extra_i", [1, 8], I32))
        fing = biasT[:, 0:D]
        ps = ctx.enter_context(nc.psum_tensor("ps", [P, 8, 512], F32))

        ident = cst[:, C_IDENT:C_IDENT + P]

        init_loaded = sem("init_loaded")
        INIT_LOADS = 7
        SMALL_L = 16 * 27
        init_dve = sem("init_dve")
        act_init = sem("act_init")
        slot_loaded = [sem(f"slot_loaded{i}") for i in range(SLOTS)]
        chunk_done = sem("chunk_done")
        gains_loaded = sem("gains_loaded")
        small_loaded = sem("small_loaded")
        adab_loaded = sem("adab_loaded")
        ADA = 12
        ada_row = sem("ada_row")
        mod_psum, MODP = sem("mod_psum"), 2
        mod_ready, MODR = sem("mod_ready"), 4
        gb_psum, GB = sem("gb_psum"), 8
        gb_ready = sem("gb_ready")
        x_ready, XR = sem("x_ready"), 2
        ssq_ready, SSQ = sem("ssq_ready"), 6
        pool_step = sem("pool_step")
        POOL_L = 3
        rstd_ready, RS = sem("rstd_ready"), 2
        xn_ready, XN = sem("xn_ready"), 6
        xT_psum, XT = sem("xT_psum"), 16
        hT_dve, HT = sem("hT_dve"), 16
        hT_act = sem("hT_act")
        zt_dve, ZD = sem("zt_dve"), Z_CHUNKS // 2
        zt_act = sem("zt_act")
        kv_stored = sem("kv_stored")
        KV_L = 5 * 16
        rot_act = sem("rot_act")
        rot_dve = sem("rot_dve")
        RD = 6
        t_psum, TP = sem("t_psum"), 17
        t_dve, TD = sem("t_dve"), 9
        t_act, TA = sem("t_act"), 8
        bias_psum = sem("bias_psum")
        bias_ready = sem("bias_ready")
        BIAS_L = 2 + HEADS_NA
        s_psum, SU = sem("s_psum"), 36
        s_ready = sem("s_ready")
        nmax_ready, NG = sem("nmax_ready"), 9
        exp_ready = sem("exp_ready")
        sink_exp = sem("sink_exp")
        pt_psum = sem("pt_psum")
        pT_ready = sem("pT_ready")
        pv_done = sem("pv_done")
        o_ready = sem("o_ready")
        kd_ready = sem("kd_ready")
        kv_psum = sem("kv_psum")
        state_ready = sem("state_ready")
        a_psum = sem("a_psum")
        am_ready = sem("am_ready")
        ro_psum = sem("ro_psum")
        tgr_ready = sem("tgr_ready")
        ret_ssq = sem("ret_ssq")
        rsq_ready = sem("rsq_ready")
        router_sub = sem("router_sub")
        router_exp = sem("router_exp")
        ro_ready = sem("ro_ready")
        ot_psum = sem("ot_psum")
        ot_dve = sem("ot_dve")
        ot_act = sem("ot_act")
        gate_psum = sem("gate_psum")
        GT = 24
        gate_ready = sem("gate_ready")
        br_psum = sem("br_psum")
        br_read = sem("br_read")
        zT_ready = sem("zT_ready")
        out_read = sem("out_read")
        lo_psum = sem("lo_psum")
        h2_psum = sem("h2_psum")
        h2_ready = sem("h2_ready")
        hot_ready = sem("hot_ready")
        rank_psum = sem("rank_psum")
        slots_ready = sem("slots_ready")
        routed = sem("routed")
        filled = sem("filled")
        scattered = sem("scattered")
        xg_loaded = [sem(f"xg_loaded{i}") for i in range(4)]
        xgT_psum = sem("xgT_psum")
        hg_act = sem("hg_act")
        hg_dve = sem("hg_dve")
        th_ready = sem("th_ready")
        e_mul = sem("e_mul")
        a_made = sem("a_made")
        aT_psum = sem("aT_psum")
        aTs_ready = sem("aTs_ready")
        y_psum = sem("y_psum")
        y_act = sem("y_act")
        y_dve = sem("y_dve")
        y_stored = sem("y_stored")
        y_free = sem("y_free")
        yg_loaded = [sem(f"yg_loaded{i}") for i in range(TILES)]
        y1_scaled = sem("y1_scaled")
        ov_w, ov_x, ov_xT, ov_hg, ov_g = sem("ov_w"), sem("ov_x"), sem("ov_xT"), sem("ov_hg"), sem("ov_g")
        ov_u, ov_t, ov_m, ov_a, ov_aT = sem("ov_u"), sem("ov_t"), sem("ov_m"), sem("ov_a"), sem("ov_aT")
        ov_as, ov_y, ov_ye, ov_ys = sem("ov_as"), sem("ov_y"), sem("ov_ye"), sem("ov_ys")
        dve_chain = sem("dve_chain")
        DVE_CHAIN = 132
        fin_ready = sem("fin_ready")
        stored = sem("stored")

        w_in = a["w_in"]
        w_br = [a["w_br_na"], a["w_br_swa"], a["w_br_ret"]]

        GROUPS = [(t, kind) for t in range(TILES) for kind in range(3)]
        SCALED = (0, 1, 2, 3, 8, 9, 13, 14)
        POSITION = [0, 2, 1, 3]

        SEG = {}
        n = 0
        for name, count in (("ada0", 8), ("z", Z_CHUNKS), ("g", G_CHUNKS), ("ada2", 4), ("br", 4), ("out", 4),
                            ("ada3", 8), ("ada5", 4), ("moe", 3 * N_EXP)):
            SEG[name] = n
            n += count
        BR_EXTRA = 32
        SLOT_LAYER = SLOT_LOADS + BR_EXTRA

        def moe_seq(u):
            return 0 if u < 0 else 2 + 3 * u

        def moe_down_seq(u):
            return 3 * (u + 1) + 4

        def blocks(l, i, u):
            return l * N_EXP + i * 4 + (u + 1)

        passed = sem("passed")

        def wait_apart(eng, semaphore, value):
            eng.wait_ge(semaphore, value)
            eng.sem_inc(passed, 1)

        INTER = {1: (3, 0), 2: (4, 1)}

        block = ctx.enter_context(nc.Block())

        @block.sync
        def _(sp):
            sp.sem_inc(chunk_done, SLOTS)
            for one in (x_ready, ada_row, zt_dve, zt_act, gb_psum, a_made, y_act, y_dve):
                sp.sem_inc(one, 1)
            sp.dma_start(x[:, 0, :], a["x_prompt"][0]).then_inc(init_loaded, 16)
            sp.dma_start(x[:, 1:3, :], a["x_sample"][0].rearrange("(t p) d -> p t d", p=P)).then_inc(init_loaded, 16)
            sp.dma_start(cst[:, :], a["consts"][:, 0:C_END]).then_inc(init_loaded, 16)
            sp.dma_start(condr[:, 0, :], a["c_ctx"].rearrange("(p k) -> p k", k=KT)).then_inc(init_loaded, 16)
            sp.dma_start(condr[:, 1, :], a["c"][0].rearrange("(p k) -> p k", k=KT)).then_inc(init_loaded, 16)
            sp.dma_start(lgt[:, 0, :], a["ret_decay"].rearrange("l r h -> (l r h)").unsqueeze(0).to_broadcast([P, 16])).then_inc(init_loaded, 16)

            sp.dma_start(once, a["consts"][:, C_END:C_ALL]).then_inc(init_loaded, 16)

            def put(slot, src, l, seq):
                sp.wait_ge(chunk_done, l * LAYER_CHUNKS + (seq + 1))
                sp.dma_start(ring[:, slot] if src.shape[1] == KT else
                             ring[:, slot].rearrange("p k c -> p (k c)").rearrange("p (j n) -> p j n", n=D),
                             src).then_inc(slot_loaded[slot], 16)

            with sp.Fori(0, DEPTH) as l:
                seq = [0]

                def columns(w, first, count, rows="(p k) c -> p k c"):
                    base = seq[0]
                    with sp.Fori(0, count // SLOTS) as i:
                        for s in range(SLOTS):
                            col = sp.snap(i * (SLOTS * CH) + (first + s * CH))
                            kw = {"k": KT} if rows.startswith("(p k)") else {"p": P}
                            src = w[bass.ds(l, 1)].rearrange("a r c -> (a r) c").rearrange(rows, **kw)[:, :, bass.ds(col, CH)]
                            put(s, src, l, i * SLOTS + (base + s))
                    seq[0] += count

                columns(a["ada_w"], 0, 8)
                columns(w_in, 0, Z_CHUNKS)
                columns(w_in, Z_COLS, G_CHUNKS)
                columns(a["ada_w"], 2 * D, 4)
                for s in range(4):
                    sp.wait_ge(chunk_done, l * LAYER_CHUNKS + (seq[0] + s + 1))
                    for w, k0, kn in ((0, 0, 4), (1, 4, 2), (2, 6, 2)):
                        sp.dma_start(ring[:, s, k0:k0 + kn, :],
                                     w_br[w][bass.ds(l, 1)].rearrange("a (k p) c -> p (a k) c", p=P)[:, :, s * CH:(s + 1) * CH]
                                     ).then_inc(slot_loaded[s], 16)
                seq[0] += 4
                columns(a["w_out"], 0, 4, "(k p) c -> p k c")
                columns(a["ada_w"], 3 * D, 8)
                columns(a["ada_w"], 5 * D, 4)

                def expert(name, e, slot, i, n):
                    w = a[name].rearrange("l e r c -> (l e) r c")[bass.ds(e, 1)]
                    w = w.rearrange("a (p j) c -> p (a j) c", j=2) if name == "w_down" else \
                        w.rearrange("a (p k) c -> p (a k) c", k=KT)
                    put(slot, w, l, i * 12 + (SEG["moe"] + n))

                e = sp.snap(l * N_EXP)
                expert("w_gate", e, 0, 0, 0)
                expert("w_up", e, 1, 0, 1)

                def step(i, u):
                    n = moe_seq(u)
                    e = sp.snap(l * N_EXP + i * 4 + (u + 1))
                    expert("w_gate", e, n % SLOTS, i, n)
                    expert("w_up", e, (n + 1) % SLOTS, i, n + 1)
                    before = sp.snap(l * N_EXP + i * 4 + u)
                    expert("w_down", before, (n + 2) % SLOTS, i, n + 2)

                with sp.Fori(0, 3) as i:
                    for u in range(4):
                        step(i, u)
                for u in range(3):
                    step(3, u)
                expert("w_down", sp.snap(l * N_EXP + (N_EXP - 1)), (3 * N_EXP - 1) % SLOTS, 3, 11)
                seq[0] += 3 * N_EXP

                wait_apart(sp, routed, l + 1)
                extra = sp.value_load(extra_i[0:1, 0:1], min_val=0, max_val=EXTRA)
                with sp.If(extra > 0):
                    wait_apart(sp, chunk_done, l * LAYER_CHUNKS + (LAYER_CHUNKS + SLOTS))
                    for n in range(EXTRA):
                        owner_of = sp.value_load(extra_i[0:1, n + 1:n + 2], min_val=0, max_val=N_EXP - 1)
                        e = sp.snap(l * N_EXP + owner_of)
                        if n:
                            wait_apart(sp, ov_y, l * EXTRA + n)
                        for slot, name in enumerate(("w_gate", "w_up", "w_down")):
                            w = a[name].rearrange("l e r c -> (l e) r c")[bass.ds(e, 1)]
                            if name == "w_down":
                                sp.dma_start(ring[:, slot].rearrange("p k c -> p (k c)").rearrange("p (j n) -> p j n", n=D),
                                             w.rearrange("a (p j) c -> p (a j) c", j=2)).then_inc(ov_w, 16)
                            else:
                                sp.dma_start(ring[:, slot], w.rearrange("a (p k) c -> p (a k) c", k=KT)).then_inc(ov_w, 16)
                    wait_apart(sp, ov_y, l * EXTRA + EXTRA)
                with sp.Else():
                    sp.sem_inc(ov_w, 16 * 3 * EXTRA)
                assert seq[0] == LAYER_CHUNKS

        @block.tensor
        def _(pe):
            def loaded(seg, l, i, s, more=0):
                first = 16 * (SEG[seg] // SLOTS + 1 + more) + (BR_EXTRA if SEG[seg] >= SEG["br"] else 0)
                pe.wait_ge(slot_loaded[s], l * SLOT_LAYER + i * 16 + first)

            def columns_of_mod(l, section, which):
                pe.wait_ge(ada_row, l * ADA + 2 * section + 4 + 1)
                for sec in range(2):
                    for k in range(KT):
                        mm = pe.matmul(ps[:, 7, (sec * KT + k) * 2:(sec * KT + k) * 2 + 2],
                                       mrow[0:2, sec * D + k:(sec + 1) * D:KT], cst[0:2, C_IDENT:C_IDENT + 2],
                                       start=True, stop=True)
                mm.then_inc(mod_psum, 1)

            def broadcast_gate(l, section):
                pe.wait_ge(ada_row, l * ADA + 2 * section + 2 + 1)
                for cnd in range(2):
                    for half in range(2):
                        pe.matmul(ps[:, 4 + 2 * cnd + half, :], cst[0:2, C_IDENT + cnd:C_IDENT + cnd + 1].to_broadcast([2, P]),
                                  mrow[0:2, half * 512:(half + 1) * 512], start=True, stop=True).then_inc(gb_psum, 1)

            def norm_transposes(l, section, which):
                pe.wait_ge(xn_ready, l * XN + 3 * which + 3)
                pe.wait_ge(ada_row, l * ADA + 2 * section + 4 + 1)
                for k in range(KT):
                    if k == KT - 1:
                        columns_of_mod(l, section, which)
                        pe.wait_ge(mod_ready, l * MODR + 2 * which + 2)
                    for t in range(TILES):
                        mm = pe.transpose(ps[:, k, t * P:(t + 1) * P], xn[:, t, k:D:KT], ident)
                    mm.then_inc(xT_psum, 1)
                pe.wait_ge(hT_dve, l * HT + 8 * which + 8)
                wait_apart(pe, hT_act, l * HT + 8 * which + 8)

            pe.wait_ge(init_loaded, 16 * INIT_LOADS)
            pe.wait_ge(init_dve, 3)
            with pe.Fori(0, DEPTH) as l:
                def ada_rows(seg, count, b0=0):
                    for i in range(count):
                        for s in range(SLOTS):
                            loaded(seg, l, i, s)
                            for k in range(KT):
                                mm = pe.matmul(ps[0:2, b0 + 2 * i + s // 2, (s % 2) * CH:(s % 2 + 1) * CH], cond[:, k, :],
                                               ring[:, s, k, :], start=(k == 0), stop=(k == KT - 1))
                            mm.then_inc(chunk_done, 1)

                ada_rows("ada0", 2)
                norm_transposes(l, 0, 0)
                with pe.Fori(0, Z_CHUNKS // SLOTS) as i:
                    for s in range(SLOTS):
                        loaded("z", l, i, s)
                        b = 3 * (s % 2)
                        if s % 2 == 0:
                            pe.wait_ge(zt_dve, l * ZD + i * 2 + s // 2 + 1)
                        else:
                            pe.wait_ge(zt_act, l * ZD + i * 2 + s // 2 + 1)
                        for t in range(TILES):
                            for k in range(KT):
                                mm = pe.matmul(ps[:, b + t, 0:CH], hT[:, k, t * P:(t + 1) * P], ring[:, s, k, :],
                                               start=(k == 0), stop=(k == KT - 1))
                        mm.then_inc(chunk_done, 1)

                pe.wait_ge(zt_dve, l * ZD + ZD + 1)
                pe.wait_ge(zt_act, l * ZD + ZD + 1)
                pe.wait_ge(small_loaded, l * SMALL_L + SMALL_L)
                for h in range(HEADS_NA):
                    pe.matmul(ps[:, h, 0:384], cst[:, C_TURN:C_TURN + P], bias_turned[:, h, :],
                              start=True, stop=True).then_inc(bias_psum, 1)

                pe.wait_ge(bias_ready, l * BIAS_L + BIAS_L)
                for u in range(TP):
                    if u == 10:
                        pe.wait_ge(rot_dve, l * RD + RD)
                        pe.wait_ge(rot_act, l * 2 + 2)
                    if u >= 8:
                        pe.wait_ge(*((t_dve, l * TD + ((u - 8) // 2 + 1)) if u % 2 == 0 else
                                     (t_act, l * TA + ((u - 8) // 2 + 1))))
                    b = u % 8
                    if u == 8:
                        for j in range(4):
                            mm = pe.transpose(ps[:, b, j * P:(j + 1) * P],
                                              cache_k[:, 2 * j:2 * j + 2, :].rearrange("p h d -> p (h d)"), ident)
                    elif u == 9:
                        mm = pe.transpose(ps[:, b, 0:P], cache_k[:, 8:10, :].rearrange("p h d -> p (h d)"), ident)
                    else:
                        v = u if u < 8 else u - 2
                        for t in range(TILES):
                            if v < 8:
                                src = zt[:, t, QA + v * P:QA + (v + 1) * P]
                            elif v < 11:
                                src = rot[:, t, (v - 8) * P:(v - 7) * P]
                            else:
                                src = zt[:, t, QR + (v - 11) * P:QR + (v - 10) * P]
                            mm = pe.transpose(ps[:, b, t * P:(t + 1) * P], src, ident)
                    mm.then_inc(t_psum, 1)

                pe.wait_ge(t_dve, l * TD + TD)
                pe.wait_ge(t_act, l * TA + TA)

                def heads_of(g):
                    t, kind = GROUPS[g]
                    for j in range(4):
                        if kind < 2:
                            h = 4 * kind + j
                            hp, qb, kb, cb = HD * (h % 2), h // 2, 4 + h // 2, h // 2
                            v0, vc = VA + h * HD, h
                        else:
                            pos = POSITION[j]
                            hp, qb, kb, cb = HD * (pos % 2), 8 + pos // 2, 10, 4
                            v0, vc = VS + (j // 2) * HD, 8 + j // 2
                        yield t, j, hp, qb, kb, cb, v0, vc

                def scores(g):
                    for t, j, hp, qb, kb, cb, v0, vc in heads_of(g):
                        u = 4 * g + j
                        if u >= 4:
                            pe.wait_ge(s_ready, l * SU + (u - 3))
                        q = qkT[hp:hp + HD, qb, t * P:(t + 1) * P]
                        if t == 0:
                            mm = pe.matmul(ps[:, u % 4, 0:P], q, qkT[hp:hp + HD, kb, 0:P], start=True, stop=True)
                        else:
                            loc, c0 = (0, 256) if t == 1 else (P, 0)
                            pe.matmul(ps[:, u % 4, loc:loc + 256], q, qkT[hp:hp + HD, kb, P:TOK], start=True, stop=True)
                            mm = pe.matmul(ps[:, u % 4, c0:c0 + P], q, kcT[hp:hp + HD, cb, :], start=True, stop=True)
                        mm.then_inc(s_psum, 1)

                def prob_transposes(g, j):
                    t = GROUPS[g][0]
                    u = 4 * g + j
                    pe.wait_ge(exp_ready, l * SU + (u + 1))
                    if u >= 2:
                        pe.wait_ge(pT_ready, l * SU + (u - 1))
                    for c in range(1 if t == 0 else 3):
                        mm = pe.transpose(ps[:, 4 + u % 2, c * P:(c + 1) * P], sbuf_s[:, g % 2, j, c * P:(c + 1) * P], ident)
                    mm.then_inc(pt_psum, 1)

                def values(g, jj):
                    for t, j, hp, qb, kb, cb, v0, vc in heads_of(g):
                        if j != jj:
                            continue
                        u = 4 * g + j
                        if j == 0 and g >= 2:
                            pe.wait_ge(o_ready, l * NG + (g - 1))
                        pe.wait_ge(pT_ready, l * SU + (u + 1))
                        new = [zt[:, tt, v0:v0 + HD] for tt in (1, 2)]
                        old = cache_v[:, vc, :]
                        vs = {0: [zt[:, 0, v0:v0 + HD]], 1: new + [old], 2: [old] + new}[t]
                        for c, v in enumerate(vs):
                            mm = pe.matmul(ps[:, 6 + g % 2, j * HD:(j + 1) * HD], pT[:, u % 2, c * P:(c + 1) * P], v,
                                           start=(c == 0), stop=(c == len(vs) - 1))
                        mm.then_inc(pv_done, 1)

                scores(0)
                for g in range(NG):
                    if g + 1 < NG:
                        scores(g + 1)
                    prob_transposes(g, 0)
                    for j in range(4):
                        if j < 3:
                            prob_transposes(g, j + 1)
                        values(g, j)

                pe.wait_ge(o_ready, l * NG + NG)
                pe.wait_ge(kd_ready, l * 4 + 4)
                for i, t in enumerate((0, 0, 1, 2)):
                    for hb in range(2):
                        mm = pe.matmul(ps[:, i // 2, ((i % 2) * 2 + hb) * P:((i % 2) * 2 + hb + 1) * P],
                                       kd[:, i, hb * P:(hb + 1) * P], zt[:, t, VR + hb * P:VR + (hb + 1) * P],
                                       start=True, stop=True)
                    if i % 2:
                        mm.then_inc(kv_psum, 1)
                for t in range(TILES):
                    for h in range(4):
                        hp = HD * (h % 2)
                        mm = pe.matmul(ps[:, (2, 5)[h % 2] + t, (h // 2) * P:(h // 2 + 1) * P], qkT[hp:hp + HD, 13 + h // 2, t * P:(t + 1) * P],
                                       qkT[hp:hp + HD, 11 + h // 2, t * P:(t + 1) * P], start=True, stop=True)
                    mm.then_inc(a_psum, 1)
                for t in range(TILES):
                    pe.wait_ge(am_ready, l * 3 + (t + 1))
                    if t == 1:
                        pe.wait_ge(state_ready, l * 10 + 10)
                    for h in range(4):
                        mm = pe.matmul(ps[:, 5 + t, h * HD:(h + 1) * HD], am[:, t, h * P:(h + 1) * P],
                                       zt[:, t, VR + h * HD:VR + (h + 1) * HD], start=True, stop=True)
                    if t:
                        for d in range(2):
                            st = state0 if (t == 1) == (d == 0) else state1
                            for h in range(4):
                                hp = HD * (h % 2)
                                o = (2 * d + h // 2) * HD
                                mm = pe.matmul(ps[:, INTER[t][h % 2], o:o + HD], qkT[hp:hp + HD, 11 + h // 2, t * P:(t + 1) * P],
                                               st[hp:hp + HD, d, h // 2, :], start=True, stop=True)
                    mm.then_inc(ro_psum, 1)

                pe.wait_ge(ro_ready, l * 1 + 1)
                for j in range(KT):
                    c0 = (QA + j * P) if j < 4 else (QS + (j - 4) * P) if j < 6 else QR + (j - 6) * P
                    for t in range(TILES):
                        mm = pe.transpose(ps[:, j, t * P:(t + 1) * P], zt[:, t, c0:c0 + P], ident)
                    mm.then_inc(ot_psum, 1)

                pe.wait_ge(ot_dve, l * 4 + 4)
                wait_apart(pe, ot_act, l * 4 + 4)
                with pe.Fori(0, G_CHUNKS // SLOTS) as i:
                    for s in range(SLOTS):
                        loaded("g", l, i, s)
                        for j in range(2):
                            b = 2 * s + j
                            pe.wait_ge(gate_ready, l * GT + i * 8 + (b + 1))
                            for k in range(KT):
                                mm = pe.matmul(ps[:, b, 0:TOK], ring[:, s, k, j * P:(j + 1) * P], hT[:, k, :],
                                               start=(k == 0), stop=(k == KT - 1))
                            mm.then_inc(gate_psum if j == 0 else chunk_done, 1)

                pe.wait_ge(gate_ready, l * GT + GT + 8)
                ada_rows("ada2", 1)
                broadcast_gate(l, 2)

                for j in range(KT):
                    s = j // 2
                    b = 3 * (j % 2)
                    if j % 2 == 0:
                        first = 16 * (SEG["br"] // SLOTS) + 48
                        pe.wait_ge(slot_loaded[s], l * SLOT_LAYER + first)
                    if j == 0:
                        pe.wait_ge(gb_ready, l * GB + 4)
                    if j >= 2:
                        pe.wait_ge(br_read, l * 8 + (j - 1))
                    for n_, (k0, kn) in enumerate(((0, 4), (4, 2), (6, 2))):
                        for k in range(k0, k0 + kn):
                            mm = pe.matmul(ps[:, b + n_, 0:TOK], ring[:, s, k, (j % 2) * P:(j % 2 + 1) * P], oT[:, k, :],
                                           start=(k == k0), stop=(k == k0 + kn - 1))
                    mm.then_inc(br_psum if j % 2 == 0 else chunk_done, 1)

                pe.wait_ge(br_read, l * 8 + 8)
                pe.wait_ge(zT_ready, l * 8 + 8)
                for s in range(4):
                    loaded("out", l, 0, s)
                    if s >= 2:
                        pe.wait_ge(out_read, l * 4 + (s - 1))
                    for t in range(TILES):
                        for k in range(KT):
                            mm = pe.matmul(ps[:, 3 * (s % 2) + t, 0:CH], zT[:, k, t * P:(t + 1) * P], ring[:, s, k, :],
                                           start=(k == 0), stop=(k == KT - 1))
                    mm.then_inc(chunk_done, 1)

                pe.wait_ge(out_read, l * 4 + 4)
                ada_rows("ada3", 2)
                norm_transposes(l, 3, 1)

                for t in range(TILES):
                    for k in range(KT):
                        mm = pe.matmul(ps[:, 0, t * 20:(t + 1) * 20], hT[:, k, t * P:(t + 1) * P], rw[:, k, :],
                                       start=(k == 0), stop=(k == KT - 1))
                mm.then_inc(lo_psum, 1)
                for t in range(TILES):
                    for k in range(KT):
                        mm = pe.transpose(ps[:, 2 + 2 * t + k // 4, (k % 4) * P:(k % 4 + 1) * P], hT[:, k, t * P:(t + 1) * P], ident)
                    mm.then_inc(h2_psum, 1)
                ones = cst[:, C_ONE:C_ONE + 1].to_broadcast([P, P])
                pe.wait_ge(hot_ready, l * 1 + 1)
                for t in range(TILES):
                    for before in range(t):
                        pe.matmul(ps[:, 0, 64 + 16 * t:80 + 16 * t], ones, hotsum[:, before, :], start=(before == 0), stop=False)
                    pe.matmul(ps[:, 0, 64 + 16 * t:80 + 16 * t], cst[:, C_BEFORE:C_BEFORE + P], hotsum[:, t, :],
                              start=(t == 0), stop=True)
                for t in range(TILES):
                    mm = pe.matmul(ps[:, 0, 112:128], ones, hotsum[:, t, :], start=(t == 0), stop=(t == TILES - 1))
                mm.then_inc(rank_psum, 1)

                pe.wait_ge(h2_ready, l * TILES + TILES)
                ada_rows("ada5", 1, 2)
                broadcast_gate(l, 5)

                def inputs_turned(i, u):
                    buf = (u + 1) % 4
                    pe.wait_ge(xg_loaded[buf], l * 64 + i * 16 + 16 * ((u + 1) // 4 + 1))
                    if u >= 0:
                        pe.wait_ge(hg_act, blocks(l, i, u))
                        pe.wait_ge(hg_dve, blocks(l, i, u))
                    for k in range(KT):
                        mm = pe.transpose(ps[:, k // 4, (k % 4) * P:(k % 4 + 1) * P], xg[:, buf, k * P:(k + 1) * P], ident)
                    mm.then_inc(xgT_psum, 1)

                def gate_up(i, u):
                    par = (u + 1) % 2
                    pe.wait_ge(hg_act, blocks(l, i, u) + 1)
                    pe.wait_ge(hg_dve, blocks(l, i, u) + 1)
                    if u >= 0:
                        pe.wait_ge(a_made, blocks(l, i, u))
                    for w in range(2):
                        n = moe_seq(u) + w
                        loaded("moe", l, i * 3, n % SLOTS, n // SLOTS)
                        for k in range(KT):
                            mm = pe.matmul(ps[:, 2 + par, w * CH:(w + 1) * CH], hgT[:, par, k, :], ring[:, n % SLOTS, k, :],
                                           start=(k == 0), stop=(k == KT - 1))
                        mm.then_inc(chunk_done, 1)

                def activations_turned(i, u):
                    pe.wait_ge(a_made, blocks(l, i, u) + 2)
                    for j in range(2):
                        mm = pe.transpose(ps[:, 4, j * P:(j + 1) * P], act_a[:, (u + 1) % 2, j:CH:2], ident)
                    mm.then_inc(aT_psum, 1)

                def down(i, u, last=False):
                    pe.wait_ge(aTs_ready, blocks(l, i, u) + 1)
                    pe.wait_ge(y_act, blocks(l, i, u) + 1)
                    pe.wait_ge(y_dve, blocks(l, i, u) + 1)
                    n = 11 if last else moe_down_seq(u)
                    loaded("moe", l, i * 3, n % SLOTS, n // SLOTS)
                    w = ring[:, n % SLOTS].rearrange("p k c -> p (k c)").rearrange("p (j n) -> p j n", n=D)
                    for half in range(2):
                        for j in range(2):
                            mm = pe.matmul(ps[:, 5 + half, :], aTs[:, (u + 1) % 2, j, :], w[:, j, half * 512:(half + 1) * 512],
                                           start=(j == 0), stop=(j == 1))
                        mm.then_inc(y_psum if half == 0 else chunk_done, 1)

                pe.wait_ge(ada_row, l * ADA + ADA + 1)
                pe.wait_ge(gb_ready, l * GB + GB)
                inputs_turned(0, -1)
                gate_up(0, -1)
                inputs_turned(0, 0)
                with pe.Fori(0, 3) as i:
                    for u in range(4):
                        gate_up(i, u)
                        activations_turned(i, u - 1)
                        inputs_turned(i, u + 1)
                        down(i, u - 1)
                for u in range(3):
                    gate_up(3, u)
                    activations_turned(3, u - 1)
                    if u < 2:
                        inputs_turned(3, u + 1)
                    down(3, u - 1)
                activations_turned(3, 2)
                down(3, 2, last=True)

                pe.wait_ge(y_act, l * N_EXP + N_EXP + 1)
                pe.wait_ge(y_dve, l * N_EXP + N_EXP + 1)
                wait_apart(pe, routed, l + 1)
                extra = pe.value_load(extra_i[0:1, 0:1], min_val=0, max_val=EXTRA)
                with pe.If(extra > 0):
                    with pe.Fori(0, EXTRA) as n:
                        pe.wait_ge(ov_x, l * (16 * EXTRA) + n * 16 + 16)
                        for k in range(KT):
                            mm = pe.transpose(ps[:, k // 4, (k % 4) * P:(k % 4 + 1) * P], xg[:, 0, k * P:(k + 1) * P], ident)
                        mm.then_inc(ov_xT, 1)
                        pe.wait_ge(ov_w, l * (48 * EXTRA) + n * 48 + 48)
                        pe.wait_ge(ov_hg, l * EXTRA + n + 1)
                        for w in range(2):
                            for k in range(KT):
                                mm = pe.matmul(ps[:, 2, w * CH:(w + 1) * CH], hgT[:, 0, k, :], ring[:, w, k, :],
                                               start=(k == 0), stop=(k == KT - 1))
                        mm.then_inc(ov_g, 1)
                        pe.wait_ge(ov_a, l * EXTRA + n + 1)
                        for j in range(2):
                            mm = pe.transpose(ps[:, 4, j * P:(j + 1) * P], act_a[:, 0, j:CH:2], ident)
                        mm.then_inc(ov_aT, 1)
                        pe.wait_ge(ov_as, l * EXTRA + n + 1)
                        w = ring[:, 2].rearrange("p k c -> p (k c)").rearrange("p (j n) -> p j n", n=D)
                        for half in range(2):
                            for j in range(2):
                                mm = pe.matmul(ps[:, 5 + half, :], aTs[:, 0, j, :], w[:, j, half * 512:(half + 1) * 512],
                                               start=(j == 0), stop=(j == 1))
                        mm.then_inc(ov_y, 1)
                        pe.wait_ge(ov_ye, l * EXTRA + n + 1)
                with pe.Else():
                    for one in (ov_xT, ov_g, ov_aT, ov_y):
                        pe.sem_inc(one, EXTRA)

        @block.vector
        def _(dve):
            count = [0]

            def link(ins):
                count[0] += 1
                ins.then_inc(dve_chain, 1)

            def linked(l):
                dve.wait_ge(dve_chain, l * DVE_CHAIN + count[0])

            def bcast(ap, shape, axis):
                return ap.unsqueeze(axis).to_broadcast(shape)

            dve.wait_ge(init_loaded, 16 * INIT_LOADS)
            dve.memset(mhalf[:, :], -0.5)
            dve.memset(zero1[:, :], 0.0)
            dve.scalar_tensor_tensor(out=lgt[:, 1, :], in0=lgt[:, 0, :], scalar=-1.0, in1=lgt[:, 0, :],
                                     op0=ALU.mult, op1=ALU.max).then_inc(init_dve, 1)
            dve.wait_ge(act_init, 1)
            dve.scalar_tensor_tensor(out=cond[:, :, :].rearrange("p k c -> p c k"), in0=condt[:, :, :], scalar=1.0, in1=condr[:, :, :],
                                     op0=ALU.add, op1=ALU.mult).then_inc(init_dve, 1)
            dve.wait_ge(init_dve, 2)
            dve.tensor_scalar(cond[:, :, :], cond[:, :, :], 0.5, None, ALU.mult).then_inc(init_dve, 1)
            dve.wait_ge(act_init, 3)
            dve.scalar_tensor_tensor(out=lg[:, :], in0=lgt[:, 0, :], scalar=0.0, in1=lgt[:, 3, :],
                                     op0=ALU.min, op1=ALU.subtract).then_inc(init_dve, 1)
            dve.wait_ge(init_dve, 4)
            lgv = lg[:, :].rearrange("p (l r h) -> p l r h", l=DEPTH, r=2)
            for d in range(2):
                dve.tensor_scalar(qdec[:, :, d, :], lgv[:, :, d, :], cst[:, C_POS + d:C_POS + d + 1], None,
                                  ALU.mult).then_inc(init_dve, 1)
                dve.tensor_scalar(kdec[:, :, d, :], lgv[:, :, d, :], cst[:, C_POS + 2 + d:C_POS + 3 + d], None,
                                  ALU.mult).then_inc(init_dve, 1)
                rows = slice(d * HD, (d + 1) * HD)
                dve.tensor_scalar(cdl[rows, :, :, :], lgv[rows, :, :, d:4:2], float(P), None,
                                  ALU.mult).then_inc(init_dve, 1)
            dve.wait_ge(act_init, 22)
            dve.tensor_scalar(kdec[:, :, :, :], kdec[:, :, :, :], HD ** -0.5, None, ALU.mult).then_inc(init_dve, 1)
            decv = dec[:, :, :, :].rearrange("p l h q -> p (l h) q")
            back = work[:, 0:1024].rearrange("p (n q) -> p n q", q=P)
            dve.tensor_tensor(decv, decv, bcast(once[:, 0:128], [P, 8, P], 1), ALU.mult).then_inc(init_dve, 1)
            dve.tensor_tensor(back, back, bcast(once[:, 128:256], [P, 8, P], 1), ALU.mult).then_inc(init_dve, 1)
            dve.wait_ge(init_dve, 13)
            dve.tensor_tensor(decv, decv, back, ALU.add).then_inc(init_dve, 1)
            dve.wait_ge(init_dve, 14)

            with dve.Fori(0, DEPTH) as l:
                def done(seg, n):
                    dve.wait_ge(chunk_done, l * LAYER_CHUNKS + (SEG[seg] + SLOTS) + n)

                def ada_rows(seg, which, count, b0=0):
                    dve.wait_ge(adab_loaded, l * 64 + 16 * (which + 1))
                    for n in range(2 * count):
                        done(seg, 2 * (n + 1))
                        row = mrow[0:2, n * 512:(n + 1) * 512]
                        dve.tensor_tensor(row, row, ps[0:2, b0 + n, :], ALU.add).then_inc(ada_row, 1)

                def modulation_columns(which):
                    dve.wait_ge(mod_psum, l * MODP + which + 1)
                    dve.wait_ge(gains_loaded, l * 32 + 32)
                    v = ps[:, 7, 0:32].rearrange("p (s k c) -> p s k c", s=2, c=2)
                    dve.tensor_copy(shift[:, :, :], v[:, 0]).then_inc(mod_ready, 1)
                    dve.scalar_tensor_tensor(out=scale[:, :, :], in0=v[:, 1], scalar=1.0,
                                             in1=bcast(gain[:, which, :], [P, KT, 2], 2),
                                             op0=ALU.add, op1=ALU.mult).then_inc(mod_ready, 1)

                def norm(which):
                    dve.wait_ge(rstd_ready, l * RS + which + 1)
                    for t in range(TILES):
                        dve.tensor_scalar(xn[:, t, :], x[:, t, :], rstd[:, t:t + 1], None, ALU.mult).then_inc(xn_ready, 1)
                    ada_rows("ada3" if which else "ada0", 2 * which, 2)
                    modulation_columns(which)
                    dve.wait_ge(mod_ready, l * MODR + 2 * which + 2)
                    for k in range(0, KT, 2):
                        dve.wait_ge(xT_psum, l * XT + 8 * which + k + 1)
                        for c, (n0, n1) in enumerate(((0, P), (P, TOK))):
                            dve.tensor_scalar(hT[:, k, n0:n1], ps[:, k, n0:n1], scale[:, k, c:c + 1], shift[:, k, c:c + 1],
                                              ALU.mult, ALU.add).then_inc(hT_dve, 1)

                norm(0)

                with dve.Fori(0, Z_CHUNKS // SLOTS) as i:
                    for s in (0, 2):
                        done("z", i * SLOTS + (s + 1))
                        dve.tensor_copy(zt[:, :, bass.ds(i * (SLOTS * CH) + s * CH, CH)],
                                        ps[:, 0:3, 0:CH]).then_inc(zt_dve, 1)

                for h in range(HEADS_NA):
                    dve.wait_ge(bias_psum, l * HEADS_NA + h + 1)
                    dve.tensor_tensor(bias[:, h, P:P + 384].rearrange("p (s c) -> p s c", s=6),
                                      ps[:, h, 0:384].rearrange("p (s c) -> p s c", s=6),
                                      bcast(cst[:, C_COLMASK:C_COLMASK + GRID_W], [P, 6, GRID_W], 1),
                                      ALU.add).then_inc(bias_ready, 1)

                dve.wait_ge(zt_dve, l * ZD + ZD + 1)
                dve.wait_ge(zt_act, l * ZD + ZD + 1)
                for n, (odd, tab) in enumerate(((0, C_COS), (1, C_SIN), (0, C_SIN), (1, C_COS))):
                    src = zt[:, 1:3, QS + odd:QS + 384:2].rearrange("p t (h i) -> p t h i", i=32)
                    tabs = bcast(cst[:, tab:tab + 64].rearrange("p (t i) -> p t i", t=2), [P, 2, 6, 32], 2)
                    link(dve.tensor_tensor(rprod[:, n], src, tabs, ALU.mult))
                linked(l)
                for odd in range(2):
                    op = ALU.add if odd else ALU.subtract
                    for t in range(2):
                        o = rot[:, 1 + t, odd:256:2].rearrange("p (ha hb i) -> p hb ha i", ha=2, hb=2)
                        i0, i1 = (rprod[:, 2 * odd + m, t, 0:4, :].rearrange("p (hb ha) i -> p hb ha i", ha=2) for m in range(2))
                        dve.tensor_tensor(o, i0, i1, op).then_inc(rot_dve, 1)
                    dve.tensor_tensor(rot[:, 1:3, 256 + odd:384:2].rearrange("p t (h i) -> p t h i", i=32),
                                      rprod[:, 2 * odd, :, 4:6, :], rprod[:, 2 * odd + 1, :, 4:6, :], op).then_inc(rot_dve, 1)

                for u in range(0, TP, 2):
                    dve.wait_ge(t_psum, l * TP + u + 1)
                    if u == 8:
                        dve.tensor_copy(kcT[:, 0:4, :].rearrange("p b n -> p (b n)"), ps[:, 0, :]).then_inc(t_dve, 1)
                        continue
                    v = u if u < 8 else u - 2
                    dve.tensor_scalar(qkT[:, v, :], ps[:, u % 8, 0:TOK], HD ** -0.5 if v in SCALED else 1.0, None,
                                      ALU.mult).then_inc(t_dve, 1)

                dve.wait_ge(bias_ready, l * BIAS_L + BIAS_L)
                dve.wait_ge(small_loaded, l * SMALL_L + SMALL_L)

                def maxima(g):
                    t, kind = GROUPS[g]
                    if g >= 2:
                        dve.wait_ge(pt_psum, l * SU + 4 * (g - 1))
                    for j in range(4):
                        wait_apart(dve, s_psum, l * SU + 4 * g + j + 1)
                        w = P if t == 0 else 384
                        h = 4 * kind + j if kind < 2 else 0
                        if kind == 2 and t:
                            add = cst[:, C_SWAMASK + 384 * (t - 1):C_SWAMASK + 384 * t]
                        else:
                            add = bias[:, h, (0, 256, 0)[t]:(0, 256, 0)[t] + w]
                        dve.tensor_tensor_reduce(sbuf_s[:, g % 2, j, 0:w], ps[:, (4 * g + j) % 4, 0:w], add, 1.0, NEG,
                                                 ALU.add, ALU.max, mx[:, g % 2, j:j + 1]).then_inc(s_ready, 1)
                    dve.wait_ge(s_ready, l * SU + 4 * g + 4)
                    if kind == 2:
                        link(dve.tensor_tensor(mx[:, g % 2, :], mx[:, g % 2, :], sink[:, :], ALU.max))
                        linked(l)
                        link(dve.tensor_scalar(nmx[:, g % 2, :], mx[:, g % 2, :], -1.0, None, ALU.mult))
                        linked(l)
                        dve.tensor_tensor(sk[:, g % 2, :], sink[:, :], nmx[:, g % 2, :], ALU.add).then_inc(nmax_ready, 1)
                    else:
                        dve.tensor_scalar(nmx[:, g % 2, :], mx[:, g % 2, :], -1.0, None, ALU.mult).then_inc(nmax_ready, 1)

                def normalise(g):
                    t, kind = GROUPS[g]
                    dve.wait_ge(exp_ready, l * SU + 4 * g + 4)
                    if kind == 2:
                        dve.wait_ge(sink_exp, l * 3 + t + 1)
                        link(dve.tensor_tensor(den[:, g % 2, :], den[:, g % 2, :], sk[:, g % 2, :], ALU.add))
                        linked(l)
                    link(dve.reciprocal(rden[:, g % 2, :], den[:, g % 2, :]))
                    linked(l)
                    dve.wait_ge(pv_done, l * SU + 4 * g + 4)
                    o0 = QA + 256 * kind if kind < 2 else QS
                    dve.tensor_tensor(zt[:, t, o0:o0 + 256].rearrange("p (h d) -> p h d", d=HD),
                                      ps[:, 6 + g % 2, 0:256].rearrange("p (h d) -> p h d", d=HD),
                                      bcast(rden[:, g % 2, :], [P, 4, HD], 2), ALU.mult).then_inc(o_ready, 1)

                maxima(0)
                for g in range(NG):
                    if g + 1 < NG:
                        maxima(g + 1)
                    normalise(g)

                def diagonal(bank, i, par):
                    v = ps[par * HD:(par + 1) * HD, bank, :].rearrange("p (i b e) -> p i b e", i=2, b=2)
                    return v[:, i, :, par * HD:(par + 1) * HD]

                dve.wait_ge(kv_psum, l * 2 + 1)
                for par in range(2):
                    rows = slice(par * HD, (par + 1) * HD)
                    v = ps[rows, 0, :].rearrange("p (i b e) -> p i b e", i=2, b=2)
                    dve.tensor_copy(state_out[rows, :, :, :], v[:, :, :, par * HD:(par + 1) * HD]).then_inc(state_ready, 1)
                dve.wait_ge(kv_psum, l * 2 + 2)
                for d in range(2):
                    for par in range(2):
                        rows = slice(par * HD, (par + 1) * HD)
                        for hb in range(2):
                            dve.scalar_tensor_tensor(
                                out=state1[rows, d, hb, :], in0=state0[rows, d, hb, :],
                                scalar=cdec[rows, :, :, :].rearrange("p l r b -> p (l r b)")[:, bass.ds(l * 4 + (2 * d + hb), 1)],
                                in1=diagonal(1, d, par)[:, hb, :], op0=ALU.mult, op1=ALU.add).then_inc(state_ready, 1)
                def by_parity(ap, n):
                    return ap.rearrange("p (b r n) -> p r b n", b=2, n=n)

                decl = dec[:, :, :, :].rearrange("p l h q -> p (l h q)")[:, bass.ds(l * 512, 512)]
                for t in range(TILES):
                    dve.wait_ge(a_psum, l * 3 + t + 1)
                    for par in range(2):
                        ins = dve.tensor_tensor(by_parity(am[:, t, :], P)[:, par],
                                                ps[:, (2, 5)[par] + t, 0:256].rearrange("p (b q) -> p b q", b=2),
                                                by_parity(decl, P)[:, par], ALU.mult)
                        if par == 0:
                            link(ins)
                    ins.then_inc(am_ready, 1)

                def head_view(ap):
                    return ap.rearrange("p (h d) -> p h d", d=HD)

                for t in range(TILES):
                    dve.wait_ge(ro_psum, l * 3 + t + 1)
                    ot = ret_o[:, t * 256:(t + 1) * 256]
                    if t == 0:
                        link(dve.tensor_copy(ot, ps[:, 5, 0:256]))
                        continue
                    u, w = ret_u[:, t * 256:(t + 1) * 256], ret_w[:, (t - 1) * 256:t * 256]
                    for d, dst in ((0, u), (1, w)):
                        qd = by_parity(qdec[:, :, :, :].rearrange("p l r h -> p (l r h)")[:, bass.ds(l * 8 + 4 * d, 4)], 1)
                        for par in range(2):
                            link(dve.tensor_tensor(by_parity(dst, HD)[:, par],
                                                   ps[:, INTER[t][par], 128 * d:128 * d + 128].rearrange("p (b n) -> p b n", b=2),
                                                   qd[:, par].to_broadcast([P, 2, HD]), ALU.mult))
                    linked(l)
                    link(dve.tensor_tensor(u, u, w, ALU.add))
                    linked(l)
                    link(dve.tensor_tensor(ot, ps[:, 5 + t, 0:256], u, ALU.add))
                linked(l)
                link(dve.tensor_tensor(ret_u, ret_o, ret_o, ALU.mult))
                linked(l)
                dve.tensor_reduce(ssq12[:, :], head_view(ret_u), AX_X, ALU.add).then_inc(ret_ssq, 1)
                dve.wait_ge(rsq_ready, l * 1 + 1)
                link(dve.tensor_tensor(head_view(ret_o), head_view(ret_o), bcast(rstd12[:, :], [P, 12, HD], 2), ALU.mult))
                dve.wait_ge(tgr_ready, l * 1 + 1)
                dve.wait_ge(ret_ssq, l * 1 + 1)
                link(dve.scalar_tensor_tensor(out=ret_u.rearrange("p (t c) -> p t c", t=TILES), in0=tgr, scalar=1.0,
                                              in1=zt[:, :, GR:GR + 256], op0=ALU.add, op1=ALU.mult))
                linked(l)
                ro3 = ret_o.rearrange("p (t c) -> p t c", t=TILES)
                link(dve.tensor_tensor(ro3, ro3, bcast(ret_g[:, :], [P, TILES, 256], 1), ALU.mult))
                linked(l)
                dve.scalar_tensor_tensor(out=zt[:, :, QR:QR + 256], in0=ro3, scalar=0.5,
                                         in1=ret_u.rearrange("p (t c) -> p t c", t=TILES),
                                         op0=ALU.mult, op1=ALU.mult).then_inc(ro_ready, 1)

                for j in range(0, KT, 2):
                    dve.wait_ge(ot_psum, l * KT + j + 1)
                    dve.tensor_copy(oT[:, j, :], ps[:, j, 0:TOK]).then_inc(ot_dve, 1)

                ada_rows("ada2", 1, 1)

                dve.wait_ge(gate_ready, l * GT + GT + 8)
                dve.wait_ge(kv_stored, l * KV_L + KV_L)
                for j in range(KT):
                    if j % 2 == 0:
                        dve.wait_ge(br_psum, l * 4 + j // 2 + 1)
                    else:
                        done("br", j // 2 + 1)
                    b = 3 * (j % 2)
                    dsts = (zT[:, j, :], br_u, br_w)
                    for n in range(3):
                        ins = dve.scalar_tensor_tensor(out=dsts[n], in0=gates[:, n * KT + j, :], scalar=1.0,
                                                       in1=ps[:, b + n, 0:TOK], op0=ALU.add, op1=ALU.mult)
                        if n < 2:
                            link(ins)
                    ins.then_inc(br_read, 1)
                    linked(l)
                    link(dve.tensor_tensor(zT[:, j, :], zT[:, j, :], br_u, ALU.add))
                    linked(l)
                    dve.wait_ge(br_read, l * 8 + j + 1)
                    dve.tensor_tensor(zT[:, j, :], zT[:, j, :], br_w, ALU.add).then_inc(zT_ready, 1)
                    dve.wait_ge(zT_ready, l * 8 + j + 1)

                dve.wait_ge(gb_ready, l * GB + 4)
                for s in range(4):
                    done("out", s + 1)
                    b = 3 * (s % 2)
                    cols = slice(s * CH, (s + 1) * CH)
                    tmp = work[:, (s % 2) * 768:(s % 2 + 1) * 768].rearrange("p (t c) -> p t c", t=TILES)
                    link(dve.tensor_tensor(tmp[:, 0], ps[:, b, 0:CH], gb[:, 0, cols], ALU.mult))
                    dve.tensor_tensor(tmp[:, 1:3], ps[:, b + 1:b + 3, 0:CH], bcast(gb[:, 1, cols], [P, 2, CH], 1),
                                      ALU.mult).then_inc(out_read, 1)
                    linked(l)
                    dve.wait_ge(out_read, l * 4 + s + 1)
                    ins = dve.tensor_tensor(x[:, :, cols], x[:, :, cols], tmp, ALU.add)
                    if s < 3:
                        link(ins)
                    else:
                        ins.then_inc(x_ready, 1)

                linked(l)
                wait_apart(dve, x_ready, l * XR + 1 + 1)
                norm(1)

                iota16 = cst[:, C_IOTA:C_IOTA + 16]
                iota4 = cst[:, C_IOTA:C_IOTA + 4]

                def one_hot(values, n, iota, maximum, tmp, idx, out_hot):
                    link(dve.tensor_reduce(maximum, values, AX_X, ALU.max))
                    linked(l)
                    link(dve.tensor_tensor(tmp, values, bcast(maximum, [P, TILES, n], 2), ALU.is_equal))
                    linked(l)
                    link(dve.scalar_tensor_tensor(out=tmp, in0=tmp, scalar=-99.0, in1=bcast(iota, [P, TILES, n], 1),
                                                  op0=ALU.mult, op1=ALU.add))
                    linked(l)
                    link(dve.tensor_reduce(idx, tmp, AX_X, ALU.min))
                    linked(l)
                    link(dve.tensor_tensor(out_hot, tmp, bcast(idx, [P, TILES, n], 2), ALU.is_equal))
                    linked(l)

                dve.wait_ge(lo_psum, l * 1 + 1)
                link(dve.tensor_tensor(lo[:, :, :], ps[:, 0, 0:60].rearrange("p (t c) -> p t c", t=TILES),
                                       bcast(rb[:, :], [P, TILES, 20], 1), ALU.add))
                linked(l)
                g = lo[:, :, 0:4]
                one_hot(g, 4, iota4, r1[:, 0, :], r4[:, 0], r1[:, 1, :], r4[:, 1])
                dve.tensor_tensor(r4[:, 2], g, bcast(r1[:, 0, :], [P, TILES, 4], 2), ALU.subtract).then_inc(router_sub, 1)
                e4 = lo[:, :, 4:20].rearrange("p t (g e) -> p t g e", e=4)
                em = r16[:, 0]
                link(dve.tensor_tensor(em.rearrange("p t (g e) -> p t g e", e=4), e4,
                                       bcast(r4[:, 1], [P, TILES, 4, 4], 3), ALU.mult))
                link(dve.tensor_scalar(r4[:, 0], r4[:, 1], -NEG, NEG, ALU.mult, ALU.add))
                linked(l)
                link(dve.tensor_tensor(em.rearrange("p t (g e) -> p t g e", e=4), em.rearrange("p t (g e) -> p t g e", e=4),
                                       bcast(r4[:, 0], [P, TILES, 4, 4], 3), ALU.add))
                linked(l)
                one_hot(em, 16, iota16, r1[:, 2, :], r16[:, 1], r1[:, 1, :], r16[:, 2])
                link(dve.scalar_tensor_tensor(out=em, in0=r16[:, 2], scalar=2 * NEG, in1=em, op0=ALU.mult, op1=ALU.add))
                linked(l)
                one_hot(em, 16, iota16, r1[:, 3, :], r16[:, 1], r1[:, 1, :], r16[:, 3])
                dve.tensor_tensor(hotsum[:, :, :], r16[:, 2], r16[:, 3], ALU.add).then_inc(hot_ready, 1)
                dve.tensor_tensor(r1[:, 4, :], r1[:, 3, :], r1[:, 2, :], ALU.subtract).then_inc(router_sub, 1)
                dve.wait_ge(router_exp, l * 2 + 1)
                link(dve.tensor_reduce(r1[:, 5, :], r4[:, 2], AX_X, ALU.add))
                linked(l)
                dve.wait_ge(router_exp, l * 2 + 2)
                link(dve.tensor_scalar(r1[:, 6, :], r1[:, 4, :], 1.0, 2.0, ALU.add, ALU.mult))
                linked(l)
                link(dve.tensor_tensor(r1[:, 5, :], r1[:, 5, :], r1[:, 6, :], ALU.mult))
                linked(l)
                link(dve.reciprocal(r1[:, 6, :], r1[:, 5, :]))
                linked(l)
                link(dve.tensor_tensor(r1[:, 7, :], r1[:, 6, :], r1[:, 4, :], ALU.mult))

                dve.wait_ge(rank_psum, l * 1 + 1)
                rank = ps[:, 0, 64:112].rearrange("p (t e) -> p t e", t=TILES)
                counts = ps[:, 0, 112:128]
                link(dve.tensor_scalar(e16[:, 0, :], counts, P + 0.5, None, ALU.is_gt))
                linked(l)
                link(dve.scalar_tensor_tensor(out=e16[:, 0, :], in0=counts, scalar=2 * P + 0.5, in1=e16[:, 0, :],
                                              op0=ALU.is_gt, op1=ALU.add))
                linked(l)
                link(dve.tensor_copy(e16[:, 1, :], e16[:, 0, :]))
                for n, shift_by in enumerate((1, 2, 4, 8)):
                    linked(l)
                    src, dst = e16[:, 1 + n % 2, :], e16[:, 2 - n % 2, :]
                    link(dve.tensor_tensor(dst[:, shift_by:16], src[:, shift_by:16], src[:, 0:16 - shift_by], ALU.add))
                    link(dve.tensor_copy(dst[:, 0:shift_by], src[:, 0:shift_by]))
                linked(l)
                ends = e16[:, 1, :]
                link(dve.tensor_tensor(e16[:, 3, :], ends, e16[:, 0, :], ALU.subtract))
                linked(l)
                link(dve.tensor_scalar(e16[:, 3, :], e16[:, 3, :], float(N_EXP - 1), float(P), ALU.add, ALU.mult))
                linked(l)
                link(dve.tensor_tensor(e16[:, 3, :], e16[:, 3, :], cst[:, C_BLOCK:C_BLOCK + 16], ALU.subtract))
                link(dve.tensor_tensor(r16[:, 0], rank, bcast(cst[:, C_BLOCK:C_BLOCK + 16], [P, TILES, 16], 1), ALU.add))
                linked(l)
                link(dve.scalar_tensor_tensor(out=r16[:, 1], in0=rank, scalar=P - 0.5, in1=bcast(e16[:, 3, :], [P, TILES, 16], 1),
                                              op0=ALU.is_gt, op1=ALU.mult))
                linked(l)
                link(dve.tensor_tensor(r16[:, 0], r16[:, 0], r16[:, 1], ALU.add))
                linked(l)
                for k in range(2):
                    link(dve.tensor_tensor(r16[:, 2 + k], r16[:, 2 + k], r16[:, 0], ALU.mult))
                linked(l)
                for k in range(2):
                    link(dve.tensor_reduce(slot_f[:, k, :], r16[:, 2 + k], AX_X, ALU.add))
                linked(l)
                dve.tensor_copy(slot_i[:, :, :], slot_f[:, :, :]).then_inc(slots_ready, 1)
                link(dve.tensor_tensor(owner[:, :, :], cst[:, C_IOTA5:C_IOTA5 + 80].rearrange("p (n e) -> p n e", e=16),
                                       bcast(ends, [P, EXTRA, 16], 1), ALU.is_ge))
                linked(l)
                link(dve.tensor_reduce(ownerf[:, :], owner[:, :, :], AX_X, ALU.add))
                linked(l)
                link(dve.tensor_scalar(ownerf[:, :], ownerf[:, :], float(N_EXP - 1), None, ALU.min))
                linked(l)
                link(dve.tensor_copy(extra_i[0:1, 0:1], ends[0:1, 15:16]))
                link(dve.tensor_copy(extra_i[0:1, 1:6], ownerf[0:1, :]))
                linked(l)
                dve.tensor_copy(extra_i[0:1, 6:7], ends[0:1, 15:16]).then_inc(routed, 1)

                ada_rows("ada5", 3, 1, 2)

                def inputs_copied(i, u):
                    dve.wait_ge(xgT_psum, blocks(l, i, u) + 1)
                    dve.tensor_copy(hgT[:, (u + 1) % 2, 4:8, :].rearrange("p k n -> p (k n)"), ps[:, 1, :]).then_inc(hg_dve, 1)

                def activated(i, u):
                    par = (u + 1) % 2
                    dve.wait_ge(th_ready, blocks(l, i, u) + 1)
                    dve.scalar_tensor_tensor(out=act_t[:, par], in0=act_t[:, par], scalar=1.0, in1=ps[:, 2 + par, 0:CH],
                                             op0=ALU.add, op1=ALU.mult).then_inc(e_mul, 1)
                    dve.wait_ge(e_mul, blocks(l, i, u) + 1)
                    done("moe", i * 12 + moe_seq(u) + 2)
                    dve.tensor_tensor(act_a[:, par], act_t[:, par], ps[:, 2 + par, CH:2 * CH], ALU.mult).then_inc(a_made, 1)

                def activations_copied(i, u):
                    dve.wait_ge(aT_psum, blocks(l, i, u) + 1)
                    dve.tensor_copy(aTs[:, (u + 1) % 2].rearrange("p j n -> p (j n)"), ps[:, 4, 0:CH]).then_inc(aTs_ready, 1)

                def output_copied(i, u, last=False):
                    buf = (u + 1) % 4
                    done("moe", i * 12 + (11 if last else moe_down_seq(u)) + 1)
                    dve.wait_ge(y_free, blocks(l, i, u) + 1)
                    dve.tensor_copy(yb[:, buf, 512:D], ps[:, 6, :]).then_inc(y_dve, 1)

                inputs_copied(0, -1)
                activated(0, -1)
                inputs_copied(0, 0)
                with dve.Fori(0, 3) as i:
                    for u in range(4):
                        activations_copied(i, u - 1)
                        activated(i, u)
                        inputs_copied(i, u + 1)
                        output_copied(i, u - 1)
                for u in range(3):
                    activations_copied(3, u - 1)
                    activated(3, u)
                    if u < 2:
                        inputs_copied(3, u + 1)
                    output_copied(3, u - 1)
                activations_copied(3, 2)
                output_copied(3, 2, last=True)

                wait_apart(dve, routed, l + 1)
                extra = dve.value_load(extra_i[0:1, 0:1], min_val=0, max_val=EXTRA)
                with dve.If(extra > 0):
                    wait_apart(dve, y_free, l * N_EXP + N_EXP + 4)
                    with dve.Fori(0, EXTRA) as n:
                        dve.wait_ge(ov_xT, l * EXTRA + n + 1)
                        dve.tensor_copy(hgT[:, 0].rearrange("p (b k) n -> p b (k n)", b=2), ps[:, 0:2, :]).then_inc(ov_hg, 1)
                        dve.wait_ge(ov_t, l * EXTRA + n + 1)
                        dve.scalar_tensor_tensor(out=act_t[:, 0], in0=act_t[:, 0], scalar=1.0, in1=ps[:, 2, 0:CH],
                                                 op0=ALU.add, op1=ALU.mult).then_inc(ov_m, 1)
                        dve.wait_ge(ov_m, l * EXTRA + n + 1)
                        dve.tensor_tensor(act_a[:, 0], act_t[:, 0], ps[:, 2, CH:2 * CH], ALU.mult).then_inc(ov_a, 1)
                        dve.wait_ge(ov_aT, l * EXTRA + n + 1)
                        dve.tensor_copy(aTs[:, 0].rearrange("p j n -> p (j n)"), ps[:, 4, 0:CH]).then_inc(ov_as, 1)
                        dve.wait_ge(ov_y, l * EXTRA + n + 1)
                        dve.tensor_copy(yb[:, 0].rearrange("p (h c) -> p h c", h=2), ps[:, 5:7, :]).then_inc(ov_ye, 1)
                        dve.wait_ge(ov_ys, l * (16 * EXTRA) + n * 16 + 16)
                with dve.Else():
                    for one in (ov_hg, ov_m, ov_a, ov_as, ov_ye):
                        dve.sem_inc(one, EXTRA)

                dve.wait_ge(gb_ready, l * GB + GB)
                for t in range(TILES):
                    dve.wait_ge(yg_loaded[t], l * 32 + 32)
                    dve.wait_ge(y1_scaled, l * TILES + t + 1)
                    link(dve.scalar_tensor_tensor(out=yg[:, 0, t], in0=yg[:, 1, t], scalar=r1[:, 7, t:t + 1], in1=yg[:, 0, t],
                                                  op0=ALU.mult, op1=ALU.add))
                    linked(l)
                    link(dve.tensor_tensor(yg[:, 0, t], yg[:, 0, t], gb[:, min(t, 1), :], ALU.mult))
                    linked(l)
                    ins = dve.tensor_tensor(x[:, t, :], x[:, t, :], yg[:, 0, t], ALU.add)
                    if t < TILES - 1:
                        link(ins)
                    else:
                        ins.then_inc(x_ready, 1)
                linked(l)
                dve.wait_ge(x_ready, l * XR + XR + 1)
                assert count[0] == DVE_CHAIN, count[0]

            dve.wait_ge(rstd_ready, DEPTH * RS + 1)
            dve.wait_ge(stored, 16)
            for t in range(TILES):
                dve.scalar_tensor_tensor(out=xn[:, t, :], in0=x[:, t, :], scalar=rstd[:, t:t + 1], in1=fing,
                                         op0=ALU.mult, op1=ALU.mult).then_inc(fin_ready, 1)

        @block.scalar
        def _(act):
            act.wait_ge(init_loaded, 16 * INIT_LOADS)
            act.activation(condt[:, :, :], condr[:, :, :], ACT.Tanh, scale=0.5).then_inc(act_init, 1)
            act.wait_ge(init_dve, 1)
            act.activation(lgt[:, 2, :], lgt[:, 1, :], ACT.Exp, scale=-1.0).then_inc(act_init, 1)
            act.wait_ge(act_init, 2)
            act.activation(lgt[:, 3, :], lgt[:, 2, :], ACT.Ln, bias=1.0).then_inc(act_init, 1)
            act.wait_ge(init_dve, 10)
            act.activation(qdec[:, :, :, :], qdec[:, :, :, :], ACT.Exp).then_inc(act_init, 1)
            act.activation(kdec[:, :, :, :], kdec[:, :, :, :], ACT.Exp).then_inc(act_init, 1)
            act.activation(cdec[:, :, :, :], cdl[:, :, :, :], ACT.Exp).then_inc(act_init, 1)
            for ll in range(DEPTH):
                for h in range(4):
                    n = ll * 8 + h
                    act.activation(dec[:, ll, h, :], once[:, 256:384], ACT.Exp,
                                   scale=lg[:, n:n + 1]).then_inc(act_init, 1)
                    act.activation(work[:, (ll * 4 + h) * P:(ll * 4 + h + 1) * P], once[:, 384:512], ACT.Exp,
                                   scale=lg[:, n + 4:n + 5]).then_inc(act_init, 1)
            act.wait_ge(init_dve, 14)

            def squares(ready):
                act.wait_ge(*ready)
                for t in range(TILES):
                    act.activation(xn[:, t, :], x[:, t, :], ACT.Square, accum_out=ssq[:, t:t + 1]).then_inc(ssq_ready, 1)

            with act.Fori(0, DEPTH) as l:
                def done(seg, n):
                    act.wait_ge(chunk_done, l * LAYER_CHUNKS + (SEG[seg] + SLOTS) + n)

                act.wait_ge(x_ready, l * XR + 1)
                row = bass.ds(l, 1)
                for n, name in enumerate(("norm1_g", "norm2_g")):
                    act.dma_start(gain[:, n, :], a[name][row].rearrange("a (p k) -> p (a k)", k=KT)).then_inc(gains_loaded, 16)
                loads = [
                    (rw[:, :, 0:4], a["router_group_w"][row].rearrange("a (p k) c -> p (a k) c", k=KT)),
                    (rw[:, :, 4:20], a["router_expert_w"][row].rearrange("a (p k) c -> p (a k) c", k=KT)),
                    (rb[:, 0:4], a["router_group_b"][row].to_broadcast([P, 4])),
                    (rb[:, 4:20], a["router_expert_b"][row].to_broadcast([P, 16])),
                    (ret_g[:, :], a["ret_norm_g"][row].to_broadcast([P, 256])),
                    (sink[:, :], a["swa_sink"][row].to_broadcast([P, 4])),
                    (cache_k[:, 0:8, :], a["cache_na_k"][0][row].rearrange("a h s d -> s (a h) d")),
                    (cache_k[:, 8:10, :], a["cache_swa_k"][0][row].rearrange("a h s d -> s (a h) d")),
                    (cache_v[:, 0:8, :], a["cache_na_v"][0][row].rearrange("a h s d -> s (a h) d")),
                    (cache_v[:, 8:10, :], a["cache_swa_v"][0][row].rearrange("a h s d -> s (a h) d")),
                    (state0[:, :, :, :].rearrange("p r b e -> p (r b) e"),
                     a["state_ret"][0][row].rearrange("a r h d e -> (a r h d) e").rearrange("(n p) e -> p n e", p=P)),
                ]
                for dst, src in loads:
                    act.dma_start(dst, src).then_inc(small_loaded, 16)
                for rp in range(2):
                    for h in range(HEADS_NA):
                        off = l * (HEADS_NA * RPB) + (h * RPB + (5 - rp) * RPB_W + WIN_COLS - GRID_W)
                        src = bass.AP(tensor=a["na_rpb_flat"].tensor, offset=off,
                                      ap=[[1, GRID_W], [RPB_W, 6], [1, GRID_W]])
                        act.dma_start(bias_turned[rp * GRID_W:(rp + 1) * GRID_W, h, :].rearrange("p (s c) -> p s c", s=6),
                                      src).then_inc(small_loaded, 16)

                def norm(which):
                    act.wait_ge(mod_ready, l * MODR + 2 * which + 2)
                    for k in range(1, KT, 2):
                        act.wait_ge(xT_psum, l * XT + 8 * which + k + 1)
                        for c, (n0, n1) in enumerate(((0, P), (P, TOK))):
                            act.activation(hT[:, k, n0:n1], ps[:, k, n0:n1], ACT.Identity, scale=scale[:, k, c:c + 1],
                                           bias=shift[:, k, c:c + 1]).then_inc(hT_act, 1)

                def gate_rows(which, factor):
                    for n in range(4):
                        act.wait_ge(gb_psum, l * GB + 4 * which + n + 1 + 1)
                        act.activation(gb[:, n // 2, (n % 2) * 512:(n % 2 + 1) * 512], ps[:, 4 + n, :], ACT.Copy,
                                       scale=factor).then_inc(gb_ready, 1)

                squares((x_ready, l * XR + 1))
                norm(0)

                with act.Fori(0, Z_CHUNKS // SLOTS) as i:
                    for s in (1, 3):
                        done("z", i * SLOTS + (s + 1))
                        act.activation(zt[:, :, bass.ds(i * (SLOTS * CH) + s * CH, CH)], ps[:, 3:6, 0:CH],
                                       ACT.Copy).then_inc(zt_act, 1)

                act.wait_ge(bias_psum, l * HEADS_NA + HEADS_NA)
                act.wait_ge(zt_dve, l * ZD + ZD + 1)
                act.wait_ge(zt_act, l * ZD + ZD + 1)
                act.activation(rot[:, 0, 0:256].rearrange("p (ha hb i) -> p hb ha i", ha=2, hb=2),
                               zt[:, 0, QS:QS + 256].rearrange("p (hb ha i) -> p hb ha i", ha=2, hb=2), ACT.Copy).then_inc(rot_act, 1)
                act.activation(rot[:, 0, 256:384], zt[:, 0, KS:KS + P], ACT.Copy).then_inc(rot_act, 1)

                for u in range(1, TP, 2):
                    act.wait_ge(t_psum, l * TP + u + 1)
                    if u == 9:
                        act.activation(kcT[:, 4, :], ps[:, 1, 0:P], ACT.Copy).then_inc(t_act, 1)
                        continue
                    v = u if u < 8 else u - 2
                    act.activation(qkT[:, v, :], ps[:, u % 8, 0:TOK], ACT.Copy,
                                   scale=HD ** -0.5 if v in SCALED else 1.0).then_inc(t_act, 1)
                act.activation(tgr, zt[:, :, GR:GR + 256], ACT.Tanh, scale=0.5).then_inc(tgr_ready, 1)

                def exp(g, j):
                    t, kind = GROUPS[g]
                    w = P if t == 0 else 384
                    if j == 0:
                        act.wait_ge(nmax_ready, l * NG + g + 1)
                    act.activation(sbuf_s[:, g % 2, j, 0:w], sbuf_s[:, g % 2, j, 0:w], ACT.Exp,
                                   bias=nmx[:, g % 2, j:j + 1], accum_out=den[:, g % 2, j:j + 1]).then_inc(exp_ready, 1)
                    if kind == 2 and j == 3:
                        act.activation(sk[:, g % 2, :], sk[:, g % 2, :], ACT.Exp).then_inc(sink_exp, 1)

                def copy(g, j):
                    w = P if GROUPS[g][0] == 0 else 384
                    u = 4 * g + j
                    act.wait_ge(pt_psum, l * SU + u + 1)
                    if u >= 2:
                        act.wait_ge(pv_done, l * SU + u - 1)
                    act.activation(pT[:, u % 2, 0:w], ps[:, 4 + u % 2, 0:w], ACT.Copy).then_inc(pT_ready, 1)

                for j in range(4):
                    exp(0, j)
                for g in range(NG):
                    copy(g, 0)
                    copy(g, 1)
                    for j in range(4):
                        if g + 1 < NG:
                            exp(g + 1, j)
                        if j < 2:
                            copy(g, j + 2)

                for j in range(1, KT, 2):
                    act.wait_ge(ot_psum, l * KT + j + 1)
                    act.activation(oT[:, j, :], ps[:, j, 0:TOK], ACT.Copy).then_inc(ot_act, 1)

                with act.Fori(0, G_CHUNKS // SLOTS) as i:
                    for b in range(8):
                        if b % 2 == 0:
                            act.wait_ge(gate_psum, l * G_CHUNKS + i * SLOTS + b // 2 + 1)
                        else:
                            done("g", i * SLOTS + b // 2 + 1)
                        act.activation(arena[:, bass.ds(i * (8 * TOK) + (9216 + b * TOK), TOK)], ps[:, b, 0:TOK],
                                       ACT.Tanh, scale=0.5).then_inc(gate_ready, 1)
                gate_rows(0, 0.5)

                squares((x_ready, l * XR + 1 + 1))
                norm(1)

                for t in range(TILES):
                    act.wait_ge(h2_psum, l * TILES + t + 1)
                    act.activation(xn[:, t, :].rearrange("p (h c) -> p h c", h=2), ps[:, 2 + 2 * t:4 + 2 * t, :],
                                   ACT.Copy).then_inc(h2_ready, 1)

                act.wait_ge(router_sub, l * 2 + 1)
                act.activation(r4[:, 2], r4[:, 2], ACT.Exp).then_inc(router_exp, 1)
                act.wait_ge(router_sub, l * 2 + 2)
                act.activation(r1[:, 4, :], r1[:, 4, :], ACT.Exp).then_inc(router_exp, 1)

                gate_rows(1, 1.0)

                def inputs_copied(i, u):
                    act.wait_ge(xgT_psum, blocks(l, i, u) + 1)
                    act.activation(hgT[:, (u + 1) % 2, 0:4, :].rearrange("p k n -> p (k n)"), ps[:, 0, :],
                                   ACT.Copy).then_inc(hg_act, 1)

                def gate_tanh(i, u):
                    par = (u + 1) % 2
                    if u >= 0:
                        act.wait_ge(a_made, blocks(l, i, u))
                    done("moe", i * 12 + moe_seq(u) + 2)
                    act.activation(act_t[:, par], ps[:, 2 + par, 0:CH], ACT.Tanh, scale=0.5).then_inc(th_ready, 1)

                def output_copied(i, u):
                    buf = (u + 1) % 4
                    act.wait_ge(y_psum, blocks(l, i, u) + 1)
                    act.wait_ge(y_free, blocks(l, i, u) + 1)
                    act.activation(yb[:, buf, 0:512], ps[:, 5, :], ACT.Copy).then_inc(y_act, 1)

                inputs_copied(0, -1)
                gate_tanh(0, -1)
                inputs_copied(0, 0)
                with act.Fori(0, 3) as i:
                    for u in range(4):
                        gate_tanh(i, u)
                        inputs_copied(i, u + 1)
                        output_copied(i, u - 1)
                for u in range(3):
                    gate_tanh(3, u)
                    if u < 2:
                        inputs_copied(3, u + 1)
                    output_copied(3, u - 1)
                output_copied(3, 2)

                wait_apart(act, routed, l + 1)
                extra = act.value_load(extra_i[0:1, 0:1], min_val=0, max_val=EXTRA)
                with act.If(extra > 0):
                    wait_apart(act, y_free, l * N_EXP + N_EXP + 4)
                    with act.Fori(0, EXTRA) as n:
                        row = act.snap(n * P + N_EXP * P)
                        act.dma_start(xg[:, 0, :], a["xs"][bass.ds(row, P)]).then_inc(ov_x, 16)
                        act.wait_ge(ov_g, l * EXTRA + n + 1)
                        act.activation(act_t[:, 0], ps[:, 2, 0:CH], ACT.Tanh, scale=0.5).then_inc(ov_t, 1)
                        wait_apart(act, ov_ye, l * EXTRA + n + 1)
                        act.dma_start(a["ys"][bass.ds(row, P)], yb[:, 0, :]).then_inc(ov_ys, 16)
                        wait_apart(act, ov_ys, l * (16 * EXTRA) + n * 16 + 16)
                with act.Else():
                    act.sem_inc(ov_t, EXTRA)
                    act.sem_inc(ov_x, 16 * EXTRA)
                    act.sem_inc(ov_ys, 16 * EXTRA)

                for t in range(TILES):
                    act.wait_ge(yg_loaded[t], l * 32 + 32)
                    act.activation(yg[:, 0, t], yg[:, 0, t], ACT.Identity, scale=r1[:, 6, t:t + 1], bias=zero1[:, 0:1]).then_inc(y1_scaled, 1)

            squares((x_ready, DEPTH * XR + 1))

        @block.gpsimd
        def _(pool):
            def root(n, ready, src, mid, dst, width, mean, signal):
                wait_apart(pool, *ready)
                pool.tensor_scalar(mid[:, :], src[:, :], 1.0 / mean, EPS, ALU.mult, ALU.add).then_inc(pool_step, 1)
                pool.wait_ge(pool_step, n)
                pool.tensor_tensor(dst[:, :], mid[:, :], mhalf[:, 0:width], ALU.pow).then_inc(signal, 1)

            pool.wait_ge(init_dve, 14)
            pool.sem_inc(gate_ready, 8)
            pool.sem_inc(y_free, 4)
            with pool.Fori(0, DEPTH) as l:
                def ada_bias(first, count, ready):
                    pool.wait_ge(*ready)
                    pool.dma_start(mrow[0:2, 0:count], a["ada_b"][bass.ds(l, 1), first:first + count].to_broadcast([2, count])
                                   ).then_inc(adab_loaded, 16)

                ada_bias(0, 2 * D, (gb_psum, l * GB + 1))
                wait_apart(pool, x_ready, l * XR + 1)
                for c0 in (0, P + 384):
                    pool.memset(bias[:, :, c0:c0 + P], 0.0).then_inc(bias_ready, 1)
                root(l * POOL_L + 1, (ssq_ready, l * SSQ + 3), ssq, msq, rstd, 3, D, rstd_ready)
                ada_bias(2 * D, D, (mod_psum, l * MODP + 1))
                pool.wait_ge(zt_dve, l * ZD + ZD + 1)
                pool.wait_ge(zt_act, l * ZD + ZD + 1)
                for i, (t, d) in enumerate(((0, 0), (0, 1), (1, 0), (2, 1))):
                    kdl = kdec[:, :, :, :].rearrange("p l r h -> p (l r h)")[:, bass.ds(l * 8 + 4 * d, 4)]
                    pool.tensor_tensor(kd[:, i, :].rearrange("p (h d) -> p h d", d=HD),
                                       zt[:, t, KR:KR + 256].rearrange("p (h d) -> p h d", d=HD),
                                       kdl.unsqueeze(2).to_broadcast([P, 4, HD]), ALU.mult).then_inc(kd_ready, 1)
                for name, c0, n in (("new_na_k", KA, 8), ("new_na_v", VA, 8), ("new_swa_k", KS, 2), ("new_swa_v", VS, 2)):
                    pool.dma_start(out[name][0][bass.ds(l, 1)].rearrange("a h s d -> s (a h) d"),
                                   zt[:, 0, c0:c0 + n * HD].rearrange("p (h d) -> p h d", d=HD)).then_inc(kv_stored, 16)
                with pool.If(l < 1):
                    pool.dma_start(a["xs"].rearrange("(b p) d -> p b d", p=P),
                                   x[:, 0:1, :].to_broadcast([P, BLOCKS, D])).then_inc(filled, 16)
                    pool.dma_start(a["ys"][N_EXP * P:BLOCKS * P].rearrange("(b p) d -> p b d", p=P),
                                   x[:, 0:1, :].to_broadcast([P, EXTRA, D])).then_inc(filled, 16)
                pool.wait_ge(state_ready, l * 10 + 2)
                pool.dma_start(out["new_state"][0][bass.ds(l, 1)].rearrange("a r h d e -> (a r h d) e").rearrange("(n p) e -> p n e", p=P),
                               state_out[:, :, :, :].rearrange("p r b e -> p (r b) e")).then_inc(kv_stored, 16)
                root(l * POOL_L + 2, (ret_ssq, l * 1 + 1), ssq12, msq12, rstd12, 12, HD, rsq_ready)
                ada_bias(3 * D, 2 * D, (gb_psum, l * GB + 4 + 1))
                root(l * POOL_L + 3, (ssq_ready, l * SSQ + 6), ssq, msq, rstd, 3, D, rstd_ready)
                ada_bias(5 * D, D, (mod_psum, l * MODP + 2))

                wait_apart(pool, h2_ready, l * TILES + TILES)
                wait_apart(pool, slots_ready, l + 1)
                pool.wait_ge(filled, 32)
                for k in range(2):
                    for t in range(TILES):
                        pool.indirect_dma_start(a["xs"], bass.IndirectOffsetOnAxis(ap=slot_i[:, k, t:t + 1], axis=0),
                                                xn[:, t, :], None).then_inc(scattered, 16)
                wait_apart(pool, scattered, l * 96 + 96)

                def load_block(row, buf):
                    pool.dma_start(xg[:, buf, :], a["xs"][bass.ds(row, P)]).then_inc(xg_loaded[buf], 16)

                def store_block(i, u):
                    buf = (u + 1) % 4
                    row = pool.snap(i * (4 * P) + (u + 1) * P)
                    pool.wait_ge(y_act, blocks(l, i, u) + 2)
                    pool.wait_ge(y_dve, blocks(l, i, u) + 2)
                    pool.dma_start(a["ys"][bass.ds(row, P)], yb[:, buf, :]).then_inc(y_stored, 16)

                for buf in range(4):
                    load_block(buf * P, buf)
                with pool.Fori(0, 3) as i:
                    for u in range(-1, 3):
                        store_block(i, u)
                        row = pool.snap(i * (4 * P) + (u + 5) * P)
                        pool.wait_ge(xgT_psum, blocks(l, i, u) + 1)
                        load_block(row, (u + 1) % 4)
                        wait_apart(pool, y_stored, blocks(l, i, u) * 16 + 16)
                        pool.sem_inc(y_free, 1)
                for u in range(-1, 3):
                    pool.wait_ge(y_act, blocks(l, 3, u) + 2)
                    wait_apart(pool, y_dve, blocks(l, 3, u) + 2)
                    row = (3 * 4 + u + 1) * P
                    pool.dma_start(a["ys"][row:row + P], yb[:, u + 1, :]).then_inc(y_stored, 16)
                    wait_apart(pool, y_stored, blocks(l, 3, u) * 16 + 16)
                    pool.sem_inc(y_free, 1)

                wait_apart(pool, ov_ys, l * (16 * EXTRA) + 16 * EXTRA)
                for t in range(TILES):
                    for k in range(2):
                        pool.indirect_dma_start(yg[:, k, t], None, a["ys"],
                                                bass.IndirectOffsetOnAxis(ap=slot_i[:, k, t:t + 1], axis=0)).then_inc(yg_loaded[t], 16)

            pool.dma_start(fing, a["final_norm_g"].unsqueeze(0).to_broadcast([P, D])).then_inc(stored, 16)
            root(DEPTH * POOL_L + 1, (ssq_ready, DEPTH * SSQ + 3), ssq, msq, rstd, 3, D, rstd_ready)
            pool.wait_ge(fin_ready, 1)
            pool.dma_start(out["y_prompt"][0], xn[:, 0, :]).then_inc(stored, 16)
            pool.wait_ge(fin_ready, 3)
            pool.dma_start(out["y_sample"][0].rearrange("(t p) d -> p t d", p=P), xn[:, 1:3, :]).then_inc(stored, 16)
            pool.wait_ge(kv_stored, DEPTH * KV_L)
            pool.wait_ge(stored, 48)


_OUTS = {"y_prompt": (1, 128, 1024), "y_sample": (1, 256, 1024), "new_na_k": (1, 2, 8, 128, 64),
         "new_na_v": (1, 2, 8, 128, 64), "new_swa_k": (1, 2, 2, 128, 64), "new_swa_v": (1, 2, 2, 128, 64),
         "new_state": (1, 2, 2, 4, 64, 64)}


def kernel(**inputs):
    import numpy as _np
    import concourse.bacc as _bacc
    from concourse.bass_utils import run_bass_kernel_spmd as _run

    nc = _bacc.Bacc("TRN2", target_bir_lowering=False, num_devices=1)
    arrays, args, outs = {}, {}, {}
    laid = {k: _np.ascontiguousarray(v) for k, v in inputs.items()}
    laid["na_rpb_flat"] = laid.pop("na_rpb").reshape(1, -1)
    laid["consts"] = constants()
    for name, v in laid.items():
        arrays[f"in_{name}"] = v
        args[name] = nc.dram_tensor(f"in_{name}", v.shape, mybir.dt.from_np(v.dtype), kind="ExternalInput").ap()
    for name, shape in _OUTS.items():
        outs[name] = nc.dram_tensor(f"out_{name}", shape, F32, kind="ExternalOutput").ap()
    for name in ("xs", "ys"):
        args[name] = nc.dram_tensor(f"scratch_{name}", (BLOCKS * P, D), F32, kind="Internal").ap()
    build(nc, args, outs)
    r = _run(nc, [arrays], core_ids=[0])
    return tuple(r.results[0][f"out_{name}"] for name in _OUTS)
```

```python
from contextlib import ExitStack

import numpy as np

import concourse.bass as bass
from concourse import mybir

F32 = mybir.dt.float32
F32R = mybir.dt.float32r
U32 = mybir.dt.uint32
I32 = mybir.dt.int32
ALU = mybir.AluOpType
ACT = mybir.ActivationFunctionType
AX_X = mybir.AxisListType.X

P = 128
D = 1024
DEPTH = 2
TILES = 3
TOK = TILES * P
KT = D // P
GRID_W = 64
HD = 64
HEADS_NA, HEADS_SWA, KV_SWA, HEADS_RET = 8, 4, 2, 4
WIN_COLS, WIN_ROWS = 16, 8
RPB_W = 2 * WIN_COLS - 1
RPB = (2 * WIN_ROWS - 1) * RPB_W
N_EXP, N_GRP, D_EXP = 16, 4, 256
IN_COLS = 6144
EPS = 1e-6
NEG = -1e30
EXTRA = 5
BLOCKS = N_EXP + EXTRA

QA, KA, VA, QS, KS, VS, QR, KR, VR, GR = 0, 512, 1024, 1536, 1792, 1920, 2048, 2304, 2560, 2816
Z_COLS = 3072

CH = 256
SLOTS = 4
Z_CHUNKS = Z_COLS // CH
G_CHUNKS = (IN_COLS - Z_COLS) // CH
LAYER_CHUNKS = 6 * 4 + Z_CHUNKS + G_CHUNKS + 4 + 4 + 2 * N_EXP + N_EXP
SLOT_LOADS = 16 * LAYER_CHUNKS // SLOTS

BIAS_W = P + 6 * GRID_W

C_IDENT, C_COS, C_SIN = 0, 128, 192
C_COLMASK = 256
C_SWAMASK = 320
C_POS = 1088
C_IOTA = 1092
C_TURN = 1108
C_BEFORE = 1236
C_ONE = 1364
C_BLOCK = 1365
C_GROUP = 1381
C_LANE = 1383
C_TOKEN = 1511
C_BLOCKS = 1514
C_END = 1536
C_MASKF, C_MASKB, C_DIFFF, C_DIFFB = 1536, 1664, 1792, 1920
C_ALL = 2048


def constants():
    c = np.zeros((P, C_ALL), np.float32)
    p = np.arange(P)
    c[:, C_IDENT:C_IDENT + P] = np.eye(P)
    inv = (np.float32(10000.0) ** (-np.arange(16, dtype=np.float32) / np.float32(16))).astype(np.float32)
    for t in range(2):
        tok = p + P * t
        ang = np.concatenate([(tok // GRID_W).astype(np.float32)[:, None] * inv,
                              (tok % GRID_W).astype(np.float32)[:, None] * inv], axis=1)
        c[:, C_COS + 32 * t:C_COS + 32 * t + 32] = np.cos(ang)
        c[:, C_SIN + 32 * t:C_SIN + 32 * t + 32] = np.sin(ang)
    col = p % GRID_W
    start = np.clip(col - WIN_COLS // 2, 0, GRID_W - WIN_COLS)
    k = np.arange(GRID_W)
    inside = (k[None] >= start[:, None]) & (k[None] < start[:, None] + WIN_COLS)
    c[:, C_COLMASK:C_COLMASK + GRID_W] = np.where(inside, 0, NEG)
    keys = np.arange(256)
    far0 = np.abs(p[:, None] - keys[None]) > 128
    far1 = np.abs(p[:, None] + P - keys[None]) > 128
    c[:, C_SWAMASK:C_SWAMASK + 256] = np.where(far0, NEG, 0)
    c[:, C_SWAMASK + 384 + 128:C_SWAMASK + 768] = np.where(far1, NEG, 0)
    q = np.arange(P)[None]
    kk = p[:, None]
    c[:, C_MASKF:C_MASKF + P] = q >= kk
    c[:, C_MASKB:C_MASKB + P] = kk >= q
    c[:, C_DIFFF:C_DIFFF + P] = np.maximum(q - kk, 0)
    c[:, C_DIFFB:C_DIFFB + P] = np.maximum(kk - q, 0)
    c[:, C_POS:C_POS + 4] = np.stack([p + 1, P - p, P - 1 - p, p], 1)
    c[:, C_IOTA:C_IOTA + 16] = np.arange(16)[None]
    c[:, C_BEFORE:C_BEFORE + P] = kk < q
    c[:, C_ONE] = 1
    c[:, C_LANE:C_LANE + P] = np.arange(P)[None]
    c[:, C_TOKEN:C_TOKEN + TILES] = p[:, None] + P * np.arange(TILES)[None]
    c[:, C_BLOCKS:C_BLOCKS + 22] = P * np.arange(22)[None]
    for n in range(2):
        c[p % 32 == n, C_GROUP + n] = 1
    c[:, C_BLOCK:C_BLOCK + 16] = P * np.arange(16)[None]
    c[p, C_TURN + (p // GRID_W) * GRID_W + (GRID_W - 1 - p % GRID_W)] = 1
    return c


def build(nc, a, out):
    ctx = ExitStack()
    with ctx:
        def sb(name, shape, dtype=F32):
            return ctx.enter_context(nc.sbuf_tensor(name, shape, dtype))

        def sem(name):
            return ctx.enter_context(nc.semaphore(name))

        x = sb("x", [P, TILES, D])
        h_hi = sb("h_hi", [P, KT, TOK], F32R)
        h_lo = sb("h_lo", [P, KT, TOK], F32R)
        w_hi = sb("w_hi", [P, 2, 2, CH], F32R)
        w_lo = sb("w_lo", [P, 2, 2, CH], F32R)
        arena = sb("arena", [P, 60 * 256])
        hT = arena[:, 0:KT * TOK].rearrange("p (k n) -> p k n", k=KT)
        zt = arena[:, 0:TILES * Z_COLS].rearrange("p (t c) -> p t c", t=TILES)

        def gate_tile(f):
            at = 9216 + f * TOK
            if f >= 16:
                at = (1 + (f - 16) % 4 // 2) * Z_COLS + (KA if f < 20 else KR) + (f % 2) * TOK
            return arena[:, at:at + TOK]

        qkT = arena[:, 9216:9216 + 15 * TOK].rearrange("p (b n) -> p b n", n=TOK)
        ret_g = arena[:, 14976:15232]
        bias_turned = arena[:, 11904:11904 + HEADS_NA * 384].rearrange("p (h c) -> p h c", c=384)
        zT = arena[:, 0:KT * TOK].rearrange("p (b n) -> p b n", n=TOK)
        xg = arena[:, 0:4096].rearrange("p (b c) -> p b c", b=4)
        yb = arena[:, 4096:8192].rearrange("p (b c) -> p b c", b=4)
        hgT = arena[:, 8192:10240].rearrange("p (b k n) -> p b k n", b=2, k=KT)
        act_a = arena[:, 10240:10752].rearrange("p (b c) -> p b c", b=2)
        act_t = arena[:, 10752:11264].rearrange("p (b c) -> p b c", b=2)
        aTs = arena[:, 11264:11776].rearrange("p (b j n) -> p b j n", b=2, j=2)
        hotsum = arena[:, 11776:11824].rearrange("p (t e) -> p t e", e=16)
        e16 = arena[:, 11824:11888].rearrange("p (n e) -> p n e", e=16)
        owner = arena[:, 11888:11968].rearrange("p (n e) -> p n e", e=16)
        ownerf = arena[:, 11968:11973]
        r16 = arena[:, 11976:12168].rearrange("p (n t e) -> p n t e", n=4, t=TILES)
        lo = arena[:, 12168:12228].rearrange("p (t c) -> p t c", t=TILES)
        rmod = arena[:, 12288:12336].rearrange("p (t e) -> p t e", e=16)
        hot_rmod = arena[:, 12336:12432].rearrange("p (k t e) -> p k t e", k=2, e=16)
        lane = arena[:, 12432:12438].rearrange("p (k t) -> p k t", k=2)
        first = arena[:, 12438:12444].rearrange("p (k t) -> p k t", k=2)
        at_lane = arena[:, 12448:13216].rearrange("p (k t n) -> p k t n", k=2, t=TILES)
        at_block = arena[:, 13216:13348].rearrange("p (k t n) -> p k t n", k=2, t=TILES)
        loT = arena[0:20, 13400:13400 + TOK]
        spare = arena[0:1, 13348:13348 + 4 * EXTRA]
        yg = arena[:, 0:6144].rearrange("p (k t c) -> p k t c", k=2, t=TILES)
        ring = sb("ring", [P, SLOTS, KT, CH])
        biasT = sb("biasT", [P, HEADS_NA * BIAS_W + P])
        oT = biasT[:, 0:KT * TOK].rearrange("p (b n) -> p b n", n=TOK)
        tgr = biasT[:, 3072:3840].rearrange("p (t c) -> p t c", t=TILES)
        gb = sb("gb", [P, 2, D])
        mrow = sb("mrow", [P, 2 * D])
        work = sb("work", [P, 15 * 256])
        sbuf_s = work[:, 0:3072].rearrange("p (g h c) -> p g h c", g=2, h=4)
        pT = work[:, 3072:3840].rearrange("p (b c) -> p b c", b=2)
        xn = work[:, 0:3072].rearrange("p (t c) -> p t c", t=TILES)
        rot = work[:, 1536:1536 + TILES * 384].rearrange("p (t c) -> p t c", t=TILES)
        rprod = work[:, 0:1536].rearrange("p (n t h i) -> p n t h i", n=4, t=2, h=6)
        am = work[:, 0:1536].rearrange("p (t c) -> p t c", t=TILES)
        ret_o = work[:, 1536:2304]
        ret_u = work[:, 2304:3072]
        ret_w = work[:, 3072:3584]
        cache_k = work[:, 3072:3712].rearrange("p (h d) -> p h d", d=HD)
        state1 = work[:, 3584:3840].rearrange("p (r b e) -> p r b e", r=2, b=2)
        br_u = work[:, 0:384]
        br_w = work[:, 384:768]
        cst = sb("cst", [P, C_END])
        once = work[:, 2048:2560]
        kcT = sb("kcT", [P, 5, P])
        cache_v = sb("cache_v", [P, 10, HD])
        cond = sb("cond", [P, KT, 2])
        cond32 = sb("cond32", [P, KT, 32])
        modb = sb("modb", [P, 4, KT])
        condr = work[:, 2560:2576].rearrange("p (c k) -> p c k", c=2)
        condt = work[:, 2576:2592].rearrange("p (c k) -> p c k", c=2)
        gain = sb("gain", [P, 2, KT])
        shift = sb("shift", [P, KT, 2])
        scale = sb("scale", [P, KT, 2])
        ssq = sb("ssq", [P, TILES])
        msq = sb("msq", [P, TILES])
        rstd = sb("rstd", [P, TILES])
        ssq12 = sb("ssq12", [P, 12])
        msq12 = sb("msq12", [P, 12])
        rstd12 = sb("rstd12", [P, 12])
        mhalf = sb("mhalf", [P, 12])
        zero1 = sb("zero1", [P, 1])
        rw = sb("rw", [P, KT, 20])
        rb = sb("rb", [P, 20])
        sink = sb("sink", [P, 4])
        state0 = sb("state0", [P, 2, 2, HD])
        state_out = sb("state_out", [P, 2, 2, HD])
        kd = sb("kd", [P, 4, 256])
        lg = sb("lg", [P, 16])
        lgt = work[:, 2592:2656].rearrange("p (n c) -> p n c", c=16)
        qdec = sb("qdec", [P, DEPTH, 2, 4])
        kdec = sb("kdec", [P, DEPTH, 2, 4])
        cdec = sb("cdec", [P, DEPTH, 2, 2])
        cdl = sb("cdl", [P, DEPTH, 2, 2])
        dec = sb("dec", [P, DEPTH, 4, P])
        mx = sb("mx", [P, 2, 4])
        nmx = sb("nmx", [P, 2, 4])
        den = sb("den", [P, 2, 4])
        rden = sb("rden", [P, 2, 4])
        sk = sb("sk", [P, 2, 4])
        r4 = sb("r4", [P, 3, TILES, 4])
        r1 = sb("r1", [P, 8, TILES])
        slot_f = sb("slot_f", [P, 2, TILES])
        slot_i = ctx.enter_context(nc.sbuf_tensor("slot_i", [P, 2, TILES], U32))
        token_i = ctx.enter_context(nc.sbuf_tensor("token_i", [P, 22], U32))
        extra_i = ctx.enter_context(nc.sbuf_tensor("extra_i", [1, 8], I32))
        fing = biasT[:, 0:D]
        ps = ctx.enter_context(nc.psum_tensor("ps", [P, 8, 512], F32))

        ident = cst[:, C_IDENT:C_IDENT + P]

        init_loaded = sem("init_loaded")
        INIT_LOADS = 5
        x_loaded = sem("x_loaded")
        SMALL_L = 16 * 27
        init_dve = sem("init_dve")
        act_init = sem("act_init")
        slot_loaded = [sem(f"slot_loaded{i}") for i in range(SLOTS)]
        chunk_done = sem("chunk_done")
        gains_loaded = sem("gains_loaded")
        small_loaded = sem("small_loaded")
        adab_loaded = sem("adab_loaded")
        ADA = 12
        ada_row = sem("ada_row")
        mod_psum, MODP = sem("mod_psum"), 2
        mod_ready, MODR = sem("mod_ready"), 4
        gb_psum, GB = sem("gb_psum"), 8
        gb_ready = sem("gb_ready")
        x_ready, XR = sem("x_ready"), 2
        ssq_ready, SSQ = sem("ssq_ready"), 6
        pool_step = sem("pool_step")
        POOL_L = 3
        rstd_ready, RS = sem("rstd_ready"), 2
        xn_ready, XN = sem("xn_ready"), 6
        xT_psum, XT = sem("xT_psum"), 16
        hT_dve, HT = sem("hT_dve"), 16
        hT_act = sem("hT_act")
        split_hi, split_lo = sem("split_hi"), sem("split_lo")
        whi_ready, wlo_ready = sem("whi_ready"), sem("wlo_ready")
        QUARTERS = 4 * (Z_CHUNKS + G_CHUNKS + 4)
        quarter_done = sem("quarter_done")
        QD = 3 * (Z_CHUNKS + G_CHUNKS + 4)
        zt_dve, ZD = sem("zt_dve"), Z_CHUNKS // 2
        zt_act = sem("zt_act")
        kv_stored = sem("kv_stored")
        KV_L = 5 * 16
        rot_act = sem("rot_act")
        rot_dve = sem("rot_dve")
        RD = 6
        t_psum, TP = sem("t_psum"), 17
        t_dve, TD = sem("t_dve"), 9
        t_act, TA = sem("t_act"), 8
        bias_psum = sem("bias_psum")
        bias_ready = sem("bias_ready")
        BIAS_L = 2 + HEADS_NA
        s_psum, SU = sem("s_psum"), 36
        s_ready = sem("s_ready")
        nmax_ready, NG = sem("nmax_ready"), 9
        exp_ready = sem("exp_ready")
        sink_exp = sem("sink_exp")
        pt_psum = sem("pt_psum")
        pT_ready = sem("pT_ready")
        pv_done = sem("pv_done")
        o_ready = sem("o_ready")
        kd_ready = sem("kd_ready")
        kv_psum = sem("kv_psum")
        state_ready = sem("state_ready")
        a_psum = sem("a_psum")
        am_ready = sem("am_ready")
        ro_psum = sem("ro_psum")
        ret_read = sem("ret_read")
        tgr_ready = sem("tgr_ready")
        ret_ssq = sem("ret_ssq")
        rsq_ready = sem("rsq_ready")
        router_sub = sem("router_sub")
        router_exp = sem("router_exp")
        ro_ready = sem("ro_ready")
        ot_psum = sem("ot_psum")
        ot_dve = sem("ot_dve")
        ot_act = sem("ot_act")
        GT = 24
        gate_ready = sem("gate_ready")
        br_psum = sem("br_psum")
        br_read = sem("br_read")
        zT_ready = sem("zT_ready")
        z_hi, z_lo = sem("z_hi"), sem("z_lo")
        out_read = sem("out_read")
        loT_psum, loT_ready = sem("loT_psum"), sem("loT_ready")
        lo_psum = sem("lo_psum")
        h2_psum = sem("h2_psum")
        h2_ready = sem("h2_ready")
        hot_ready = sem("hot_ready")
        rank_psum = sem("rank_psum")
        routed = sem("routed")
        filled = sem("filled")
        xs_stored = sem("xs_stored")
        places_ready = sem("places_ready")
        token_psum = sem("token_psum")
        tokens_ready = sem("tokens_ready")
        xg_loaded = [sem(f"xg_loaded{i}") for i in range(4)]
        xgT_psum = sem("xgT_psum")
        hg_act = sem("hg_act")
        hg_dve = sem("hg_dve")
        th_ready = sem("th_ready")
        e_mul = sem("e_mul")
        a_made = sem("a_made")
        aT_psum = sem("aT_psum")
        aTs_ready = sem("aTs_ready")
        y_psum = sem("y_psum")
        y_act = sem("y_act")
        y_dve = sem("y_dve")
        y_stored = sem("y_stored")
        y_free = sem("y_free")
        yg_loaded = [sem(f"yg_loaded{i}") for i in range(TILES)]
        y1_scaled = sem("y1_scaled")
        ov_w, ov_x, ov_xT, ov_hg, ov_g = sem("ov_w"), sem("ov_x"), sem("ov_xT"), sem("ov_hg"), sem("ov_g")
        ov_t, ov_m, ov_a, ov_aT = sem("ov_t"), sem("ov_m"), sem("ov_a"), sem("ov_aT")
        ov_as, ov_y, ov_ye, ov_ys = sem("ov_as"), sem("ov_y"), sem("ov_ye"), sem("ov_ys")
        dve_chain = sem("dve_chain")
        DVE_CHAIN = 138
        fin_ready = sem("fin_ready")
        stored = sem("stored")

        w_in = a["w_in"]
        w_br = [a["w_br_na"], a["w_br_swa"], a["w_br_ret"]]

        GROUPS = [(t, kind) for t in range(TILES) for kind in range(3)]
        SCALED = (0, 1, 2, 3, 8, 9, 13, 14)
        POSITION = [0, 2, 1, 3]

        SEG = {}
        n = 0
        for name, count in (("ada0", 8), ("z", Z_CHUNKS), ("g", G_CHUNKS), ("ada2", 4), ("br", 4), ("out", 4),
                            ("ada3", 8), ("ada5", 4), ("moe", 3 * N_EXP)):
            SEG[name] = n
            n += count
        BR_EXTRA = 32
        SLOT_LAYER = SLOT_LOADS + BR_EXTRA

        def moe_seq(u):
            return 0 if u < 0 else 2 + 3 * u

        def moe_down_seq(u):
            return 3 * (u + 1) + 4

        def blocks(l, i, u):
            return l * N_EXP + i * 4 + (u + 1)

        passed = sem("passed")

        def wait_apart(eng, semaphore, value):
            eng.wait_ge(semaphore, value)
            eng.sem_inc(passed, 1)

        SPLIT = {"z": 0, "g": Z_CHUNKS, "out": Z_CHUNKS + G_CHUNKS}

        def hi_quarter(eng, l, seg, i, u, q):
            n = SPLIT[seg] + u + 1
            slot = (u + 1) % SLOTS
            if q == 0:
                eng.wait_ge(slot_loaded[slot], l * SLOT_LAYER + i * 16 + 16 * (SEG[seg] // SLOTS + (u + 1) // SLOTS + 1)
                            + (BR_EXTRA if seg == "out" else 0))
            if q == 1:
                eng.wait_ge(chunk_done, l * LAYER_CHUNKS + i * SLOTS + (SEG[seg] + SLOTS + u + 1))
            else:
                eng.wait_ge(quarter_done, l * QD + i * 12 + (3 * n + max(q - 1, 0) + 1))
            eng.activation(w_hi[:, q % 2], ring[:, slot, 2 * q:2 * q + 2, :], ACT.Copy).then_inc(whi_ready, 1)

        def lo_quarter(eng, l, seg, i, u, q):
            n = SPLIT[seg] + u + 1
            eng.wait_ge(whi_ready, l * QUARTERS + i * 16 + (4 * n + q + 1))
            eng.tensor_tensor(w_lo[:, q % 2], ring[:, (u + 1) % SLOTS, 2 * q:2 * q + 2, :], w_hi[:, q % 2].bitcast(F32),
                              ALU.subtract).then_inc(wlo_ready, 1)

        def split_segment(quarter, eng, l, seg, after, first=0):
            for q in range(first, 4):
                quarter(eng, l, seg, 0, -1, q)
            with eng.Fori(0, G_CHUNKS // SLOTS - 1) as i:
                for u in range(4):
                    for q in range(4):
                        quarter(eng, l, seg, i, u, q)
                        if q == 1:
                            after(i, u - 1)
            for u in range(3):
                for q in range(4):
                    quarter(eng, l, seg, G_CHUNKS // SLOTS - 1, u, q)
                    if q == 1:
                        after(G_CHUNKS // SLOTS - 1, u - 1)
            after(G_CHUNKS // SLOTS - 1, 2)

        INTER = {1: (3, 0), 2: (4, 1)}

        block = ctx.enter_context(nc.Block())

        @block.sync
        def _(sp):
            sp.sem_inc(chunk_done, SLOTS)
            for one in (x_ready, ada_row, zt_dve, zt_act, gb_psum, a_made, y_act, y_dve, quarter_done):
                sp.sem_inc(one, 1)
            sp.dma_start(cst[:, :], a["consts"][:, 0:C_END]).then_inc(init_loaded, 16)
            sp.dma_start(condr[:, 0, :], a["c_ctx"].rearrange("(p k) -> p k", k=KT)).then_inc(init_loaded, 16)
            sp.dma_start(condr[:, 1, :], a["c"][0].rearrange("(p k) -> p k", k=KT)).then_inc(init_loaded, 16)
            sp.dma_start(lgt[:, 0, :], a["ret_decay"].rearrange("l r h -> (l r h)").unsqueeze(0).to_broadcast([P, 16])).then_inc(init_loaded, 16)

            sp.dma_start(once, a["consts"][:, C_END:C_ALL]).then_inc(init_loaded, 16)

            def put(slot, src, l, seq):
                sp.wait_ge(chunk_done, l * LAYER_CHUNKS + (seq + 1))
                sp.dma_start(ring[:, slot] if src.shape[1] == KT else
                             ring[:, slot].rearrange("p k c -> p (k c)").rearrange("p (j n) -> p j n", n=D),
                             src).then_inc(slot_loaded[slot], 16)

            with sp.Fori(0, DEPTH) as l:
                seq = [0]

                def columns(w, first, count, rows="(p k) c -> p k c"):
                    base = seq[0]
                    with sp.Fori(0, count // SLOTS) as i:
                        for s in range(SLOTS):
                            col = sp.snap(i * (SLOTS * CH) + (first + s * CH))
                            kw = {"k": KT} if rows.startswith("(p k)") else {"p": P}
                            src = w[bass.ds(l, 1)].rearrange("a r c -> (a r) c").rearrange(rows, **kw)[:, :, bass.ds(col, CH)]
                            put(s, src, l, i * SLOTS + (base + s))
                    seq[0] += count

                columns(a["ada_w"], 0, 8)
                columns(w_in, 0, Z_CHUNKS)
                columns(w_in, Z_COLS, G_CHUNKS)
                columns(a["ada_w"], 2 * D, 4)
                for s in range(4):
                    sp.wait_ge(chunk_done, l * LAYER_CHUNKS + (seq[0] + s + 1))
                    for w, k0, kn in ((0, 0, 4), (1, 4, 2), (2, 6, 2)):
                        sp.dma_start(ring[:, s, k0:k0 + kn, :],
                                     w_br[w][bass.ds(l, 1)].rearrange("a (k p) c -> p (a k) c", p=P)[:, :, s * CH:(s + 1) * CH]
                                     ).then_inc(slot_loaded[s], 16)
                seq[0] += 4
                columns(a["w_out"], 0, 4, "(k p) c -> p k c")
                columns(a["ada_w"], 3 * D, 8)
                columns(a["ada_w"], 5 * D, 4)

                def expert(name, e, slot, i, n):
                    w = a[name].rearrange("l e r c -> (l e) r c")[bass.ds(e, 1)]
                    w = w.rearrange("a (p j) c -> p (a j) c", j=2) if name == "w_down" else \
                        w.rearrange("a (p k) c -> p (a k) c", k=KT)
                    put(slot, w, l, i * 12 + (SEG["moe"] + n))

                e = sp.snap(l * N_EXP)
                expert("w_gate", e, 0, 0, 0)
                expert("w_up", e, 1, 0, 1)

                def step(i, u):
                    n = moe_seq(u)
                    e = sp.snap(l * N_EXP + i * 4 + (u + 1))
                    expert("w_gate", e, n % SLOTS, i, n)
                    expert("w_up", e, (n + 1) % SLOTS, i, n + 1)
                    before = sp.snap(l * N_EXP + i * 4 + u)
                    expert("w_down", before, (n + 2) % SLOTS, i, n + 2)

                with sp.Fori(0, 3) as i:
                    for u in range(4):
                        step(i, u)
                for u in range(3):
                    step(3, u)
                expert("w_down", sp.snap(l * N_EXP + (N_EXP - 1)), (3 * N_EXP - 1) % SLOTS, 3, 11)
                seq[0] += 3 * N_EXP

                wait_apart(sp, routed, l + 1)
                extra = sp.value_load(extra_i[0:1, 0:1], min_val=0, max_val=EXTRA)
                with sp.If(extra > 0):
                    wait_apart(sp, chunk_done, l * LAYER_CHUNKS + (LAYER_CHUNKS + SLOTS))
                    for n in range(EXTRA):
                        owner_of = sp.value_load(extra_i[0:1, n + 1:n + 2], min_val=0, max_val=N_EXP - 1)
                        e = sp.snap(l * N_EXP + owner_of)
                        if n:
                            wait_apart(sp, ov_y, l * EXTRA + n)
                        for slot, name in enumerate(("w_gate", "w_up", "w_down")):
                            w = a[name].rearrange("l e r c -> (l e) r c")[bass.ds(e, 1)]
                            if name == "w_down":
                                sp.dma_start(ring[:, slot].rearrange("p k c -> p (k c)").rearrange("p (j n) -> p j n", n=D),
                                             w.rearrange("a (p j) c -> p (a j) c", j=2)).then_inc(ov_w, 16)
                            else:
                                sp.dma_start(ring[:, slot], w.rearrange("a (p k) c -> p (a k) c", k=KT)).then_inc(ov_w, 16)
                    wait_apart(sp, ov_y, l * EXTRA + EXTRA)
                with sp.Else():
                    sp.sem_inc(ov_w, 16 * 3 * EXTRA)
                assert seq[0] == LAYER_CHUNKS

        @block.tensor
        def _(pe):
            def loaded(seg, l, i, s, more=0):
                first = 16 * (SEG[seg] // SLOTS + 1 + more) + (BR_EXTRA if SEG[seg] >= SEG["br"] else 0)
                pe.wait_ge(slot_loaded[s], l * SLOT_LAYER + i * 16 + first)

            def columns_of_mod(l, section, which):
                pe.wait_ge(ada_row, l * ADA + 2 * section + 4 + 1)
                for sec in range(2):
                    for k in range(KT):
                        mm = pe.matmul(ps[:, 7, (sec * KT + k) * 2:(sec * KT + k) * 2 + 2],
                                       mrow[:, sec * D + k:(sec + 1) * D:KT], cst[:, C_GROUP:C_GROUP + 2],
                                       start=True, stop=True)
                mm.then_inc(mod_psum, 1)

            def broadcast_gate(l, section):
                pe.wait_ge(ada_row, l * ADA + 2 * section + 2 + 1)
                for cnd in range(2):
                    for half in range(2):
                        pe.matmul(ps[:, 4 + 2 * cnd + half, :], cst[:, C_GROUP + cnd:C_GROUP + cnd + 1].to_broadcast([P, P]),
                                  mrow[:, half * 512:(half + 1) * 512], start=True, stop=True).then_inc(gb_psum, 1)

            def norm_transposes(l, section, which):
                pe.wait_ge(xn_ready, l * XN + 3 * which + 3)
                pe.wait_ge(ada_row, l * ADA + 2 * section + 4 + 1)
                for k in range(KT):
                    if k == KT - 1:
                        columns_of_mod(l, section, which)
                        pe.wait_ge(mod_ready, l * MODR + 2 * which + 2)
                    for t in range(TILES):
                        mm = pe.transpose(ps[:, k, t * P:(t + 1) * P], xn[:, t, k:D:KT], ident)
                    mm.then_inc(xT_psum, 1)
                pe.wait_ge(hT_dve, l * HT + 8 * which + 8)
                wait_apart(pe, hT_act, l * HT + 8 * which + 8)

            pe.wait_ge(init_loaded, 16 * INIT_LOADS)
            pe.wait_ge(init_dve, 3)
            with pe.Fori(0, DEPTH) as l:
                def ada_rows(seg, count, b0=0):
                    for i in range(count):
                        for s in range(SLOTS):
                            loaded(seg, l, i, s)
                            for k in range(KT):
                                g = 32 * (k % 4)
                                mm = pe.matmul(ps[g:g + 32, b0 + 2 * i + s // 2, (s % 2) * CH:(s % 2 + 1) * CH], cond32[:, k, :],
                                               ring[:, s, k, :], start=(k < 4), stop=(k >= 4), tile_position=(0, g))
                            mm.then_inc(chunk_done, 1)

                ada_rows("ada0", 2)
                norm_transposes(l, 0, 0)
                wait_apart(pe, split_lo, l * 4 + 4)
                with pe.Fori(0, Z_CHUNKS // SLOTS) as i:
                    for s in range(SLOTS):
                        b = 3 * (s % 2)
                        if s % 2 == 0:
                            pe.wait_ge(zt_dve, l * ZD + i * 2 + s // 2 + 1)
                        else:
                            pe.wait_ge(zt_act, l * ZD + i * 2 + s // 2 + 1)
                        for q in range(4):
                            pe.wait_ge(wlo_ready, l * QUARTERS + i * 16 + (4 * s + q + 1))
                            for t in range(TILES):
                                for k in range(2 * q, 2 * q + 2):
                                    for n, (hx, wx) in enumerate(((h_hi, w_hi), (h_hi, w_lo), (h_lo, w_hi))):
                                        mm = pe.matmul(ps[:, b + t, 0:CH], hx[:, k, t * P:(t + 1) * P], wx[:, q % 2, k % 2, :],
                                                       start=(k == 0 and n == 0), stop=(k == KT - 1 and n == 2))
                            mm.then_inc(quarter_done if q < 3 else chunk_done, 1)

                pe.wait_ge(zt_dve, l * ZD + ZD + 1)
                pe.wait_ge(zt_act, l * ZD + ZD + 1)
                pe.wait_ge(small_loaded, l * SMALL_L + SMALL_L)
                for h in range(HEADS_NA):
                    pe.matmul(ps[:, h, 0:384], cst[:, C_TURN:C_TURN + P], bias_turned[:, h, :],
                              start=True, stop=True).then_inc(bias_psum, 1)

                pe.wait_ge(bias_ready, l * BIAS_L + BIAS_L)
                for u in range(TP):
                    if u == 10:
                        pe.wait_ge(rot_dve, l * RD + RD)
                        pe.wait_ge(rot_act, l * 2 + 2)
                    if u >= 8:
                        pe.wait_ge(*((t_dve, l * TD + ((u - 8) // 2 + 1)) if u % 2 == 0 else
                                     (t_act, l * TA + ((u - 8) // 2 + 1))))
                    b = u % 8
                    if u == 8:
                        for j in range(4):
                            mm = pe.transpose(ps[:, b, j * P:(j + 1) * P],
                                              cache_k[:, 2 * j:2 * j + 2, :].rearrange("p h d -> p (h d)"), ident)
                    elif u == 9:
                        mm = pe.transpose(ps[:, b, 0:P], cache_k[:, 8:10, :].rearrange("p h d -> p (h d)"), ident)
                    else:
                        v = u if u < 8 else u - 2
                        for t in range(TILES):
                            if v < 8:
                                src = zt[:, t, QA + v * P:QA + (v + 1) * P]
                            elif v < 11:
                                src = rot[:, t, (v - 8) * P:(v - 7) * P]
                            else:
                                src = zt[:, t, QR + (v - 11) * P:QR + (v - 10) * P]
                            mm = pe.transpose(ps[:, b, t * P:(t + 1) * P], src, ident)
                    mm.then_inc(t_psum, 1)

                pe.wait_ge(t_dve, l * TD + TD)
                pe.wait_ge(t_act, l * TA + TA)

                def heads_of(g):
                    t, kind = GROUPS[g]
                    for j in range(4):
                        if kind < 2:
                            h = 4 * kind + j
                            hp, qb, kb, cb = HD * (h % 2), h // 2, 4 + h // 2, h // 2
                            v0, vc = VA + h * HD, h
                        else:
                            pos = POSITION[j]
                            hp, qb, kb, cb = HD * (pos % 2), 8 + pos // 2, 10, 4
                            v0, vc = VS + (j // 2) * HD, 8 + j // 2
                        yield t, j, hp, qb, kb, cb, v0, vc

                def scores(g):
                    t, kind = GROUPS[g]
                    heads = list(heads_of(g))
                    order = (0, 2, 1, 3) if kind == 2 else (0, 1, 2, 3)

                    def product(j, keys, at, n):
                        _, _, hp, qb, kb, cb, _, _ = heads[j]
                        k = kcT[hp:hp + HD, cb, :] if keys == "context" else qkT[hp:hp + HD, kb, (0 if t == 0 else P):(P if t == 0 else TOK)]
                        return pe.matmul(ps[:, j, at:at + n], qkT[hp:hp + HD, qb, t * P:(t + 1) * P], k, start=True, stop=True)

                    if g >= 1:
                        pe.wait_ge(s_ready, l * SU + 4 * g)
                    if t == 0:
                        for j in order:
                            product(j, "own", 0, P).then_inc(s_psum, 1)
                    else:
                        loc, c0 = (0, 256) if t == 1 else (P, 0)
                        for pair in (order[:2], order[2:]):
                            for j in pair:
                                product(j, "own", loc, 256)
                            for j in pair:
                                product(j, "context", c0, P).then_inc(s_psum, 1)

                def prob_transposes(g, j):
                    t = GROUPS[g][0]
                    u = 4 * g + j
                    pe.wait_ge(exp_ready, l * SU + (u + 1))
                    if u >= 2:
                        pe.wait_ge(pT_ready, l * SU + (u - 1))
                    for c in range(1 if t == 0 else 3):
                        mm = pe.transpose(ps[:, 4 + u % 2, c * P:(c + 1) * P], sbuf_s[:, g % 2, j, c * P:(c + 1) * P], ident)
                    mm.then_inc(pt_psum, 1)

                def values(g, jj):
                    for t, j, hp, qb, kb, cb, v0, vc in heads_of(g):
                        if j != jj:
                            continue
                        u = 4 * g + j
                        if j == 0 and g >= 2:
                            pe.wait_ge(o_ready, l * NG + (g - 1))
                        pe.wait_ge(pT_ready, l * SU + (u + 1))
                        new = [zt[:, tt, v0:v0 + HD] for tt in (1, 2)]
                        old = cache_v[:, vc, :]
                        vs = {0: [zt[:, 0, v0:v0 + HD]], 1: new + [old], 2: [old] + new}[t]
                        for c, v in enumerate(vs):
                            mm = pe.matmul(ps[:, 6 + g % 2, j * HD:(j + 1) * HD], pT[:, u % 2, c * P:(c + 1) * P], v,
                                           start=(c == 0), stop=(c == len(vs) - 1))
                        mm.then_inc(pv_done, 1)

                scores(0)
                for g in range(NG):
                    if g + 1 < NG:
                        scores(g + 1)
                    prob_transposes(g, 0)
                    for j in range(4):
                        if j < 3:
                            prob_transposes(g, j + 1)
                        values(g, j)

                pe.wait_ge(o_ready, l * NG + NG)
                pe.wait_ge(kd_ready, l * 4 + 4)
                for i, t in enumerate((0, 0, 1, 2)):
                    for hb in range(2):
                        mm = pe.matmul(ps[:, i // 2, ((i % 2) * 2 + hb) * P:((i % 2) * 2 + hb + 1) * P],
                                       kd[:, i, hb * P:(hb + 1) * P], zt[:, t, VR + hb * P:VR + (hb + 1) * P],
                                       start=True, stop=True)
                    if i % 2:
                        mm.then_inc(kv_psum, 1)
                for t in range(TILES):
                    for h in range(4):
                        hp = HD * (h % 2)
                        mm = pe.matmul(ps[:, (2, 5)[h % 2] + t, (h // 2) * P:(h // 2 + 1) * P], qkT[hp:hp + HD, 13 + h // 2, t * P:(t + 1) * P],
                                       qkT[hp:hp + HD, 11 + h // 2, t * P:(t + 1) * P], start=True, stop=True)
                    mm.then_inc(a_psum, 1)
                for t in range(TILES):
                    pe.wait_ge(am_ready, l * 3 + (t + 1))
                    if t == 1:
                        pe.wait_ge(state_ready, l * 10 + 10)
                    for h in range(4):
                        mm = pe.matmul(ps[:, 5 + t, h * HD:(h + 1) * HD], am[:, t, h * P:(h + 1) * P],
                                       zt[:, t, VR + h * HD:VR + (h + 1) * HD], start=True, stop=True)
                    if t:
                        for d in range(2):
                            st = state0 if (t == 1) == (d == 0) else state1
                            for h in range(4):
                                hp = HD * (h % 2)
                                o = (2 * d + h // 2) * HD
                                mm = pe.matmul(ps[:, INTER[t][h % 2], o:o + HD], qkT[hp:hp + HD, 11 + h // 2, t * P:(t + 1) * P],
                                               st[hp:hp + HD, d, h // 2, :], start=True, stop=True)
                    mm.then_inc(ro_psum, 1)

                wait_apart(pe, ret_read, l + 1)
                with pe.Fori(0, G_CHUNKS // SLOTS) as i:
                    for s in range(SLOTS):
                        for j in range(2):
                            pe.wait_ge(gate_ready, l * GT + i * 8 + (2 * s + j + 1))
                        for q in range(4):
                            pe.wait_ge(wlo_ready, l * QUARTERS + i * 16 + (4 * (Z_CHUNKS + s) + q + 1))
                            for j in range(2):
                                for k in range(2 * q, 2 * q + 2):
                                    for n, (hx, wx) in enumerate(((h_hi, w_hi), (h_lo, w_hi), (h_hi, w_lo))):
                                        mm = pe.matmul(ps[:, 2 * s + j, 0:TOK], wx[:, q % 2, k % 2, j * P:(j + 1) * P], hx[:, k, :],
                                                       start=(k == 0 and n == 0), stop=(k == KT - 1 and n == 2))
                            mm.then_inc(quarter_done if q < 3 else chunk_done, 1)

                pe.wait_ge(gate_ready, l * GT + GT + 8)
                pe.wait_ge(ro_ready, l * 1 + 1)
                for j in range(KT):
                    c0 = (QA + j * P) if j < 4 else (QS + (j - 4) * P) if j < 6 else QR + (j - 6) * P
                    for t in range(TILES):
                        mm = pe.transpose(ps[:, j, t * P:(t + 1) * P], zt[:, t, c0:c0 + P], ident)
                    mm.then_inc(ot_psum, 1)

                pe.wait_ge(ot_dve, l * 4 + 4)
                pe.wait_ge(ot_act, l * 4 + 4)
                ada_rows("ada2", 1)
                broadcast_gate(l, 2)

                for j in range(KT):
                    s = j // 2
                    b = 3 * (j % 2)
                    if j % 2 == 0:
                        first = 16 * (SEG["br"] // SLOTS) + 48
                        pe.wait_ge(slot_loaded[s], l * SLOT_LAYER + first)
                    if j == 0:
                        pe.wait_ge(gb_ready, l * GB + 4)
                    if j >= 2:
                        pe.wait_ge(br_read, l * 8 + (j - 1))
                    for n_, (k0, kn) in enumerate(((0, 4), (4, 2), (6, 2))):
                        for k in range(k0, k0 + kn):
                            mm = pe.matmul(ps[:, b + n_, 0:TOK], ring[:, s, k, (j % 2) * P:(j % 2 + 1) * P], oT[:, k, :],
                                           start=(k == k0), stop=(k == k0 + kn - 1))
                    mm.then_inc(br_psum if j % 2 == 0 else chunk_done, 1)

                pe.wait_ge(br_read, l * 8 + 8)
                pe.wait_ge(z_lo, l * 8 + 8)
                for s in range(4):
                    if s >= 2:
                        pe.wait_ge(out_read, l * 4 + (s - 1))
                    for q in range(4):
                        pe.wait_ge(wlo_ready, l * QUARTERS + 4 * (SPLIT["out"] + s) + q + 1)
                        for t in range(TILES):
                            for k in range(2 * q, 2 * q + 2):
                                for n, (zx, wx) in enumerate(((h_hi, w_hi), (h_hi, w_lo), (h_lo, w_hi))):
                                    mm = pe.matmul(ps[:, 3 * (s % 2) + t, 0:CH], zx[:, k, t * P:(t + 1) * P], wx[:, q % 2, k % 2, :],
                                                   start=(k == 0 and n == 0), stop=(k == KT - 1 and n == 2))
                        mm.then_inc(quarter_done if q < 3 else chunk_done, 1)

                pe.wait_ge(out_read, l * 4 + 4)
                ada_rows("ada3", 2)
                norm_transposes(l, 3, 1)

                for k in range(KT):
                    mm = pe.matmul(ps[0:20, 0, 0:TOK], rw[:, k, :], hT[:, k, :], start=(k == 0), stop=(k == KT - 1))
                mm.then_inc(loT_psum, 1)
                for t in range(TILES):
                    for k in range(KT):
                        mm = pe.transpose(ps[:, 2 + 2 * t + k // 4, (k % 4) * P:(k % 4 + 1) * P], hT[:, k, t * P:(t + 1) * P], ident)
                    mm.then_inc(h2_psum, 1)
                    if t == 0:
                        wait_apart(pe, loT_ready, l + 1)
                        for tt in range(TILES):
                            mm = pe.transpose(ps[:, 1, tt * 20:(tt + 1) * 20], loT[:, tt * P:(tt + 1) * P],
                                              cst[0:20, C_IDENT:C_IDENT + 20])
                        mm.then_inc(lo_psum, 1)
                ones = cst[:, C_ONE:C_ONE + 1].to_broadcast([P, P])
                pe.wait_ge(hot_ready, l * 1 + 1)
                for t in range(TILES):
                    for before in range(t):
                        pe.matmul(ps[:, 0, 64 + 16 * t:80 + 16 * t], ones, hotsum[:, before, :], start=(before == 0), stop=False)
                    pe.matmul(ps[:, 0, 64 + 16 * t:80 + 16 * t], cst[:, C_BEFORE:C_BEFORE + P], hotsum[:, t, :],
                              start=(t == 0), stop=True)
                for t in range(TILES):
                    mm = pe.matmul(ps[:, 0, 112:128], ones, hotsum[:, t, :], start=(t == 0), stop=(t == TILES - 1))
                mm.then_inc(rank_psum, 1)

                pe.wait_ge(h2_ready, l * TILES + TILES)
                ada_rows("ada5", 1, 2)

                wait_apart(pe, places_ready, l * 12 + 12)
                for k in range(2):
                    for t in range(TILES):
                        mm = pe.matmul(ps[:, 0, 128:150], at_lane[:, k, t, :], at_block[:, k, t, :],
                                       start=(k == 0 and t == 0), stop=(k == 1 and t == TILES - 1))
                mm.then_inc(token_psum, 1)

                broadcast_gate(l, 5)

                def inputs_turned(i, u):
                    buf = (u + 1) % 4
                    pe.wait_ge(xg_loaded[buf], l * 64 + i * 16 + 16 * ((u + 1) // 4 + 1))
                    if u >= 0:
                        pe.wait_ge(hg_act, blocks(l, i, u))
                        pe.wait_ge(hg_dve, blocks(l, i, u))
                    for k in range(KT):
                        mm = pe.transpose(ps[:, k // 4, (k % 4) * P:(k % 4 + 1) * P], xg[:, buf, k * P:(k + 1) * P], ident)
                    mm.then_inc(xgT_psum, 1)

                def gate_up(i, u):
                    par = (u + 1) % 2
                    pe.wait_ge(hg_act, blocks(l, i, u) + 1)
                    pe.wait_ge(hg_dve, blocks(l, i, u) + 1)
                    if u >= 0:
                        pe.wait_ge(a_made, blocks(l, i, u))
                    for w in range(2):
                        n = moe_seq(u) + w
                        loaded("moe", l, i * 3, n % SLOTS, n // SLOTS)
                        for k in range(KT):
                            mm = pe.matmul(ps[:, 2 + par, w * CH:(w + 1) * CH], hgT[:, par, k, :], ring[:, n % SLOTS, k, :],
                                           start=(k == 0), stop=(k == KT - 1))
                        mm.then_inc(chunk_done, 1)

                def activations_turned(i, u):
                    pe.wait_ge(a_made, blocks(l, i, u) + 2)
                    for j in range(2):
                        mm = pe.transpose(ps[:, 4, j * P:(j + 1) * P], act_a[:, (u + 1) % 2, j:CH:2], ident)
                    mm.then_inc(aT_psum, 1)

                def down(i, u, last=False):
                    pe.wait_ge(aTs_ready, blocks(l, i, u) + 1)
                    pe.wait_ge(y_act, blocks(l, i, u) + 1)
                    pe.wait_ge(y_dve, blocks(l, i, u) + 1)
                    n = 11 if last else moe_down_seq(u)
                    loaded("moe", l, i * 3, n % SLOTS, n // SLOTS)
                    w = ring[:, n % SLOTS].rearrange("p k c -> p (k c)").rearrange("p (j n) -> p j n", n=D)
                    for half in range(2):
                        for j in range(2):
                            mm = pe.matmul(ps[:, 5 + half, :], aTs[:, (u + 1) % 2, j, :], w[:, j, half * 512:(half + 1) * 512],
                                           start=(j == 0), stop=(j == 1))
                        mm.then_inc(y_psum if half == 0 else chunk_done, 1)

                pe.wait_ge(ada_row, l * ADA + ADA + 1)
                pe.wait_ge(gb_ready, l * GB + GB)
                inputs_turned(0, -1)
                gate_up(0, -1)
                inputs_turned(0, 0)
                with pe.Fori(0, 3) as i:
                    for u in range(4):
                        gate_up(i, u)
                        activations_turned(i, u - 1)
                        inputs_turned(i, u + 1)
                        down(i, u - 1)
                for u in range(3):
                    gate_up(3, u)
                    activations_turned(3, u - 1)
                    if u < 2:
                        inputs_turned(3, u + 1)
                    down(3, u - 1)
                activations_turned(3, 2)
                down(3, 2, last=True)

                pe.wait_ge(y_act, l * N_EXP + N_EXP + 1)
                pe.wait_ge(y_dve, l * N_EXP + N_EXP + 1)
                wait_apart(pe, routed, l + 1)
                extra = pe.value_load(extra_i[0:1, 0:1], min_val=0, max_val=EXTRA)
                with pe.If(extra > 0):
                    with pe.Fori(0, EXTRA) as n:
                        pe.wait_ge(ov_x, l * (16 * EXTRA) + n * 16 + 16)
                        for k in range(KT):
                            mm = pe.transpose(ps[:, k // 4, (k % 4) * P:(k % 4 + 1) * P], xg[:, 0, k * P:(k + 1) * P], ident)
                        mm.then_inc(ov_xT, 1)
                        pe.wait_ge(ov_w, l * (48 * EXTRA) + n * 48 + 48)
                        pe.wait_ge(ov_hg, l * EXTRA + n + 1)
                        for w in range(2):
                            for k in range(KT):
                                mm = pe.matmul(ps[:, 2, w * CH:(w + 1) * CH], hgT[:, 0, k, :], ring[:, w, k, :],
                                               start=(k == 0), stop=(k == KT - 1))
                        mm.then_inc(ov_g, 1)
                        pe.wait_ge(ov_a, l * EXTRA + n + 1)
                        for j in range(2):
                            mm = pe.transpose(ps[:, 4, j * P:(j + 1) * P], act_a[:, 0, j:CH:2], ident)
                        mm.then_inc(ov_aT, 1)
                        pe.wait_ge(ov_as, l * EXTRA + n + 1)
                        w = ring[:, 2].rearrange("p k c -> p (k c)").rearrange("p (j n) -> p j n", n=D)
                        for half in range(2):
                            for j in range(2):
                                mm = pe.matmul(ps[:, 5 + half, :], aTs[:, 0, j, :], w[:, j, half * 512:(half + 1) * 512],
                                               start=(j == 0), stop=(j == 1))
                        mm.then_inc(ov_y, 1)
                        pe.wait_ge(ov_ye, l * EXTRA + n + 1)
                with pe.Else():
                    for one in (ov_xT, ov_g, ov_aT, ov_y):
                        pe.sem_inc(one, EXTRA)

        @block.vector
        def _(dve):
            count = [0]

            def link(ins):
                count[0] += 1
                ins.then_inc(dve_chain, 1)

            def linked(l):
                dve.wait_ge(dve_chain, l * DVE_CHAIN + count[0])

            def bcast(ap, shape, axis):
                return ap.unsqueeze(axis).to_broadcast(shape)

            dve.wait_ge(init_loaded, 16 * INIT_LOADS)
            dve.memset(mhalf[:, :], -0.5)
            dve.memset(zero1[:, :], 0.0)
            dve.memset(cond32[:, :, 2:32], 0.0)
            dve.scalar_tensor_tensor(out=lgt[:, 1, :], in0=lgt[:, 0, :], scalar=-1.0, in1=lgt[:, 0, :],
                                     op0=ALU.mult, op1=ALU.max).then_inc(init_dve, 1)
            dve.wait_ge(act_init, 1)
            dve.scalar_tensor_tensor(out=cond[:, :, :].rearrange("p k c -> p c k"), in0=condt[:, :, :], scalar=1.0, in1=condr[:, :, :],
                                     op0=ALU.add, op1=ALU.mult).then_inc(init_dve, 1)
            dve.wait_ge(init_dve, 2)
            dve.tensor_scalar(cond32[:, :, 0:2], cond[:, :, :], 0.5, None, ALU.mult).then_inc(init_dve, 1)
            dve.wait_ge(act_init, 3)
            dve.scalar_tensor_tensor(out=lg[:, :], in0=lgt[:, 0, :], scalar=0.0, in1=lgt[:, 3, :],
                                     op0=ALU.min, op1=ALU.subtract).then_inc(init_dve, 1)
            dve.wait_ge(init_dve, 4)
            lgv = lg[:, :].rearrange("p (l r h) -> p l r h", l=DEPTH, r=2)
            for d in range(2):
                dve.tensor_scalar(qdec[:, :, d, :], lgv[:, :, d, :], cst[:, C_POS + d:C_POS + d + 1], None,
                                  ALU.mult).then_inc(init_dve, 1)
                dve.tensor_scalar(kdec[:, :, d, :], lgv[:, :, d, :], cst[:, C_POS + 2 + d:C_POS + 3 + d], None,
                                  ALU.mult).then_inc(init_dve, 1)
                rows = slice(d * HD, (d + 1) * HD)
                dve.tensor_scalar(cdl[rows, :, :, :], lgv[rows, :, :, d:4:2], float(P), None,
                                  ALU.mult).then_inc(init_dve, 1)
            dve.wait_ge(act_init, 22)
            dve.tensor_scalar(kdec[:, :, :, :], kdec[:, :, :, :], HD ** -0.5, None, ALU.mult).then_inc(init_dve, 1)
            decv = dec[:, :, :, :].rearrange("p l h q -> p (l h) q")
            back = work[:, 0:1024].rearrange("p (n q) -> p n q", q=P)
            dve.tensor_tensor(decv, decv, bcast(once[:, 0:128], [P, 8, P], 1), ALU.mult).then_inc(init_dve, 1)
            dve.tensor_tensor(back, back, bcast(once[:, 128:256], [P, 8, P], 1), ALU.mult).then_inc(init_dve, 1)
            dve.wait_ge(init_dve, 13)
            dve.tensor_tensor(decv, decv, back, ALU.add).then_inc(init_dve, 1)
            dve.wait_ge(init_dve, 14)

            with dve.Fori(0, DEPTH) as l:
                def done(seg, n):
                    dve.wait_ge(chunk_done, l * LAYER_CHUNKS + (SEG[seg] + SLOTS) + n)

                def ada_rows(seg, count, b0=0):
                    for n in range(2 * count):
                        done(seg, 2 * (n + 1))
                        dve.tensor_copy(mrow[:, n * 512:(n + 1) * 512], ps[:, b0 + n, :]).then_inc(ada_row, 1)

                def gate_rows(which):
                    dve.wait_ge(adab_loaded, l * 64 + 32 * (which + 1))
                    for n in range(4):
                        dve.wait_ge(gb_psum, l * GB + 4 * which + n + 1 + 1)
                        row = gb[:, n // 2, (n % 2) * 512:(n % 2 + 1) * 512]
                        dve.tensor_tensor(row, row, ps[:, 4 + n, :], ALU.add).then_inc(gb_ready, 1)

                def modulation_columns(which):
                    dve.wait_ge(mod_psum, l * MODP + which + 1)
                    dve.wait_ge(gains_loaded, l * 64 + 64)
                    v = ps[:, 7, 0:32].rearrange("p (s k c) -> p s k c", s=2, c=2)
                    link(dve.tensor_tensor(scale[:, :, :], v[:, 1], bcast(modb[:, 2 * which + 1, :], [P, KT, 2], 2), ALU.add))
                    dve.tensor_tensor(shift[:, :, :], v[:, 0], bcast(modb[:, 2 * which, :], [P, KT, 2], 2),
                                      ALU.add).then_inc(mod_ready, 1)
                    linked(l)
                    dve.scalar_tensor_tensor(out=scale[:, :, :], in0=scale[:, :, :], scalar=1.0,
                                             in1=bcast(gain[:, which, :], [P, KT, 2], 2),
                                             op0=ALU.add, op1=ALU.mult).then_inc(mod_ready, 1)

                def norm(which):
                    dve.wait_ge(rstd_ready, l * RS + which + 1)
                    for t in range(TILES):
                        dve.tensor_scalar(xn[:, t, :], x[:, t, :], rstd[:, t:t + 1], None, ALU.mult).then_inc(xn_ready, 1)
                    ada_rows("ada3" if which else "ada0", 2)
                    modulation_columns(which)
                    dve.wait_ge(mod_ready, l * MODR + 2 * which + 2)
                    for k in range(0, KT, 2):
                        dve.wait_ge(xT_psum, l * XT + 8 * which + k + 1)
                        for c, (n0, n1) in enumerate(((0, P), (P, TOK))):
                            dve.tensor_scalar(hT[:, k, n0:n1], ps[:, k, n0:n1], scale[:, k, c:c + 1], shift[:, k, c:c + 1],
                                              ALU.mult, ALU.add).then_inc(hT_dve, 1)

                norm(0)

                for r in range(4):
                    dve.wait_ge(split_hi, l * 4 + r + 1)
                    dve.tensor_tensor(h_lo[:, 2 * r:2 * r + 2, :], hT[:, 2 * r:2 * r + 2, :],
                                      h_hi[:, 2 * r:2 * r + 2, :].bitcast(F32), ALU.subtract).then_inc(split_lo, 1)

                def even_products(i, u):
                    if (u + 1) % 2 == 0:
                        done("z", i * SLOTS + (u + 2))
                        dve.tensor_copy(zt[:, :, bass.ds(i * (SLOTS * CH) + (u + 1) * CH, CH)],
                                        ps[:, 0:3, 0:CH]).then_inc(zt_dve, 1)

                split_segment(lo_quarter, dve, l, "z", even_products)
                for q in range(2):
                    lo_quarter(dve, l, "g", 0, -1, q)

                for h in range(HEADS_NA):
                    dve.wait_ge(bias_psum, l * HEADS_NA + h + 1)
                    dve.tensor_tensor(biasT[:, h * BIAS_W + P:(h + 1) * BIAS_W].rearrange("p (s c) -> p s c", s=6),
                                      ps[:, h, 0:384].rearrange("p (s c) -> p s c", s=6),
                                      bcast(cst[:, C_COLMASK:C_COLMASK + GRID_W], [P, 6, GRID_W], 1),
                                      ALU.add).then_inc(bias_ready, 1)

                dve.wait_ge(zt_dve, l * ZD + ZD + 1)
                dve.wait_ge(zt_act, l * ZD + ZD + 1)
                for n, (odd, tab) in enumerate(((0, C_COS), (1, C_SIN), (0, C_SIN), (1, C_COS))):
                    src = zt[:, 1:3, QS + odd:QS + 384:2].rearrange("p t (h i) -> p t h i", i=32)
                    tabs = bcast(cst[:, tab:tab + 64].rearrange("p (t i) -> p t i", t=2), [P, 2, 6, 32], 2)
                    link(dve.tensor_tensor(rprod[:, n], src, tabs, ALU.mult))
                linked(l)
                for odd in range(2):
                    op = ALU.add if odd else ALU.subtract
                    for t in range(2):
                        o = rot[:, 1 + t, odd:256:2].rearrange("p (ha hb i) -> p hb ha i", ha=2, hb=2)
                        i0, i1 = (rprod[:, 2 * odd + m, t, 0:4, :].rearrange("p (hb ha) i -> p hb ha i", ha=2) for m in range(2))
                        dve.tensor_tensor(o, i0, i1, op).then_inc(rot_dve, 1)
                    dve.tensor_tensor(rot[:, 1:3, 256 + odd:384:2].rearrange("p t (h i) -> p t h i", i=32),
                                      rprod[:, 2 * odd, :, 4:6, :], rprod[:, 2 * odd + 1, :, 4:6, :], op).then_inc(rot_dve, 1)

                for u in range(0, TP, 2):
                    dve.wait_ge(t_psum, l * TP + u + 1)
                    if u == 8:
                        dve.tensor_copy(kcT[:, 0:4, :].rearrange("p b n -> p (b n)"), ps[:, 0, :]).then_inc(t_dve, 1)
                        continue
                    v = u if u < 8 else u - 2
                    dve.tensor_scalar(qkT[:, v, :], ps[:, u % 8, 0:TOK], HD ** -0.5 if v in SCALED else 1.0, None,
                                      ALU.mult).then_inc(t_dve, 1)

                dve.wait_ge(bias_ready, l * BIAS_L + BIAS_L)
                dve.wait_ge(small_loaded, l * SMALL_L + SMALL_L)

                def maxima(g):
                    t, kind = GROUPS[g]
                    if g >= 2:
                        dve.wait_ge(pt_psum, l * SU + 4 * (g - 1))
                    for j in range(4):
                        wait_apart(dve, s_psum, l * SU + 4 * g + ((0, 2, 3, 3)[j] if kind == 2 else j) + 1)
                        w = P if t == 0 else 384
                        h = 4 * kind + j if kind < 2 else 0
                        if kind == 2 and t:
                            add = cst[:, C_SWAMASK + 384 * (t - 1):C_SWAMASK + 384 * t]
                        else:
                            b0 = h * BIAS_W + (0, 256, 0)[t]
                            add = biasT[:, b0:b0 + w]
                        dve.tensor_tensor_reduce(sbuf_s[:, g % 2, j, 0:w], ps[:, (4 * g + j) % 4, 0:w], add, 1.0, NEG,
                                                 ALU.add, ALU.max, mx[:, g % 2, j:j + 1]).then_inc(s_ready, 1)
                    dve.wait_ge(s_ready, l * SU + 4 * g + 4)
                    if kind == 2:
                        link(dve.tensor_tensor(mx[:, g % 2, :], mx[:, g % 2, :], sink[:, :], ALU.max))
                        linked(l)
                        link(dve.tensor_scalar(nmx[:, g % 2, :], mx[:, g % 2, :], -1.0, None, ALU.mult))
                        linked(l)
                        dve.tensor_tensor(sk[:, g % 2, :], sink[:, :], nmx[:, g % 2, :], ALU.add).then_inc(nmax_ready, 1)
                    else:
                        dve.tensor_scalar(nmx[:, g % 2, :], mx[:, g % 2, :], -1.0, None, ALU.mult).then_inc(nmax_ready, 1)

                def normalise(g):
                    t, kind = GROUPS[g]
                    dve.wait_ge(exp_ready, l * SU + 4 * g + 4)
                    if kind == 2:
                        dve.wait_ge(sink_exp, l * 3 + t + 1)
                        link(dve.tensor_tensor(den[:, g % 2, :], den[:, g % 2, :], sk[:, g % 2, :], ALU.add))
                        linked(l)
                    link(dve.reciprocal(rden[:, g % 2, :], den[:, g % 2, :]))
                    linked(l)
                    dve.wait_ge(pv_done, l * SU + 4 * g + 4)
                    o0 = QA + 256 * kind if kind < 2 else QS
                    dve.tensor_tensor(zt[:, t, o0:o0 + 256].rearrange("p (h d) -> p h d", d=HD),
                                      ps[:, 6 + g % 2, 0:256].rearrange("p (h d) -> p h d", d=HD),
                                      bcast(rden[:, g % 2, :], [P, 4, HD], 2), ALU.mult).then_inc(o_ready, 1)

                maxima(0)
                for g in range(NG):
                    if g + 1 < NG:
                        maxima(g + 1)
                    normalise(g)

                def diagonal(bank, i, par):
                    v = ps[par * HD:(par + 1) * HD, bank, :].rearrange("p (i b e) -> p i b e", i=2, b=2)
                    return v[:, i, :, par * HD:(par + 1) * HD]

                dve.wait_ge(kv_psum, l * 2 + 1)
                for par in range(2):
                    rows = slice(par * HD, (par + 1) * HD)
                    v = ps[rows, 0, :].rearrange("p (i b e) -> p i b e", i=2, b=2)
                    dve.tensor_copy(state_out[rows, :, :, :], v[:, :, :, par * HD:(par + 1) * HD]).then_inc(state_ready, 1)
                dve.wait_ge(kv_psum, l * 2 + 2)
                for d in range(2):
                    for par in range(2):
                        rows = slice(par * HD, (par + 1) * HD)
                        for hb in range(2):
                            dve.scalar_tensor_tensor(
                                out=state1[rows, d, hb, :], in0=state0[rows, d, hb, :],
                                scalar=cdec[rows, :, :, :].rearrange("p l r b -> p (l r b)")[:, bass.ds(l * 4 + (2 * d + hb), 1)],
                                in1=diagonal(1, d, par)[:, hb, :], op0=ALU.mult, op1=ALU.add).then_inc(state_ready, 1)
                def by_parity(ap, n):
                    return ap.rearrange("p (b r n) -> p r b n", b=2, n=n)

                decl = dec[:, :, :, :].rearrange("p l h q -> p (l h q)")[:, bass.ds(l * 512, 512)]
                for t in range(TILES):
                    dve.wait_ge(a_psum, l * 3 + t + 1)
                    for par in range(2):
                        ins = dve.tensor_tensor(by_parity(am[:, t, :], P)[:, par],
                                                ps[:, (2, 5)[par] + t, 0:256].rearrange("p (b q) -> p b q", b=2),
                                                by_parity(decl, P)[:, par], ALU.mult)
                        if par == 0:
                            link(ins)
                    ins.then_inc(am_ready, 1)

                def head_view(ap):
                    return ap.rearrange("p (h d) -> p h d", d=HD)

                for t in range(TILES):
                    dve.wait_ge(ro_psum, l * 3 + t + 1)
                    ot = ret_o[:, t * 256:(t + 1) * 256]
                    if t == 0:
                        link(dve.tensor_copy(ot, ps[:, 5, 0:256]))
                        continue
                    u, w = ret_u[:, t * 256:(t + 1) * 256], ret_w[:, (t - 1) * 256:t * 256]
                    for d, dst in ((0, u), (1, w)):
                        qd = by_parity(qdec[:, :, :, :].rearrange("p l r h -> p (l r h)")[:, bass.ds(l * 8 + 4 * d, 4)], 1)
                        for par in range(2):
                            link(dve.tensor_tensor(by_parity(dst, HD)[:, par],
                                                   ps[:, INTER[t][par], 128 * d:128 * d + 128].rearrange("p (b n) -> p b n", b=2),
                                                   qd[:, par].to_broadcast([P, 2, HD]), ALU.mult))
                    linked(l)
                    link(dve.tensor_tensor(u, u, w, ALU.add))
                    linked(l)
                    ins = dve.tensor_tensor(ot, ps[:, 5 + t, 0:256], u, ALU.add)
                    if t < TILES - 1:
                        link(ins)
                    else:
                        ins.then_inc(ret_read, 1)
                lo_quarter(dve, l, "g", 0, -1, 2)
                linked(l)
                dve.wait_ge(ret_read, l + 1)
                link(dve.tensor_tensor(ret_u, ret_o, ret_o, ALU.mult))
                linked(l)
                dve.tensor_reduce(ssq12[:, :], head_view(ret_u), AX_X, ALU.add).then_inc(ret_ssq, 1)
                lo_quarter(dve, l, "g", 0, -1, 3)
                dve.wait_ge(rsq_ready, l * 1 + 1)
                link(dve.tensor_tensor(head_view(ret_o), head_view(ret_o), bcast(rstd12[:, :], [P, 12, HD], 2), ALU.mult))
                dve.wait_ge(tgr_ready, l * 1 + 1)
                dve.wait_ge(ret_ssq, l * 1 + 1)
                link(dve.scalar_tensor_tensor(out=ret_u.rearrange("p (t c) -> p t c", t=TILES), in0=tgr, scalar=1.0,
                                              in1=zt[:, :, GR:GR + 256], op0=ALU.add, op1=ALU.mult))
                linked(l)
                ro3 = ret_o.rearrange("p (t c) -> p t c", t=TILES)
                link(dve.tensor_tensor(ro3, ro3, bcast(ret_g, [P, TILES, 256], 1), ALU.mult))
                linked(l)
                dve.scalar_tensor_tensor(out=zt[:, :, QR:QR + 256], in0=ro3, scalar=0.5,
                                         in1=ret_u.rearrange("p (t c) -> p t c", t=TILES),
                                         op0=ALU.mult, op1=ALU.mult).then_inc(ro_ready, 1)

                split_segment(lo_quarter, dve, l, "g", lambda i, u: None, first=4)

                for j in range(0, KT, 2):
                    dve.wait_ge(ot_psum, l * KT + j + 1)
                    dve.tensor_copy(oT[:, j, :], ps[:, j, 0:TOK]).then_inc(ot_dve, 1)

                ada_rows("ada2", 1)
                gate_rows(0)

                dve.wait_ge(gate_ready, l * GT + GT + 8)
                dve.wait_ge(kv_stored, l * KV_L + KV_L)
                def z_rest(j):
                    dve.wait_ge(z_hi, l * 8 + j + 1)
                    dve.tensor_tensor(h_lo[:, j, :], zT[:, j, :], h_hi[:, j, :].bitcast(F32), ALU.subtract).then_inc(z_lo, 1)

                for j in range(KT):
                    if j % 2 == 0:
                        dve.wait_ge(br_psum, l * 4 + j // 2 + 1)
                    else:
                        done("br", j // 2 + 1)
                    b = 3 * (j % 2)
                    dsts = (zT[:, j, :], br_u, br_w)
                    for n in range(3):
                        ins = dve.scalar_tensor_tensor(out=dsts[n], in0=gate_tile(n * KT + j), scalar=1.0,
                                                       in1=ps[:, b + n, 0:TOK], op0=ALU.add, op1=ALU.mult)
                        if n < 2:
                            link(ins)
                    ins.then_inc(br_read, 1)
                    linked(l)
                    link(dve.tensor_tensor(zT[:, j, :], zT[:, j, :], br_u, ALU.add))
                    linked(l)
                    dve.wait_ge(br_read, l * 8 + j + 1)
                    dve.tensor_tensor(zT[:, j, :], zT[:, j, :], br_w, ALU.add).then_inc(zT_ready, 1)
                    dve.wait_ge(zT_ready, l * 8 + j + 1)
                    if j:
                        z_rest(j - 1)
                lo_quarter(dve, l, "out", 0, -1, 0)
                z_rest(KT - 1)

                dve.wait_ge(gb_ready, l * GB + 4)
                def x_update(s):
                    done("out", s + 1)
                    b = 3 * (s % 2)
                    cols = slice(s * CH, (s + 1) * CH)
                    tmp = work[:, (s % 2) * 768:(s % 2 + 1) * 768].rearrange("p (t c) -> p t c", t=TILES)
                    link(dve.tensor_tensor(tmp[:, 0], ps[:, b, 0:CH], gb[:, 0, cols], ALU.mult))
                    dve.tensor_tensor(tmp[:, 1:3], ps[:, b + 1:b + 3, 0:CH], bcast(gb[:, 1, cols], [P, 2, CH], 1),
                                      ALU.mult).then_inc(out_read, 1)
                    linked(l)
                    dve.wait_ge(out_read, l * 4 + s + 1)
                    ins = dve.scalar_tensor_tensor(out=x[:, :, cols], in0=tmp, scalar=0.5, in1=x[:, :, cols],
                                                   op0=ALU.mult, op1=ALU.add)
                    if s < 3:
                        link(ins)
                    else:
                        ins.then_inc(x_ready, 1)

                for s in range(4):
                    for q in range(4):
                        if s or q:
                            lo_quarter(dve, l, "out", 0, s - 1, q)
                        if s and q == 1:
                            x_update(s - 1)
                x_update(3)

                linked(l)
                wait_apart(dve, x_ready, l * XR + 1 + 1)
                norm(1)

                iota16 = cst[:, C_IOTA:C_IOTA + 16]
                iota4 = cst[:, C_IOTA:C_IOTA + 4]

                def one_hot(values, n, iota, maximum, tmp, idx, out_hot):
                    link(dve.tensor_reduce(maximum, values, AX_X, ALU.max))
                    linked(l)
                    link(dve.tensor_tensor(tmp, values, bcast(maximum, [P, TILES, n], 2), ALU.is_equal))
                    linked(l)
                    link(dve.scalar_tensor_tensor(out=tmp, in0=tmp, scalar=-99.0, in1=bcast(iota, [P, TILES, n], 1),
                                                  op0=ALU.mult, op1=ALU.add))
                    linked(l)
                    link(dve.tensor_reduce(idx, tmp, AX_X, ALU.min))
                    linked(l)
                    link(dve.tensor_tensor(out_hot, tmp, bcast(idx, [P, TILES, n], 2), ALU.is_equal))
                    linked(l)

                dve.wait_ge(loT_psum, l + 1)
                dve.tensor_copy(loT, ps[0:20, 0, 0:TOK]).then_inc(loT_ready, 1)
                dve.wait_ge(lo_psum, l * 1 + 1)
                link(dve.tensor_tensor(lo[:, :, :], ps[:, 1, 0:60].rearrange("p (t c) -> p t c", t=TILES),
                                       bcast(rb[:, :], [P, TILES, 20], 1), ALU.add))
                linked(l)
                g = lo[:, :, 0:4]
                one_hot(g, 4, iota4, r1[:, 0, :], r4[:, 0], r1[:, 1, :], r4[:, 1])
                dve.tensor_tensor(r4[:, 2], g, bcast(r1[:, 0, :], [P, TILES, 4], 2), ALU.subtract).then_inc(router_sub, 1)
                e4 = lo[:, :, 4:20].rearrange("p t (g e) -> p t g e", e=4)
                em = r16[:, 0]
                link(dve.tensor_tensor(em.rearrange("p t (g e) -> p t g e", e=4), e4,
                                       bcast(r4[:, 1], [P, TILES, 4, 4], 3), ALU.mult))
                link(dve.tensor_scalar(r4[:, 0], r4[:, 1], -NEG, NEG, ALU.mult, ALU.add))
                linked(l)
                link(dve.tensor_tensor(em.rearrange("p t (g e) -> p t g e", e=4), em.rearrange("p t (g e) -> p t g e", e=4),
                                       bcast(r4[:, 0], [P, TILES, 4, 4], 3), ALU.add))
                linked(l)
                one_hot(em, 16, iota16, r1[:, 2, :], r16[:, 1], r1[:, 1, :], r16[:, 2])
                link(dve.scalar_tensor_tensor(out=em, in0=r16[:, 2], scalar=2 * NEG, in1=em, op0=ALU.mult, op1=ALU.add))
                linked(l)
                one_hot(em, 16, iota16, r1[:, 3, :], r16[:, 1], r1[:, 1, :], r16[:, 3])
                dve.tensor_tensor(hotsum[:, :, :], r16[:, 2], r16[:, 3], ALU.add).then_inc(hot_ready, 1)
                dve.tensor_tensor(r1[:, 4, :], r1[:, 3, :], r1[:, 2, :], ALU.subtract).then_inc(router_sub, 1)
                dve.wait_ge(router_exp, l * 2 + 1)
                link(dve.tensor_reduce(r1[:, 5, :], r4[:, 2], AX_X, ALU.add))
                linked(l)
                dve.wait_ge(router_exp, l * 2 + 2)
                link(dve.tensor_scalar(r1[:, 6, :], r1[:, 4, :], 1.0, 2.0, ALU.add, ALU.mult))
                linked(l)
                link(dve.tensor_tensor(r1[:, 5, :], r1[:, 5, :], r1[:, 6, :], ALU.mult))
                linked(l)
                link(dve.reciprocal(r1[:, 6, :], r1[:, 5, :]))
                linked(l)
                link(dve.tensor_tensor(r1[:, 7, :], r1[:, 6, :], r1[:, 4, :], ALU.mult))

                dve.wait_ge(rank_psum, l * 1 + 1)
                rank = ps[:, 0, 64:112].rearrange("p (t e) -> p t e", t=TILES)
                counts = ps[:, 0, 112:128]
                link(dve.tensor_scalar(e16[:, 0, :], counts, P + 0.5, None, ALU.is_gt))
                linked(l)
                link(dve.scalar_tensor_tensor(out=e16[:, 0, :], in0=counts, scalar=2 * P + 0.5, in1=e16[:, 0, :],
                                              op0=ALU.is_gt, op1=ALU.add))
                linked(l)
                link(dve.tensor_copy(e16[:, 1, :], e16[:, 0, :]))
                for n, shift_by in enumerate((1, 2, 4, 8)):
                    linked(l)
                    src, dst = e16[:, 1 + n % 2, :], e16[:, 2 - n % 2, :]
                    link(dve.tensor_tensor(dst[:, shift_by:16], src[:, shift_by:16], src[:, 0:16 - shift_by], ALU.add))
                    link(dve.tensor_copy(dst[:, 0:shift_by], src[:, 0:shift_by]))
                linked(l)
                ends = e16[:, 1, :]
                link(dve.tensor_tensor(e16[:, 3, :], ends, e16[:, 0, :], ALU.subtract))
                linked(l)
                link(dve.tensor_scalar(e16[:, 3, :], e16[:, 3, :], float(N_EXP - 1), float(P), ALU.add, ALU.mult))
                linked(l)
                link(dve.tensor_tensor(e16[:, 3, :], e16[:, 3, :], cst[:, C_BLOCK:C_BLOCK + 16], ALU.subtract))
                link(dve.tensor_tensor(r16[:, 0], rank, bcast(cst[:, C_BLOCK:C_BLOCK + 16], [P, TILES, 16], 1), ALU.add))
                linked(l)
                link(dve.scalar_tensor_tensor(out=r16[:, 1], in0=rank, scalar=P - 0.5, in1=bcast(e16[:, 3, :], [P, TILES, 16], 1),
                                              op0=ALU.is_gt, op1=ALU.mult))
                linked(l)
                link(dve.tensor_tensor(r16[:, 0], r16[:, 0], r16[:, 1], ALU.add))
                linked(l)
                link(dve.tensor_scalar(rmod, rank, P - 0.5, None, ALU.is_gt))
                linked(l)
                link(dve.scalar_tensor_tensor(out=rmod, in0=rank, scalar=2 * P - 0.5, in1=rmod, op0=ALU.is_gt, op1=ALU.add))
                linked(l)
                link(dve.scalar_tensor_tensor(out=rmod, in0=rmod, scalar=-float(P), in1=rank, op0=ALU.mult, op1=ALU.add))
                linked(l)
                hots = r16[:, 2:4]
                link(dve.tensor_tensor(hot_rmod, hots, bcast(rmod, [P, 2, TILES, 16], 1), ALU.mult))
                linked(l)
                link(dve.tensor_tensor(hots, hots, bcast(r16[:, 0], [P, 2, TILES, 16], 1), ALU.mult))
                link(dve.tensor_reduce(lane, hot_rmod, AX_X, ALU.add))
                linked(l)
                link(dve.tensor_reduce(slot_f[:, :, :], hots, AX_X, ALU.add))
                linked(l)
                link(dve.tensor_tensor(first, slot_f[:, :, :], lane, ALU.subtract))
                linked(l)
                for k in range(2):
                    for t in range(TILES):
                        dve.tensor_scalar(at_block[:, k, t, :], cst[:, C_BLOCKS:C_BLOCKS + 22], first[:, k, t:t + 1],
                                          cst[:, C_TOKEN + t:C_TOKEN + t + 1], ALU.is_equal, ALU.mult).then_inc(places_ready, 1)
                        dve.tensor_scalar(at_lane[:, k, t, :], cst[:, C_LANE:C_LANE + P], lane[:, k, t:t + 1], None,
                                          ALU.is_equal).then_inc(places_ready, 1)
                link(dve.tensor_copy(slot_i[:, :, :], slot_f[:, :, :]))
                ada_rows("ada5", 1, 2)
                link(dve.tensor_tensor(owner[:, :, :], bcast(cst[:, C_IOTA:C_IOTA + EXTRA], [P, EXTRA, 16], 2),
                                       bcast(ends, [P, EXTRA, 16], 1), ALU.is_ge))
                linked(l)
                link(dve.tensor_reduce(ownerf[:, :], owner[:, :, :], AX_X, ALU.add))
                linked(l)
                link(dve.tensor_scalar(ownerf[:, :], ownerf[:, :], float(N_EXP - 1), None, ALU.min))
                linked(l)
                link(dve.tensor_copy(extra_i[0:1, 0:1], ends[0:1, 15:16]))
                link(dve.tensor_copy(extra_i[0:1, 1:6], ownerf[0:1, :]))
                linked(l)
                dve.tensor_copy(extra_i[0:1, 6:7], ends[0:1, 15:16]).then_inc(routed, 1)
                dve.wait_ge(token_psum, l + 1)
                dve.tensor_copy(token_i[:, :], ps[:, 0, 128:150]).then_inc(tokens_ready, 1)

                gate_rows(1)

                def inputs_copied(i, u):
                    dve.wait_ge(xgT_psum, blocks(l, i, u) + 1)
                    dve.tensor_copy(hgT[:, (u + 1) % 2, 4:8, :].rearrange("p k n -> p (k n)"), ps[:, 1, :]).then_inc(hg_dve, 1)

                def activated(i, u):
                    par = (u + 1) % 2
                    dve.wait_ge(th_ready, blocks(l, i, u) + 1)
                    dve.scalar_tensor_tensor(out=act_t[:, par], in0=act_t[:, par], scalar=1.0, in1=ps[:, 2 + par, 0:CH],
                                             op0=ALU.add, op1=ALU.mult).then_inc(e_mul, 1)
                    dve.wait_ge(e_mul, blocks(l, i, u) + 1)
                    done("moe", i * 12 + moe_seq(u) + 2)
                    dve.tensor_tensor(act_a[:, par], act_t[:, par], ps[:, 2 + par, CH:2 * CH], ALU.mult).then_inc(a_made, 1)

                def activations_copied(i, u):
                    dve.wait_ge(aT_psum, blocks(l, i, u) + 1)
                    dve.tensor_copy(aTs[:, (u + 1) % 2].rearrange("p j n -> p (j n)"), ps[:, 4, 0:CH]).then_inc(aTs_ready, 1)

                def output_copied(i, u, last=False):
                    buf = (u + 1) % 4
                    done("moe", i * 12 + (11 if last else moe_down_seq(u)) + 1)
                    dve.wait_ge(y_free, blocks(l, i, u) + 1)
                    dve.tensor_copy(yb[:, buf, 512:D], ps[:, 6, :]).then_inc(y_dve, 1)

                inputs_copied(0, -1)
                activated(0, -1)
                inputs_copied(0, 0)
                with dve.Fori(0, 3) as i:
                    for u in range(4):
                        activations_copied(i, u - 1)
                        activated(i, u)
                        inputs_copied(i, u + 1)
                        output_copied(i, u - 1)
                for u in range(3):
                    activations_copied(3, u - 1)
                    activated(3, u)
                    if u < 2:
                        inputs_copied(3, u + 1)
                    output_copied(3, u - 1)
                activations_copied(3, 2)
                output_copied(3, 2, last=True)

                wait_apart(dve, routed, l + 1)
                extra = dve.value_load(extra_i[0:1, 0:1], min_val=0, max_val=EXTRA)
                with dve.If(extra > 0):
                    wait_apart(dve, y_free, l * N_EXP + N_EXP + 4)
                    with dve.Fori(0, EXTRA) as n:
                        dve.wait_ge(ov_xT, l * EXTRA + n + 1)
                        dve.tensor_copy(hgT[:, 0].rearrange("p (b k) n -> p b (k n)", b=2), ps[:, 0:2, :]).then_inc(ov_hg, 1)
                        dve.wait_ge(ov_t, l * EXTRA + n + 1)
                        dve.scalar_tensor_tensor(out=act_t[:, 0], in0=act_t[:, 0], scalar=1.0, in1=ps[:, 2, 0:CH],
                                                 op0=ALU.add, op1=ALU.mult).then_inc(ov_m, 1)
                        dve.wait_ge(ov_m, l * EXTRA + n + 1)
                        dve.tensor_tensor(act_a[:, 0], act_t[:, 0], ps[:, 2, CH:2 * CH], ALU.mult).then_inc(ov_a, 1)
                        dve.wait_ge(ov_aT, l * EXTRA + n + 1)
                        dve.tensor_copy(aTs[:, 0].rearrange("p j n -> p (j n)"), ps[:, 4, 0:CH]).then_inc(ov_as, 1)
                        dve.wait_ge(ov_y, l * EXTRA + n + 1)
                        dve.tensor_copy(yb[:, 0].rearrange("p (h c) -> p h c", h=2), ps[:, 5:7, :]).then_inc(ov_ye, 1)
                        dve.wait_ge(ov_ys, l * (16 * EXTRA) + n * 16 + 16)
                with dve.Else():
                    for one in (ov_hg, ov_m, ov_a, ov_as, ov_ye):
                        dve.sem_inc(one, EXTRA)

                dve.wait_ge(gb_ready, l * GB + GB)
                for t in range(TILES):
                    dve.wait_ge(yg_loaded[t], l * 32 + 32)
                    dve.wait_ge(y1_scaled, l * TILES + t + 1)
                    link(dve.scalar_tensor_tensor(out=yg[:, 0, t], in0=yg[:, 1, t], scalar=r1[:, 7, t:t + 1], in1=yg[:, 0, t],
                                                  op0=ALU.mult, op1=ALU.add))
                    linked(l)
                    link(dve.tensor_tensor(yg[:, 0, t], yg[:, 0, t], gb[:, min(t, 1), :], ALU.mult))
                    linked(l)
                    ins = dve.tensor_tensor(x[:, t, :], x[:, t, :], yg[:, 0, t], ALU.add)
                    if t < TILES - 1:
                        link(ins)
                    else:
                        ins.then_inc(x_ready, 1)
                linked(l)
                dve.wait_ge(x_ready, l * XR + XR + 1)
                assert count[0] == DVE_CHAIN, count[0]

            dve.wait_ge(rstd_ready, DEPTH * RS + 1)
            dve.wait_ge(stored, 16)
            for t in range(TILES):
                dve.scalar_tensor_tensor(out=xn[:, t, :], in0=x[:, t, :], scalar=rstd[:, t:t + 1], in1=fing,
                                         op0=ALU.mult, op1=ALU.mult).then_inc(fin_ready, 1)

        @block.scalar
        def _(act):
            act.wait_ge(init_loaded, 16 * INIT_LOADS)
            act.activation(condt[:, :, :], condr[:, :, :], ACT.Tanh, scale=0.5).then_inc(act_init, 1)
            act.wait_ge(init_dve, 1)
            act.activation(lgt[:, 2, :], lgt[:, 1, :], ACT.Exp, scale=-1.0).then_inc(act_init, 1)
            act.wait_ge(act_init, 2)
            act.activation(lgt[:, 3, :], lgt[:, 2, :], ACT.Ln, bias=1.0).then_inc(act_init, 1)
            act.wait_ge(init_dve, 10)
            act.activation(qdec[:, :, :, :], qdec[:, :, :, :], ACT.Exp).then_inc(act_init, 1)
            act.activation(kdec[:, :, :, :], kdec[:, :, :, :], ACT.Exp).then_inc(act_init, 1)
            act.activation(cdec[:, :, :, :], cdl[:, :, :, :], ACT.Exp).then_inc(act_init, 1)
            for ll in range(DEPTH):
                for h in range(4):
                    n = ll * 8 + h
                    act.activation(dec[:, ll, h, :], once[:, 256:384], ACT.Exp,
                                   scale=lg[:, n:n + 1]).then_inc(act_init, 1)
                    act.activation(work[:, (ll * 4 + h) * P:(ll * 4 + h + 1) * P], once[:, 384:512], ACT.Exp,
                                   scale=lg[:, n + 4:n + 5]).then_inc(act_init, 1)
            act.dma_start(x[:, 0, :], a["x_prompt"][0]).then_inc(x_loaded, 16)
            act.dma_start(x[:, 1:3, :], a["x_sample"][0].rearrange("(t p) d -> p t d", p=P)).then_inc(x_loaded, 16)
            act.wait_ge(x_loaded, 32)
            act.wait_ge(init_dve, 14)

            def squares(ready):
                act.wait_ge(*ready)
                for t in range(TILES):
                    act.activation(xn[:, t, :], x[:, t, :], ACT.Square, accum_out=ssq[:, t:t + 1]).then_inc(ssq_ready, 1)

            with act.Fori(0, DEPTH) as l:
                def done(seg, n):
                    act.wait_ge(chunk_done, l * LAYER_CHUNKS + (SEG[seg] + SLOTS) + n)

                squares((x_ready, l * XR + 1))

                row = bass.ds(l, 1)
                for n, name in enumerate(("norm1_g", "norm2_g")):
                    act.dma_start(gain[:, n, :], a[name][row].rearrange("a (p k) -> p (a k)", k=KT)).then_inc(gains_loaded, 16)
                for n in range(2):
                    act.dma_start(modb[:, 2 * n:2 * n + 2, :], a["ada_b"][row, 3 * D * n:3 * D * n + 2 * D].rearrange("a (s p k) -> p (a s) k", s=2, k=KT)
                                  ).then_inc(gains_loaded, 16)
                loads = [
                    (rw[:, :, 0:4], a["router_group_w"][row].rearrange("a (p k) c -> p (a k) c", k=KT)),
                    (rw[:, :, 4:20], a["router_expert_w"][row].rearrange("a (p k) c -> p (a k) c", k=KT)),
                    (rb[:, 0:4], a["router_group_b"][row].to_broadcast([P, 4])),
                    (rb[:, 4:20], a["router_expert_b"][row].to_broadcast([P, 16])),
                    (ret_g, a["ret_norm_g"][row].to_broadcast([P, 256])),
                    (sink[:, :], a["swa_sink"][row].to_broadcast([P, 4])),
                    (cache_k[:, 0:8, :], a["cache_na_k"][0][row].rearrange("a h s d -> s (a h) d")),
                    (cache_k[:, 8:10, :], a["cache_swa_k"][0][row].rearrange("a h s d -> s (a h) d")),
                    (cache_v[:, 0:8, :], a["cache_na_v"][0][row].rearrange("a h s d -> s (a h) d")),
                    (cache_v[:, 8:10, :], a["cache_swa_v"][0][row].rearrange("a h s d -> s (a h) d")),
                    (state0[:, :, :, :].rearrange("p r b e -> p (r b) e"),
                     a["state_ret"][0][row].rearrange("a r h d e -> (a r h d) e").rearrange("(n p) e -> p n e", p=P)),
                ]
                for dst, src in loads:
                    act.dma_start(dst, src).then_inc(small_loaded, 16)
                for rp in range(2):
                    for h in range(HEADS_NA):
                        off = l * (HEADS_NA * RPB) + (h * RPB + (5 - rp) * RPB_W + WIN_COLS - GRID_W)
                        src = bass.AP(tensor=a["na_rpb_flat"].tensor, offset=off,
                                      ap=[[1, GRID_W], [RPB_W, 6], [1, GRID_W]])
                        act.dma_start(bias_turned[rp * GRID_W:(rp + 1) * GRID_W, h, :].rearrange("p (s c) -> p s c", s=6),
                                      src).then_inc(small_loaded, 16)

                def norm(which):
                    act.wait_ge(mod_ready, l * MODR + 2 * which + 2)
                    for k in range(1, KT, 2):
                        act.wait_ge(xT_psum, l * XT + 8 * which + k + 1)
                        for c, (n0, n1) in enumerate(((0, P), (P, TOK))):
                            act.activation(hT[:, k, n0:n1], ps[:, k, n0:n1], ACT.Identity, scale=scale[:, k, c:c + 1],
                                           bias=shift[:, k, c:c + 1]).then_inc(hT_act, 1)

                norm(0)

                for r in range(4):
                    act.wait_ge(hT_dve, l * HT + 2 * r + 2)
                    act.wait_ge(hT_act, l * HT + 2 * r + 2)
                    act.activation(h_hi[:, 2 * r:2 * r + 2, :], hT[:, 2 * r:2 * r + 2, :], ACT.Copy).then_inc(split_hi, 1)

                def odd_products(i, u):
                    if (u + 1) % 2 == 1:
                        done("z", i * SLOTS + (u + 2))
                        act.activation(zt[:, :, bass.ds(i * (SLOTS * CH) + (u + 1) * CH, CH)], ps[:, 3:6, 0:CH],
                                       ACT.Copy).then_inc(zt_act, 1)

                split_segment(hi_quarter, act, l, "z", odd_products)
                for q in range(2):
                    hi_quarter(act, l, "g", 0, -1, q)

                act.wait_ge(bias_psum, l * HEADS_NA + HEADS_NA)
                act.wait_ge(zt_dve, l * ZD + ZD + 1)
                act.wait_ge(zt_act, l * ZD + ZD + 1)
                act.activation(rot[:, 0, 0:256].rearrange("p (ha hb i) -> p hb ha i", ha=2, hb=2),
                               zt[:, 0, QS:QS + 256].rearrange("p (hb ha i) -> p hb ha i", ha=2, hb=2), ACT.Copy).then_inc(rot_act, 1)
                act.activation(rot[:, 0, 256:384], zt[:, 0, KS:KS + P], ACT.Copy).then_inc(rot_act, 1)

                for u in range(1, TP, 2):
                    act.wait_ge(t_psum, l * TP + u + 1)
                    if u == 9:
                        act.activation(kcT[:, 4, :], ps[:, 1, 0:P], ACT.Copy).then_inc(t_act, 1)
                        continue
                    v = u if u < 8 else u - 2
                    act.activation(qkT[:, v, :], ps[:, u % 8, 0:TOK], ACT.Copy,
                                   scale=HD ** -0.5 if v in SCALED else 1.0).then_inc(t_act, 1)

                def exp(g, j):
                    t, kind = GROUPS[g]
                    w = P if t == 0 else 384
                    if j == 0:
                        act.wait_ge(nmax_ready, l * NG + g + 1)
                    act.activation(sbuf_s[:, g % 2, j, 0:w], sbuf_s[:, g % 2, j, 0:w], ACT.Exp,
                                   bias=nmx[:, g % 2, j:j + 1], accum_out=den[:, g % 2, j:j + 1]).then_inc(exp_ready, 1)
                    if kind == 2 and j == 3:
                        act.activation(sk[:, g % 2, :], sk[:, g % 2, :], ACT.Exp).then_inc(sink_exp, 1)

                def copy(g, j):
                    w = P if GROUPS[g][0] == 0 else 384
                    u = 4 * g + j
                    act.wait_ge(pt_psum, l * SU + u + 1)
                    if u >= 2:
                        act.wait_ge(pv_done, l * SU + u - 1)
                    act.activation(pT[:, u % 2, 0:w], ps[:, 4 + u % 2, 0:w], ACT.Copy).then_inc(pT_ready, 1)

                for j in range(4):
                    exp(0, j)
                for g in range(NG):
                    copy(g, 0)
                    copy(g, 1)
                    for j in range(4):
                        if g + 1 < NG:
                            exp(g + 1, j)
                        if j < 2:
                            copy(g, j + 2)

                act.activation(tgr, zt[:, :, GR:GR + 256], ACT.Tanh, scale=0.5).then_inc(tgr_ready, 1)

                def gates(i, u):
                    c = u + 1
                    done("g", i * SLOTS + c + 1)
                    for j in range(2):
                        f = 2 * c + j
                        dst = gate_tile(16 + f) if isinstance(i, int) else arena[:, bass.ds(i * (8 * TOK) + (9216 + f * TOK), TOK)]
                        act.activation(dst, ps[:, f, 0:TOK], ACT.Tanh, scale=0.5).then_inc(gate_ready, 1)

                for q in range(2, 4):
                    hi_quarter(act, l, "g", 0, -1, q)
                split_segment(hi_quarter, act, l, "g", gates, first=4)

                for j in range(1, KT, 2):
                    act.wait_ge(ot_psum, l * KT + j + 1)
                    act.activation(oT[:, j, :], ps[:, j, 0:TOK], ACT.Copy).then_inc(ot_act, 1)


                hi_quarter(act, l, "out", 0, -1, 0)
                for j in range(KT):
                    act.wait_ge(zT_ready, l * 8 + j + 1)
                    act.activation(h_hi[:, j, :], zT[:, j, :], ACT.Copy).then_inc(z_hi, 1)
                for s in range(4):
                    for q in range(4):
                        if s or q:
                            hi_quarter(act, l, "out", 0, s - 1, q)

                squares((x_ready, l * XR + 1 + 1))
                norm(1)

                for t in range(TILES):
                    act.wait_ge(h2_psum, l * TILES + t + 1)
                    act.activation(xn[:, t, :].rearrange("p (h c) -> p h c", h=2), ps[:, 2 + 2 * t:4 + 2 * t, :],
                                   ACT.Copy).then_inc(h2_ready, 1)

                act.wait_ge(router_sub, l * 2 + 1)
                act.activation(r4[:, 2], r4[:, 2], ACT.Exp).then_inc(router_exp, 1)
                act.wait_ge(router_sub, l * 2 + 2)
                act.activation(r1[:, 4, :], r1[:, 4, :], ACT.Exp).then_inc(router_exp, 1)


                def inputs_copied(i, u):
                    act.wait_ge(xgT_psum, blocks(l, i, u) + 1)
                    act.activation(hgT[:, (u + 1) % 2, 0:4, :].rearrange("p k n -> p (k n)"), ps[:, 0, :],
                                   ACT.Copy).then_inc(hg_act, 1)

                def gate_tanh(i, u):
                    par = (u + 1) % 2
                    if u >= 0:
                        act.wait_ge(a_made, blocks(l, i, u))
                    done("moe", i * 12 + moe_seq(u) + 2)
                    act.activation(act_t[:, par], ps[:, 2 + par, 0:CH], ACT.Tanh, scale=0.5).then_inc(th_ready, 1)

                def output_copied(i, u):
                    buf = (u + 1) % 4
                    act.wait_ge(y_psum, blocks(l, i, u) + 1)
                    act.wait_ge(y_free, blocks(l, i, u) + 1)
                    act.activation(yb[:, buf, 0:512], ps[:, 5, :], ACT.Copy).then_inc(y_act, 1)

                inputs_copied(0, -1)
                gate_tanh(0, -1)
                inputs_copied(0, 0)
                with act.Fori(0, 3) as i:
                    for u in range(4):
                        gate_tanh(i, u)
                        inputs_copied(i, u + 1)
                        output_copied(i, u - 1)
                for u in range(3):
                    gate_tanh(3, u)
                    if u < 2:
                        inputs_copied(3, u + 1)
                    output_copied(3, u - 1)
                output_copied(3, 2)

                wait_apart(act, routed, l + 1)
                extra = act.value_load(extra_i[0:1, 0:1], min_val=0, max_val=EXTRA)
                with act.If(extra > 0):
                    wait_apart(act, y_free, l * N_EXP + N_EXP + 4)
                    with act.Fori(0, EXTRA) as n:
                        row = act.snap(n * P + N_EXP * P)
                        act.wait_ge(ov_g, l * EXTRA + n + 1)
                        act.activation(act_t[:, 0], ps[:, 2, 0:CH], ACT.Tanh, scale=0.5).then_inc(ov_t, 1)
                        wait_apart(act, ov_ye, l * EXTRA + n + 1)
                        act.dma_start(a["ys"][bass.ds(row, P)], yb[:, 0, :]).then_inc(ov_ys, 16)
                        wait_apart(act, ov_ys, l * (16 * EXTRA) + n * 16 + 16)
                with act.Else():
                    act.sem_inc(ov_t, EXTRA)
                    act.sem_inc(ov_ys, 16 * EXTRA)

                for t in range(TILES):
                    act.wait_ge(yg_loaded[t], l * 32 + 32)
                    act.activation(yg[:, 0, t], yg[:, 0, t], ACT.Identity, scale=r1[:, 6, t:t + 1], bias=zero1[:, 0:1]).then_inc(y1_scaled, 1)

            squares((x_ready, DEPTH * XR + 1))

        @block.gpsimd
        def _(pool):
            def root(n, ready, src, mid, dst, width, mean, signal):
                wait_apart(pool, *ready)
                pool.tensor_scalar(mid[:, :], src[:, :], 1.0 / mean, EPS, ALU.mult, ALU.add).then_inc(pool_step, 1)
                pool.wait_ge(pool_step, n)
                pool.tensor_tensor(dst[:, :], mid[:, :], mhalf[:, 0:width], ALU.pow).then_inc(signal, 1)

            pool.wait_ge(init_dve, 14)
            pool.sem_inc(gate_ready, 8)
            pool.sem_inc(y_free, 4)
            with pool.Fori(0, DEPTH) as l:
                def gate_bias(section):
                    for c in range(2):
                        pool.dma_start(gb[:, c, :], a["ada_b"][bass.ds(l, 1), section * D:(section + 1) * D].to_broadcast([P, D])
                                       ).then_inc(adab_loaded, 16)

                wait_apart(pool, x_ready, l * XR + 1)
                pool.memset(biasT[:, 0:HEADS_NA * BIAS_W].rearrange("p (h c) -> p h c", c=BIAS_W)[:, :, 0:P], 0.0).then_inc(bias_ready, 1)
                pool.memset(biasT[:, HEADS_NA * BIAS_W:], 0.0).then_inc(bias_ready, 1)
                root(l * POOL_L + 1, (ssq_ready, l * SSQ + 3), ssq, msq, rstd, 3, D, rstd_ready)
                gate_bias(2)
                pool.wait_ge(zt_dve, l * ZD + ZD + 1)
                pool.wait_ge(zt_act, l * ZD + ZD + 1)
                for i, (t, d) in enumerate(((0, 0), (0, 1), (1, 0), (2, 1))):
                    kdl = kdec[:, :, :, :].rearrange("p l r h -> p (l r h)")[:, bass.ds(l * 8 + 4 * d, 4)]
                    pool.tensor_tensor(kd[:, i, :].rearrange("p (h d) -> p h d", d=HD),
                                       zt[:, t, KR:KR + 256].rearrange("p (h d) -> p h d", d=HD),
                                       kdl.unsqueeze(2).to_broadcast([P, 4, HD]), ALU.mult).then_inc(kd_ready, 1)
                for name, c0, n in (("new_na_k", KA, 8), ("new_na_v", VA, 8), ("new_swa_k", KS, 2), ("new_swa_v", VS, 2)):
                    pool.dma_start(out[name][0][bass.ds(l, 1)].rearrange("a h s d -> s (a h) d"),
                                   zt[:, 0, c0:c0 + n * HD].rearrange("p (h d) -> p h d", d=HD)).then_inc(kv_stored, 16)
                with pool.If(l < 1):
                    pool.dma_start(a["ys"][N_EXP * P:BLOCKS * P].rearrange("(b p) d -> p b d", p=P),
                                   x[:, 0:1, :].to_broadcast([P, EXTRA, D])).then_inc(filled, 16)
                pool.wait_ge(state_ready, l * 10 + 2)
                pool.dma_start(out["new_state"][0][bass.ds(l, 1)].rearrange("a r h d e -> (a r h d) e").rearrange("(n p) e -> p n e", p=P),
                               state_out[:, :, :, :].rearrange("p r b e -> p (r b) e")).then_inc(kv_stored, 16)
                root(l * POOL_L + 2, (ret_ssq, l * 1 + 1), ssq12, msq12, rstd12, 12, HD, rsq_ready)
                root(l * POOL_L + 3, (ssq_ready, l * SSQ + 6), ssq, msq, rstd, 3, D, rstd_ready)
                gate_bias(5)

                wait_apart(pool, h2_ready, l * TILES + TILES)
                pool.dma_start(a["xs"].rearrange("(t p) d -> p t d", p=P), xn).then_inc(xs_stored, 16)
                pool.wait_ge(filled, 16)
                wait_apart(pool, tokens_ready, l + 1)
                wait_apart(pool, xs_stored, l * 16 + 16)

                def load_block(b):
                    pool.indirect_dma_start(xg[:, b % 4, :], None, a["xs"],
                                            bass.IndirectOffsetOnAxis(ap=token_i[:, b:b + 1], axis=0)).then_inc(xg_loaded[b % 4], 16)

                for b in range(4):
                    load_block(b)
                extra = pool.value_load(extra_i[0:1, 0:1], min_val=0, max_val=EXTRA)
                with pool.If(extra < 1):
                    for n in range(EXTRA):
                        pool.dma_start(spare[:, 4 * n:4 * n + 4], a["consts"][0:1, 0:4]).then_inc(ov_x, 16)
                for b in range(N_EXP):
                    wait_apart(pool, y_act, l * N_EXP + b + 2)
                    wait_apart(pool, y_dve, l * N_EXP + b + 2)
                    pool.dma_start(a["ys"][b * P:(b + 1) * P], yb[:, b % 4, :]).then_inc(y_stored, 16)
                    if b + 4 < N_EXP:
                        wait_apart(pool, xgT_psum, l * N_EXP + b + 1)
                        load_block(b + 4)
                    wait_apart(pool, y_stored, l * (16 * N_EXP) + 16 * (b + 1))
                    pool.sem_inc(y_free, 1)

                with pool.If(extra > 0):
                    for n in range(EXTRA):
                        if n:
                            wait_apart(pool, ov_xT, l * EXTRA + n)
                        tokens = token_i[:, N_EXP + n:N_EXP + n + 1]
                        pool.indirect_dma_start(xg[:, 0, :], None, a["xs"],
                                                bass.IndirectOffsetOnAxis(ap=tokens, axis=0)).then_inc(ov_x, 16)

                wait_apart(pool, ov_ys, l * (16 * EXTRA) + 16 * EXTRA)
                for t in range(TILES):
                    for k in range(2):
                        pool.indirect_dma_start(yg[:, k, t], None, a["ys"],
                                                bass.IndirectOffsetOnAxis(ap=slot_i[:, k, t:t + 1], axis=0)).then_inc(yg_loaded[t], 16)

            pool.dma_start(fing, a["final_norm_g"].unsqueeze(0).to_broadcast([P, D])).then_inc(stored, 16)
            root(DEPTH * POOL_L + 1, (ssq_ready, DEPTH * SSQ + 3), ssq, msq, rstd, 3, D, rstd_ready)
            pool.wait_ge(fin_ready, 1)
            pool.dma_start(out["y_prompt"][0], xn[:, 0, :]).then_inc(stored, 16)
            pool.wait_ge(fin_ready, 3)
            pool.dma_start(out["y_sample"][0].rearrange("(t p) d -> p t d", p=P), xn[:, 1:3, :]).then_inc(stored, 16)
            pool.wait_ge(kv_stored, DEPTH * KV_L)
            pool.wait_ge(stored, 48)


_OUTS = {"y_prompt": (1, 128, 1024), "y_sample": (1, 256, 1024), "new_na_k": (1, 2, 8, 128, 64),
         "new_na_v": (1, 2, 8, 128, 64), "new_swa_k": (1, 2, 2, 128, 64), "new_swa_v": (1, 2, 2, 128, 64),
         "new_state": (1, 2, 2, 4, 64, 64)}


def kernel(**inputs):
    import numpy as _np
    import concourse.bacc as _bacc
    from concourse.bass_utils import run_bass_kernel_spmd as _run

    nc = _bacc.Bacc("TRN2", target_bir_lowering=False, num_devices=1)
    arrays, args, outs = {}, {}, {}
    laid = {k: _np.ascontiguousarray(v) for k, v in inputs.items()}
    laid["na_rpb_flat"] = laid.pop("na_rpb").reshape(1, -1)
    laid["consts"] = constants()
    for name, v in laid.items():
        arrays[f"in_{name}"] = v
        args[name] = nc.dram_tensor(f"in_{name}", v.shape, mybir.dt.from_np(v.dtype), kind="ExternalInput").ap()
    for name, shape in _OUTS.items():
        outs[name] = nc.dram_tensor(f"out_{name}", shape, F32, kind="ExternalOutput").ap()
    for name, rows in (("xs", TOK), ("ys", BLOCKS * P)):
        args[name] = nc.dram_tensor(f"scratch_{name}", (rows, D), F32, kind="Internal").ap()
    build(nc, args, outs)
    r = _run(nc, [arrays], core_ids=[0])
    return tuple(r.results[0][f"out_{name}"] for name in _OUTS)
```
